# Optimizing a Trainium2 kernel written in Bass

```python
import math
import jax
import jax.numpy as jnp
from jax import lax
import numpy as np
import jax, jax.numpy as jnp

D_MODEL = 1024
BATCH = 1
SEQ = 256
DEPTH = 1

ATT_HEAD_DIM = 128
ATT_HEADS = 8
ATT_WIDTH = ATT_HEADS * ATT_HEAD_DIM
MOBA_BLOCK = 256
MOBA_TOPK = 3
MOBA_QCHUNK = 64
REL_BUCKETS = 32
REL_MAX_DIST = 2048
MLSTM_HEADS = 4
MLSTM_WIDTH = D_MODEL
MLSTM_HEAD_DIM = MLSTM_WIDTH // MLSTM_HEADS
MLSTM_CHUNK = 64
QKV_BLOCK = 4
CONV_WIDTH = 4
MIX_WIDTH = ATT_WIDTH + MLSTM_WIDTH
IN_COLS = 4 * ATT_WIDTH + 2 * MLSTM_WIDTH
RMS_EPS = 1e-6
LN_EPS = 1e-5


def rmsnorm(x, g):
    xf = x.astype(jnp.float32)
    y = xf * lax.rsqrt(jnp.mean(xf * xf, axis=-1, keepdims=True) + RMS_EPS)
    return (y * g.astype(jnp.float32)).astype(x.dtype)

def split_heads(a, n_heads):
    b, s, _ = a.shape
    return a.reshape(b, s, n_heads, -1).transpose(0, 2, 1, 3)

def t5_bucket(dist):
    n = jnp.maximum(dist, 0)
    max_exact = REL_BUCKETS // 2
    nf = jnp.maximum(n, 1).astype(jnp.float32)
    large = max_exact + (jnp.log(nf / max_exact) / math.log(REL_MAX_DIST / max_exact)
                         * (REL_BUCKETS - max_exact)).astype(jnp.int32)
    large = jnp.minimum(large, REL_BUCKETS - 1)
    return jnp.where(n < max_exact, n, large)

def moba_attention(q, k, v, rel_bias):
    B, H, S, Dh = q.shape
    nb = -(-S // MOBA_BLOCK)
    pad = nb * MOBA_BLOCK - S
    kb = jnp.pad(k, ((0, 0), (0, 0), (0, pad), (0, 0))).reshape(B, H, nb, MOBA_BLOCK, Dh)
    vb = jnp.pad(v, ((0, 0), (0, 0), (0, pad), (0, 0))).reshape(B, H, nb, MOBA_BLOCK, Dh)
    kmean = jnp.mean(kb.astype(jnp.float32), axis=3)
    ksel = min(MOBA_TOPK, nb)
    scale = Dh ** -0.5
    bias_h = rel_bias.T.astype(jnp.float32)
    b_idx = jnp.arange(B)[:, None, None, None]
    h_idx = jnp.arange(H)[None, :, None, None]
    h_idx5 = h_idx[..., None]
    blk_off = jnp.arange(MOBA_BLOCK)
    nq = S // MOBA_QCHUNK
    qc = jnp.moveaxis(q.reshape(B, H, nq, MOBA_QCHUNK, Dh), 2, 0)

    def one_chunk(args):
        ci, qblk = args
        q_pos = ci * MOBA_QCHUNK + jnp.arange(MOBA_QCHUNK)
        own = (ci * MOBA_QCHUNK) // MOBA_BLOCK
        qf = qblk.astype(jnp.float32) * scale
        gate = jnp.einsum('bhqd,bhnd->bhqn', qf, kmean)
        gate = jnp.where(jnp.arange(nb) < own, gate, -jnp.inf)
        _, gidx = lax.top_k(gate, ksel)
        sel_valid = gidx < own
        k_sel = kb[b_idx, h_idx, gidx].astype(jnp.float32)
        v_sel = vb[b_idx, h_idx, gidx].astype(jnp.float32)
        s_sel = jnp.einsum('bhqd,bhqnkd->bhqnk', qf, k_sel)
        k_pos_sel = gidx[..., None] * MOBA_BLOCK + blk_off
        bucket_sel = t5_bucket(q_pos[None, None, :, None, None] - k_pos_sel)
        s_sel = s_sel + bias_h[h_idx5, bucket_sel]
        s_sel = jnp.where(sel_valid[..., None], s_sel, -jnp.inf)
        k_own = lax.dynamic_index_in_dim(kb, own, axis=2, keepdims=False).astype(jnp.float32)
        v_own = lax.dynamic_index_in_dim(vb, own, axis=2, keepdims=False).astype(jnp.float32)
        s_own = jnp.einsum('bhqd,bhkd->bhqk', qf, k_own)
        dist = q_pos[:, None] - (own * MOBA_BLOCK + blk_off)[None, :]
        s_own = s_own + bias_h[:, t5_bucket(dist)][None]
        s_own = jnp.where(dist >= 0, s_own, -jnp.inf)
        logits = jnp.concatenate(
            [s_sel.reshape(B, H, MOBA_QCHUNK, ksel * MOBA_BLOCK), s_own], axis=-1)
        p = jax.nn.softmax(logits, axis=-1)
        p_sel = p[..., :ksel * MOBA_BLOCK].reshape(B, H, MOBA_QCHUNK, ksel, MOBA_BLOCK)
        p_own = p[..., ksel * MOBA_BLOCK:]
        out = (jnp.einsum('bhqnk,bhqnkd->bhqd', p_sel, v_sel)
               + jnp.einsum('bhqk,bhkd->bhqd', p_own, v_own))
        return out.astype(q.dtype)

    out = lax.map(one_chunk, (jnp.arange(nq), qc))
    return jnp.moveaxis(out, 0, 2).reshape(B, H, S, Dh)

def causal_depthwise_conv(x, w, b):
    c = x.shape[-1]
    y = lax.conv_general_dilated(
        x, w[:, None, :], window_strides=(1,), padding=[(CONV_WIDTH - 1, 0)],
        dimension_numbers=('NWC', 'WIO', 'NWC'), feature_group_count=c)
    return y + b

def blockdiag_proj(x, w):
    b, s, width = x.shape
    xb = x.reshape(b, s, width // QKV_BLOCK, QKV_BLOCK)
    return jnp.einsum('bsni,nio->bsno', xb, w).reshape(b, s, width)

def mlstm_chunkwise(q, k, v, i_pre, f_pre):
    B, H, S, Dh = q.shape
    L = MLSTM_CHUNK
    nc = S // L
    qf = q.astype(jnp.float32)
    kf = k.astype(jnp.float32) * (Dh ** -0.5)
    vf = v.astype(jnp.float32)
    log_i = i_pre.astype(jnp.float32)
    log_f = jax.nn.log_sigmoid(f_pre.astype(jnp.float32))

    def to_chunks(a):
        return jnp.moveaxis(a.reshape((B, H, nc, L) + a.shape[3:]), 2, 0)

    causal = jnp.tril(jnp.ones((L, L), dtype=bool))

    def step(carry, inp):
        C, n, m = carry
        qc, kc, vc, li, lf = inp
        b = jnp.cumsum(lf, axis=-1)
        log_d = b[..., :, None] - b[..., None, :] + li[..., None, :]
        log_d = jnp.where(causal, log_d, -jnp.inf)
        inter = b + m[..., None]
        m_t = jnp.maximum(inter, jnp.max(log_d, axis=-1))
        d = jnp.exp(log_d - m_t[..., None])
        s = jnp.einsum('bhtd,bhsd->bhts', qc, kc) * d
        dec = jnp.exp(inter - m_t)
        num = (jnp.einsum('bhts,bhsd->bhtd', s, vc)
               + dec[..., None] * jnp.einsum('bhtd,bhde->bhte', qc, C))
        den = jnp.sum(s, axis=-1) + dec * jnp.einsum('bhtd,bhd->bht', qc, n)
        h = num / jnp.maximum(jnp.abs(den), jnp.exp(-m_t))[..., None]
        b_last = b[..., -1]
        log_w = b_last[..., None] - b + li
        m_new = jnp.maximum(b_last + m, jnp.max(log_w, axis=-1))
        w = jnp.exp(log_w - m_new[..., None])
        carry_dec = jnp.exp(b_last + m - m_new)
        C_new = carry_dec[..., None, None] * C + jnp.einsum('bhs,bhsd,bhse->bhde', w, kc, vc)
        n_new = carry_dec[..., None] * n + jnp.einsum('bhs,bhsd->bhd', w, kc)
        return (C_new, n_new, m_new), h

    init = (jnp.zeros((B, H, Dh, Dh), jnp.float32),
            jnp.zeros((B, H, Dh), jnp.float32),
            jnp.zeros((B, H), jnp.float32))
    _, hs = lax.scan(step, init, (to_chunks(qf), to_chunks(kf), to_chunks(vf),
                                  to_chunks(log_i), to_chunks(log_f)))
    return jnp.moveaxis(hs, 0, 2).reshape(B, H, S, Dh)

def headwise_layernorm(h, w):
    mu = jnp.mean(h, axis=-1, keepdims=True)
    var = jnp.mean(jnp.square(h - mu), axis=-1, keepdims=True)
    y = (h - mu) * lax.rsqrt(var + LN_EPS)
    b, s = h.shape[:2]
    return y.reshape(b, s, -1) * w.astype(jnp.float32)

def hybrid_layer(x, rel_bias, g_pre, g_post, w_in, conv_w, conv_b, wq_m, wk_m, wv_m,
                 w_if, b_if, mh_norm, skip, w_out):
    B, S, _ = x.shape
    h = rmsnorm(x, g_pre)
    proj = h @ w_in
    aw, mw = ATT_WIDTH, MLSTM_WIDTH
    q_a = proj[..., 0:aw]
    k_a = proj[..., aw:2 * aw]
    v_a = proj[..., 2 * aw:3 * aw]
    g_a = proj[..., 3 * aw:4 * aw]
    x_m = proj[..., 4 * aw:4 * aw + mw]
    z_m = proj[..., 4 * aw + mw:]
    o_a = moba_attention(split_heads(q_a, ATT_HEADS), split_heads(k_a, ATT_HEADS),
                         split_heads(v_a, ATT_HEADS), rel_bias)
    o_a = o_a.transpose(0, 2, 1, 3).reshape(B, S, aw)
    y_a = o_a * jax.nn.silu(g_a)
    x_c = jax.nn.silu(causal_depthwise_conv(x_m, conv_w, conv_b))
    q_m = blockdiag_proj(x_c, wq_m)
    k_m = blockdiag_proj(x_c, wk_m)
    v_m = blockdiag_proj(x_m, wv_m)
    gates = jnp.concatenate([q_m, k_m, v_m], axis=-1) @ w_if + b_if
    i_pre = gates[..., :MLSTM_HEADS].transpose(0, 2, 1)
    f_pre = gates[..., MLSTM_HEADS:].transpose(0, 2, 1)
    h_m = mlstm_chunkwise(split_heads(q_m, MLSTM_HEADS), split_heads(k_m, MLSTM_HEADS),
                          split_heads(v_m, MLSTM_HEADS), i_pre, f_pre)
    h_m = headwise_layernorm(h_m.transpose(0, 2, 1, 3), mh_norm)
    y_m = ((h_m + skip.astype(jnp.float32) * x_c.astype(jnp.float32))
           * jax.nn.silu(z_m.astype(jnp.float32))).astype(x.dtype)
    y = jnp.concatenate([y_a, y_m], axis=-1) @ w_out
    return x + rmsnorm(y, g_post)

def first_inputs(seed: int = 0) -> dict:
    key = jax.random.key(seed)
    ks = jax.random.split(key, 16)
    f32 = jnp.float32
    nblk = MLSTM_WIDTH // QKV_BLOCK
    x = jax.random.normal(ks[0], (BATCH, SEQ, D_MODEL), f32)
    rel_bias = 0.5 * jax.random.normal(ks[1], (REL_BUCKETS, ATT_HEADS), f32)
    g_pre = 1.0 + 0.02 * jax.random.normal(ks[2], (DEPTH, D_MODEL), f32)
    g_post = 1.0 + 0.02 * jax.random.normal(ks[3], (DEPTH, D_MODEL), f32)
    w_in = jax.random.normal(ks[4], (DEPTH, D_MODEL, IN_COLS), f32) * D_MODEL ** -0.5
    conv_w = jax.random.normal(ks[5], (DEPTH, CONV_WIDTH, MLSTM_WIDTH), f32) * CONV_WIDTH ** -0.5
    conv_b = 0.02 * jax.random.normal(ks[6], (DEPTH, MLSTM_WIDTH), f32)
    wq_m = jax.random.normal(ks[7], (DEPTH, nblk, QKV_BLOCK, QKV_BLOCK), f32) * QKV_BLOCK ** -0.5
    wk_m = jax.random.normal(ks[8], (DEPTH, nblk, QKV_BLOCK, QKV_BLOCK), f32) * QKV_BLOCK ** -0.5
    wv_m = jax.random.normal(ks[9], (DEPTH, nblk, QKV_BLOCK, QKV_BLOCK), f32) * QKV_BLOCK ** -0.5
    w_if = jax.random.normal(ks[10], (DEPTH, 3 * MLSTM_WIDTH, 2 * MLSTM_HEADS), f32) * (3 * MLSTM_WIDTH) ** -0.5
    b_i = 0.1 * jax.random.normal(ks[11], (DEPTH, MLSTM_HEADS), f32)
    b_f = (jnp.linspace(3.0, 6.0, MLSTM_HEADS, dtype=f32)[None, :]
           + 0.1 * jax.random.normal(ks[12], (DEPTH, MLSTM_HEADS), f32))
    b_if = jnp.concatenate([b_i, b_f], axis=-1)
    mh_norm = 1.0 + 0.02 * jax.random.normal(ks[13], (DEPTH, MLSTM_WIDTH), f32)
    skip = 1.0 + 0.02 * jax.random.normal(ks[14], (DEPTH, MLSTM_WIDTH), f32)
    w_out = jax.random.normal(ks[15], (DEPTH, MIX_WIDTH, D_MODEL), f32) * MIX_WIDTH ** -0.5
    return {"x": x, "rel_bias": rel_bias, "g_pre": g_pre, "g_post": g_post, "w_in": w_in,
            "conv_w": conv_w, "conv_b": conv_b, "wq_m": wq_m, "wk_m": wk_m, "wv_m": wv_m,
            "w_if": w_if, "b_if": b_if, "mh_norm": mh_norm, "skip": skip, "w_out": w_out}

def first_block(x, rel_bias, g_pre, g_post, w_in, conv_w, conv_b, wq_m, wk_m, wv_m,
              w_if, b_if, mh_norm, skip, w_out):
    for l in range(DEPTH):
        x = hybrid_layer(x, rel_bias, g_pre[l], g_post[l], w_in[l], conv_w[l], conv_b[l],
                         wq_m[l], wk_m[l], wv_m[l], w_if[l], b_if[l], mh_norm[l], skip[l],
                         w_out[l])
    return x


_first_inputs = first_inputs


def first_inputs(seed=0):
    import zlib

    import numpy as np

    out = dict(_first_inputs(seed))
    spreads = {}
    factors = {}
    for name, (base, spread) in spreads.items():
        noise = np.random.default_rng([zlib.crc32(name.encode()), seed]).standard_normal(out[name].shape)
        drawn = base * np.exp(spread * noise) if base else spread * noise
        out[name] = jnp.asarray(drawn.astype(out[name].dtype))
    for name, factor in factors.items():
        out[name] = (out[name] * factor).astype(out[name].dtype)
    return out


_narrow_inputs = first_inputs


def first_inputs(seed=0):

    out = dict(_narrow_inputs(seed))
    wider = {'g_post': 4.77, 'conv_b': 3.23, 'mh_norm': 5.45, 'skip': 8.79}
    for name, times in wider.items():
        mean = out[name].mean()
        out[name] = (mean + times * (out[name] - mean)).astype(out[name].dtype)
    return out


CHUNK = 64
Q_BLOCK = 128
HEAD_DIM = 64
N_DIFF_HEADS = 4
N_SB_HEADS = 8
DIFF_WIDTH = N_DIFF_HEADS * 2 * HEAD_DIM
SB_WIDTH = N_SB_HEADS * HEAD_DIM
MIX_WIDTH_2 = DIFF_WIDTH + SB_WIDTH
IN_WIDTH = 3 * MIX_WIDTH_2
D_FF = 4 * D_MODEL
ROPE_THETA = 10000.0
NORM_EPS = 1e-6
N_MOD = 6


def rms_norm(x, g):
    xf = x.astype(jnp.float32)
    y = xf * lax.rsqrt(jnp.mean(xf * xf, axis=-1, keepdims=True) + NORM_EPS)
    return (y * g.astype(jnp.float32)).astype(x.dtype)

def rope_tables(seq_len, dim):
    inv = 1.0 / (ROPE_THETA ** (jnp.arange(0, dim, 2, dtype=jnp.float32) / dim))
    ang = jnp.arange(seq_len, dtype=jnp.float32)[:, None] * inv[None, :]
    ang = jnp.concatenate([ang, ang], axis=-1)
    return jnp.cos(ang), jnp.sin(ang)

def apply_rope(x, cos, sin):
    x1, x2 = jnp.split(x, 2, axis=-1)
    rot = jnp.concatenate([-x2, x1], axis=-1)
    return (x * cos + rot * sin).astype(x.dtype)

def diff_attention(q, k, v, lam, subln_g, lambda_init):
    seq_len = q.shape[3]
    scale = HEAD_DIM ** -0.5
    outs = []
    for blk in range(seq_len // Q_BLOCK):
        q0 = blk * Q_BLOCK
        kv_len = q0 + Q_BLOCK
        qb = q[:, :, :, q0:kv_len]
        kb = k[:, :, :, :kv_len]
        vb = v[:, :, :kv_len]
        s = jnp.einsum("bhmqd,bhmkd->bhmqk", qb, kb).astype(jnp.float32) * scale
        q_chunk = (q0 + jnp.arange(Q_BLOCK)) // CHUNK
        k_chunk = jnp.arange(kv_len) // CHUNK
        mask = k_chunk[None, :] <= q_chunk[:, None]
        p = jax.nn.softmax(jnp.where(mask, s, -jnp.inf), axis=-1)
        w = p[:, :, 0] - lam * p[:, :, 1]
        outs.append(jnp.einsum("bhqk,bhkd->bhqd", w.astype(vb.dtype), vb))
    o = jnp.concatenate(outs, axis=2)
    return rms_norm(o, subln_g) * (1.0 - lambda_init)

def stick_breaking_attention(q, k, v):
    seq_len = q.shape[2]
    scale = HEAD_DIM ** -0.5
    outs = []
    for blk in range(seq_len // Q_BLOCK):
        q0 = blk * Q_BLOCK
        kv_len = q0 + Q_BLOCK
        qb = q[:, :, q0:kv_len]
        kb = k[:, :, :kv_len]
        vb = v[:, :, :kv_len]
        z = jnp.einsum("bhqd,bhkd->bhqk", qb, kb).astype(jnp.float32) * scale
        t_idx = q0 + jnp.arange(Q_BLOCK)
        s_idx = jnp.arange(kv_len)
        causal = s_idx[None, :] < t_idx[:, None]
        log_beta = jax.nn.log_sigmoid(z)
        log_1m = jnp.where(causal, jax.nn.log_sigmoid(-z), 0.0)
        suffix = lax.cumsum(log_1m, axis=3, reverse=True) - log_1m
        a = jnp.where(causal, jnp.exp(log_beta + suffix), 0.0)
        outs.append(jnp.einsum("bhqk,bhkd->bhqd", a.astype(vb.dtype), vb))
    return jnp.concatenate(outs, axis=2)

def second_inputs(seed: int = 0) -> dict:
    key = jax.random.key(seed)
    ks = jax.random.split(key, 16)
    f32 = jnp.float32
    x = jax.random.normal(ks[0], (BATCH, SEQ, D_MODEL), f32)
    c = jax.random.normal(ks[1], (BATCH, D_MODEL), f32)
    ada_w = jax.random.normal(ks[2], (DEPTH, D_MODEL, N_MOD * D_MODEL), f32) * (0.5 * D_MODEL ** -0.5)
    ada_b = jax.random.normal(ks[3], (DEPTH, N_MOD * D_MODEL), f32) * 0.01
    mix_norm_g = 1.0 + 0.02 * jax.random.normal(ks[4], (DEPTH, D_MODEL), f32)
    w_in = jax.random.normal(ks[5], (DEPTH, D_MODEL, IN_WIDTH), f32) * D_MODEL ** -0.5
    lambda_q1 = 0.1 * jax.random.normal(ks[6], (DEPTH, HEAD_DIM), f32)
    lambda_k1 = 0.1 * jax.random.normal(ks[7], (DEPTH, HEAD_DIM), f32)
    lambda_q2 = 0.1 * jax.random.normal(ks[8], (DEPTH, HEAD_DIM), f32)
    lambda_k2 = 0.1 * jax.random.normal(ks[9], (DEPTH, HEAD_DIM), f32)
    diff_subln_g = 1.0 + 0.02 * jax.random.normal(ks[10], (DEPTH, 2 * HEAD_DIM), f32)
    w_out = jax.random.normal(ks[11], (DEPTH, MIX_WIDTH_2, D_MODEL), f32) * MIX_WIDTH_2 ** -0.5
    ffn_norm_g = 1.0 + 0.02 * jax.random.normal(ks[12], (DEPTH, D_MODEL), f32)
    w_ff1 = jax.random.normal(ks[13], (DEPTH, D_MODEL, D_FF), f32) * D_MODEL ** -0.5
    w_ff2 = jax.random.normal(ks[14], (DEPTH, D_FF, D_MODEL), f32) * D_FF ** -0.5
    final_norm_g = 1.0 + 0.02 * jax.random.normal(ks[15], (D_MODEL,), f32)
    return {"x": x, "c": c, "ada_w": ada_w, "ada_b": ada_b, "mix_norm_g": mix_norm_g,
            "w_in": w_in, "lambda_q1": lambda_q1, "lambda_k1": lambda_k1,
            "lambda_q2": lambda_q2, "lambda_k2": lambda_k2, "diff_subln_g": diff_subln_g,
            "w_out": w_out, "ffn_norm_g": ffn_norm_g, "w_ff1": w_ff1, "w_ff2": w_ff2,
            "final_norm_g": final_norm_g}

def second_block(x, c, ada_w, ada_b, mix_norm_g, w_in, lambda_q1, lambda_k1, lambda_q2,
              lambda_k2, diff_subln_g, w_out, ffn_norm_g, w_ff1, w_ff2, final_norm_g):
    bsz, seq_len, _ = x.shape
    cos, sin = rope_tables(seq_len, HEAD_DIM)
    cos = cos.astype(x.dtype)
    sin = sin.astype(x.dtype)
    c_act = jax.nn.silu(c)
    for layer in range(DEPTH):
        lambda_init = 0.8 - 0.6 * math.exp(-0.3 * layer)
        mod = c_act @ ada_w[layer] + ada_b[layer]
        sh_m, sc_m, g_m, sh_f, sc_f, g_f = [m[:, None, :] for m in jnp.split(mod, N_MOD, axis=-1)]

        h = rms_norm(x, mix_norm_g[layer]) * (1.0 + sc_m) + sh_m
        proj = h @ w_in[layer]
        dq, dk, dv, sq, sk, sv = jnp.split(proj, 6, axis=-1)
        dq = dq.reshape(bsz, seq_len, N_DIFF_HEADS, 2, HEAD_DIM).transpose(0, 2, 3, 1, 4)
        dk = dk.reshape(bsz, seq_len, N_DIFF_HEADS, 2, HEAD_DIM).transpose(0, 2, 3, 1, 4)
        dv = dv.reshape(bsz, seq_len, N_DIFF_HEADS, 2 * HEAD_DIM).transpose(0, 2, 1, 3)
        dq = apply_rope(dq, cos, sin)
        dk = apply_rope(dk, cos, sin)
        lam = (jnp.exp(jnp.sum(lambda_q1[layer].astype(jnp.float32) * lambda_k1[layer].astype(jnp.float32)))
               - jnp.exp(jnp.sum(lambda_q2[layer].astype(jnp.float32) * lambda_k2[layer].astype(jnp.float32)))
               + lambda_init)
        o_diff = diff_attention(dq, dk, dv, lam, diff_subln_g[layer], lambda_init)
        o_diff = o_diff.transpose(0, 2, 1, 3).reshape(bsz, seq_len, DIFF_WIDTH)

        sq = sq.reshape(bsz, seq_len, N_SB_HEADS, HEAD_DIM).transpose(0, 2, 1, 3)
        sk = sk.reshape(bsz, seq_len, N_SB_HEADS, HEAD_DIM).transpose(0, 2, 1, 3)
        sv = sv.reshape(bsz, seq_len, N_SB_HEADS, HEAD_DIM).transpose(0, 2, 1, 3)
        o_sb = stick_breaking_attention(sq, sk, sv)
        o_sb = o_sb.transpose(0, 2, 1, 3).reshape(bsz, seq_len, SB_WIDTH)

        mixed = jnp.concatenate([o_diff, o_sb], axis=-1) @ w_out[layer]
        x = x + g_m * mixed

        h = rms_norm(x, ffn_norm_g[layer]) * (1.0 + sc_f) + sh_f
        f = jnp.square(jax.nn.relu(h @ w_ff1[layer])) @ w_ff2[layer]
        x = x + g_f * f
    return rms_norm(x, final_norm_g)


DEPTH_3 = 2

MEM_LEN = 256
MEM_HEADS = 4
MEM_WIDTH = MEM_HEADS * HEAD_DIM
MIX_WIDTH_3 = D_MODEL
CONV_CH = MIX_WIDTH_3 - MEM_WIDTH
CONV_WIDTH_3 = 31
SWA_Q_HEADS = 12
SWA_KV_HEADS = 4
SWA_GROUP = SWA_Q_HEADS // SWA_KV_HEADS
SWA_Q_WIDTH = SWA_Q_HEADS * HEAD_DIM
SWA_KV_WIDTH = SWA_KV_HEADS * HEAD_DIM
WINDOW = 128
BLOCK = 128
D_FF_DENSE = 2816
N_EXPERTS = 8
TOP_K = 2
D_FF_EXPERT = 3584
N_EVEN = (DEPTH_3 + 1) // 2
N_ODD = DEPTH_3 // 2
ALIBI_MAX_BIAS = 8.0
NEG_INF = -1e30


def rms_norm_3(x, g):
    xf = x.astype(jnp.float32)
    y = xf * lax.rsqrt(jnp.mean(xf * xf, axis=-1, keepdims=True) + RMS_EPS)
    return (y * g.astype(jnp.float32)).astype(x.dtype)

def layer_norm(x, g, b):
    xf = x.astype(jnp.float32)
    mu = jnp.mean(xf, axis=-1, keepdims=True)
    var = jnp.mean(jnp.square(xf - mu), axis=-1, keepdims=True)
    y = (xf - mu) * lax.rsqrt(var + LN_EPS)
    return (y * g.astype(jnp.float32) + b.astype(jnp.float32)).astype(x.dtype)

def swiglu(h, w_gate, w_up, w_down):
    return (jax.nn.silu(h @ w_gate) * (h @ w_up)) @ w_down

def alibi_slopes(n_heads):
    return jnp.exp2(-ALIBI_MAX_BIAS * (jnp.arange(n_heads, dtype=jnp.float32) + 1.0) / n_heads)

def memory_attention(q, q_g, mem_k, mem_v):
    b, s, _ = q.shape
    q = rms_norm_3(q.reshape(b, s, MEM_HEADS, HEAD_DIM), q_g)
    sc = jnp.einsum('bshd,bmhd->bhsm', q, mem_k).astype(jnp.float32) * (HEAD_DIM ** -0.5)
    p = jax.nn.softmax(sc, axis=-1).astype(mem_v.dtype)
    o = jnp.einsum('bhsm,bmhd->bshd', p, mem_v)
    return o.reshape(b, s, MEM_WIDTH)

def conv_mixer(h, w_in, b_glu, dw_w, dw_b, ln_g, ln_b, memq_g, w_out, mem_k, mem_v):
    proj = h @ w_in
    a = proj[..., :CONV_CH] + b_glu[:CONV_CH]
    gate = proj[..., CONV_CH:2 * CONV_CH] + b_glu[CONV_CH:]
    q_mem = proj[..., 2 * CONV_CH:]
    u = a * jax.nn.sigmoid(gate)
    u_pad = jnp.pad(u, ((0, 0), (CONV_WIDTH_3 - 1, 0), (0, 0)))
    c = lax.conv_general_dilated(
        u_pad, dw_w[:, None, :], window_strides=(1,), padding='VALID',
        dimension_numbers=('NWC', 'WIO', 'NWC'), feature_group_count=CONV_CH) + dw_b
    c = jax.nn.silu(layer_norm(c, ln_g, ln_b))
    m = memory_attention(q_mem, memq_g, mem_k, mem_v)
    return jnp.concatenate([c, m], axis=-1) @ w_out

def swa_mixer(h, w_in, q_g, k_g, sinks, memq_g, w_out, mem_k, mem_v):
    b, s, _ = h.shape
    nb = s // BLOCK
    proj = h @ w_in
    o1 = SWA_Q_WIDTH
    o2 = o1 + SWA_KV_WIDTH
    o3 = o2 + SWA_KV_WIDTH
    q = rms_norm_3(proj[..., :o1].reshape(b, s, SWA_KV_HEADS, SWA_GROUP, HEAD_DIM), q_g)
    k = rms_norm_3(proj[..., o1:o2].reshape(b, s, SWA_KV_HEADS, HEAD_DIM), k_g)
    v = proj[..., o2:o3].reshape(b, s, SWA_KV_HEADS, HEAD_DIM)
    q_mem = proj[..., o3:]

    qb = q.reshape(b, nb, BLOCK, SWA_KV_HEADS, SWA_GROUP, HEAD_DIM)
    def band(t):
        prev = jnp.pad(t, ((0, 0), (BLOCK, 0), (0, 0), (0, 0)))[:, :s]
        return jnp.concatenate([prev.reshape(b, nb, BLOCK, SWA_KV_HEADS, HEAD_DIM),
                                t.reshape(b, nb, BLOCK, SWA_KV_HEADS, HEAD_DIM)], axis=2)
    kk = band(k)
    vv = band(v)
    sc = jnp.einsum('bnqhgd,bnchd->bnhgqc', qb, kk).astype(jnp.float32) * (HEAD_DIM ** -0.5)

    qpos = jnp.arange(BLOCK) + BLOCK
    kpos = jnp.arange(2 * BLOCK)
    dist = (qpos[:, None] - kpos[None, :]).astype(jnp.float32)
    win = (dist >= 0) & (dist < WINDOW)
    first = (jnp.arange(nb)[:, None] > 0) | (kpos[None, :] >= BLOCK)
    mask = win[None, :, :] & first[:, None, :]
    slopes = alibi_slopes(SWA_Q_HEADS).reshape(SWA_KV_HEADS, SWA_GROUP)
    bias = -slopes[:, :, None, None] * dist[None, None]
    sc = jnp.where(mask[None, :, None, None], sc + bias[None, None], NEG_INF)

    sink = jnp.broadcast_to(sinks.astype(jnp.float32).reshape(1, 1, SWA_KV_HEADS, SWA_GROUP, 1, 1),
                            sc.shape[:-1] + (1,))
    p = jax.nn.softmax(jnp.concatenate([sc, sink], axis=-1), axis=-1)[..., :-1]
    o = jnp.einsum('bnhgqc,bnchd->bnqhgd', p.astype(vv.dtype), vv).reshape(b, s, SWA_Q_WIDTH)
    m = memory_attention(q_mem, memq_g, mem_k, mem_v)
    return jnp.concatenate([o, m], axis=-1) @ w_out

def moe_swiglu(h, router, we_gate, we_up, we_down):
    logits = (h @ router).astype(jnp.float32)
    top_v, top_i = lax.top_k(logits, TOP_K)
    top_w = jax.nn.softmax(top_v, axis=-1)
    gates = jnp.sum(jax.nn.one_hot(top_i, N_EXPERTS, dtype=jnp.float32) * top_w[..., None], axis=-2)
    gates = gates.astype(h.dtype)
    out = jnp.zeros_like(h)
    for e in range(N_EXPERTS):
        out = out + gates[..., e:e + 1] * swiglu(h, we_gate[e], we_up[e], we_down[e])
    return out

def third_inputs(seed: int = 0) -> dict:
    key = jax.random.key(seed)
    ks = iter(jax.random.split(key, 40))
    f32 = jnp.float32
    def nrm(shape, scale):
        return jax.random.normal(next(ks), shape, f32) * scale
    def gain(shape):
        return 1.0 + 0.05 * jax.random.normal(next(ks), shape, f32)
    D = D_MODEL
    return {
        "x": nrm((BATCH, SEQ, D), 1.0),
        "mem": nrm((BATCH, MEM_LEN, D), 1.0),
        "mem_norm_g": gain((D,)),
        "w_mem_kv": nrm((D, 2 * MEM_WIDTH), D ** -0.5),
        "mem_k_norm_g": gain((HEAD_DIM,)),
        "cv_attn_norm_g": gain((N_EVEN, D)),
        "cv_w_in": nrm((N_EVEN, D, 2 * CONV_CH + MEM_WIDTH), D ** -0.5),
        "cv_b_glu": nrm((N_EVEN, 2 * CONV_CH), 0.02),
        "cv_dw_w": nrm((N_EVEN, CONV_WIDTH_3, CONV_CH), CONV_WIDTH_3 ** -0.5),
        "cv_dw_b": nrm((N_EVEN, CONV_CH), 0.02),
        "cv_ln_g": gain((N_EVEN, CONV_CH)),
        "cv_ln_b": nrm((N_EVEN, CONV_CH), 0.02),
        "cv_memq_norm_g": gain((N_EVEN, HEAD_DIM)),
        "cv_w_out": nrm((N_EVEN, MIX_WIDTH_3, D), MIX_WIDTH_3 ** -0.5),
        "cv_ffn_norm_g": gain((N_EVEN, D)),
        "cv_w_gate": nrm((N_EVEN, D, D_FF_DENSE), D ** -0.5),
        "cv_w_up": nrm((N_EVEN, D, D_FF_DENSE), D ** -0.5),
        "cv_w_down": nrm((N_EVEN, D_FF_DENSE, D), D_FF_DENSE ** -0.5),
        "sw_attn_norm_g": gain((N_ODD, D)),
        "sw_w_in": nrm((N_ODD, D, SWA_Q_WIDTH + 2 * SWA_KV_WIDTH + MEM_WIDTH), D ** -0.5),
        "sw_q_norm_g": gain((N_ODD, HEAD_DIM)),
        "sw_k_norm_g": gain((N_ODD, HEAD_DIM)),
        "sw_sinks": nrm((N_ODD, SWA_Q_HEADS), 0.5),
        "sw_memq_norm_g": gain((N_ODD, HEAD_DIM)),
        "sw_w_out": nrm((N_ODD, MIX_WIDTH_3, D), MIX_WIDTH_3 ** -0.5),
        "sw_ffn_norm_g": gain((N_ODD, D)),
        "sw_router": nrm((N_ODD, D, N_EXPERTS), D ** -0.5),
        "sw_we_gate": nrm((N_ODD, N_EXPERTS, D, D_FF_EXPERT), D ** -0.5),
        "sw_we_up": nrm((N_ODD, N_EXPERTS, D, D_FF_EXPERT), D ** -0.5),
        "sw_we_down": nrm((N_ODD, N_EXPERTS, D_FF_EXPERT, D), D_FF_EXPERT ** -0.5),
    }

def third_block(x, mem, mem_norm_g, w_mem_kv, mem_k_norm_g,
              cv_attn_norm_g, cv_w_in, cv_b_glu, cv_dw_w, cv_dw_b, cv_ln_g, cv_ln_b,
              cv_memq_norm_g, cv_w_out, cv_ffn_norm_g, cv_w_gate, cv_w_up, cv_w_down,
              sw_attn_norm_g, sw_w_in, sw_q_norm_g, sw_k_norm_g, sw_sinks, sw_memq_norm_g,
              sw_w_out, sw_ffn_norm_g, sw_router, sw_we_gate, sw_we_up, sw_we_down):
    b, m_len, _ = mem.shape
    mkv = rms_norm_3(mem, mem_norm_g) @ w_mem_kv
    mem_k = rms_norm_3(mkv[..., :MEM_WIDTH].reshape(b, m_len, MEM_HEADS, HEAD_DIM), mem_k_norm_g)
    mem_v = mkv[..., MEM_WIDTH:].reshape(b, m_len, MEM_HEADS, HEAD_DIM)

    h = x
    for i in range(DEPTH_3):
        j = i // 2
        if i % 2 == 0:
            hn = rms_norm_3(h, cv_attn_norm_g[j])
            h = h + conv_mixer(hn, cv_w_in[j], cv_b_glu[j], cv_dw_w[j], cv_dw_b[j], cv_ln_g[j],
                               cv_ln_b[j], cv_memq_norm_g[j], cv_w_out[j], mem_k, mem_v)
            hn = rms_norm_3(h, cv_ffn_norm_g[j])
            h = h + swiglu(hn, cv_w_gate[j], cv_w_up[j], cv_w_down[j])
        else:
            hn = rms_norm_3(h, sw_attn_norm_g[j])
            h = h + swa_mixer(hn, sw_w_in[j], sw_q_norm_g[j], sw_k_norm_g[j], sw_sinks[j],
                              sw_memq_norm_g[j], sw_w_out[j], mem_k, mem_v)
            hn = rms_norm_3(h, sw_ffn_norm_g[j])
            h = h + moe_swiglu(hn, sw_router[j], sw_we_gate[j], sw_we_up[j], sw_we_down[j])
    return h


def setup_inputs(seed=0):
    out = dict(first_inputs(seed))
    for name, value in second_inputs(seed + 1).items():
        if name != "x":
            out[name + "_2"] = value
    for name, value in third_inputs(seed + 2).items():
        if name != "x":
            out[name + "_3"] = value
    return out


def reference(
    x, rel_bias, g_pre, g_post, w_in, conv_w, conv_b, wq_m, wk_m, wv_m, w_if, b_if, mh_norm,
    skip, w_out, c_2, ada_w_2, ada_b_2, mix_norm_g_2, w_in_2, lambda_q1_2, lambda_k1_2,
    lambda_q2_2, lambda_k2_2, diff_subln_g_2, w_out_2, ffn_norm_g_2, w_ff1_2, w_ff2_2,
    final_norm_g_2, mem_3, mem_norm_g_3, w_mem_kv_3, mem_k_norm_g_3, cv_attn_norm_g_3,
    cv_w_in_3, cv_b_glu_3, cv_dw_w_3, cv_dw_b_3, cv_ln_g_3, cv_ln_b_3, cv_memq_norm_g_3,
    cv_w_out_3, cv_ffn_norm_g_3, cv_w_gate_3, cv_w_up_3, cv_w_down_3, sw_attn_norm_g_3,
    sw_w_in_3, sw_q_norm_g_3, sw_k_norm_g_3, sw_sinks_3, sw_memq_norm_g_3, sw_w_out_3,
    sw_ffn_norm_g_3, sw_router_3, sw_we_gate_3, sw_we_up_3, sw_we_down_3,
):
    x = first_block(
        x, rel_bias, g_pre, g_post, w_in, conv_w, conv_b, wq_m, wk_m, wv_m, w_if, b_if, mh_norm,
        skip, w_out,
    )
    x = second_block(
        x, c_2, ada_w_2, ada_b_2, mix_norm_g_2, w_in_2, lambda_q1_2, lambda_k1_2, lambda_q2_2,
        lambda_k2_2, diff_subln_g_2, w_out_2, ffn_norm_g_2, w_ff1_2, w_ff2_2, final_norm_g_2,
    )
    return third_block(
        x, mem_3, mem_norm_g_3, w_mem_kv_3, mem_k_norm_g_3, cv_attn_norm_g_3, cv_w_in_3,
        cv_b_glu_3, cv_dw_w_3, cv_dw_b_3, cv_ln_g_3, cv_ln_b_3, cv_memq_norm_g_3, cv_w_out_3,
        cv_ffn_norm_g_3, cv_w_gate_3, cv_w_up_3, cv_w_down_3, sw_attn_norm_g_3, sw_w_in_3,
        sw_q_norm_g_3, sw_k_norm_g_3, sw_sinks_3, sw_memq_norm_g_3, sw_w_out_3, sw_ffn_norm_g_3,
        sw_router_3, sw_we_gate_3, sw_we_up_3, sw_we_down_3,
    )


_drawn_inputs = setup_inputs


def setup_inputs(seed=0):
    import zlib

    import numpy as np

    out = dict(_drawn_inputs(seed))
    spreads = {}
    factors = {'mix_norm_g_2': 6.391,
     'lambda_q1_2': 3.499,
     'lambda_k1_2': 3.386,
     'lambda_k2_2': 3.326,
     'diff_subln_g_2': 3.196,
     'ffn_norm_g_2': 3.861,
     'mem_norm_g_3': 2.861,
     'mem_k_norm_g_3': 4.863,
     'cv_memq_norm_g_3': 5.591,
     'sw_k_norm_g_3': 2.979,
     'sw_memq_norm_g_3': 6.935}
    for name, (base, spread) in spreads.items():
        noise = np.random.default_rng([zlib.crc32(name.encode()), seed]).standard_normal(out[name].shape)
        drawn = base * np.exp(spread * noise) if base else spread * noise
        out[name] = jnp.asarray(drawn.astype(out[name].dtype))
    for name, factor in factors.items():
        out[name] = (out[name] * factor).astype(out[name].dtype)
    return out
```

```python
from contextlib import ExitStack

import numpy as np

import concourse.bass as bass
from concourse import mybir

F32 = mybir.dt.float32
I32 = mybir.dt.int32
ALU = mybir.AluOpType
ACT = mybir.ActivationFunctionType
AX = mybir.AxisListType.X

P = 128
S = 256
NT = S // P
D = 1024
KC = D // P
HEADS1, DH1 = 8, 128
MH, MD = 4, 256
H64 = 64
NDIFF, NSB = 4, 8
FF2 = 4096
CONV, CONVW = 768, 31
CC = CONV // P
MEMH = 4
SWAH, SWAKV = 12, 4
FFD = 2816
NEXP, FFE = 8, 3584
EXTRA = (2 * S) // (P + 1)
NROUND = NEXP + EXTRA
RING = 7
PIECE = 2048
NEG = -1e30
RMS_EPS, LN_EPS = 1e-6, 1e-5
LAMBDA_INIT = 0.2

ROUND_JOBS = 28
B1_BETWEEN = {0: 3072, 1: 3584, 3: 4096, 5: 4608, 7: 5120, 9: 5632}
T384 = [(0, 0, 1), (1, 128, 2)]
T512 = [(0, 0, 2), (1, 256, 2)]


def constants():
    p = np.arange(P)[:, None]
    t = np.arange(S)[None, :]
    f = np.float32
    causal = np.concatenate([np.where(t[:, :P] <= p, 0, NEG), np.where(t <= p + P, 0, NEG)], 1)
    chunk = np.concatenate([np.where(t[:, :P] // 64 <= p // 64, 0, NEG), np.where(t // 64 <= (p + P) // 64, 0, NEG)], 1)
    d0, d1 = p - t[:, :P], p + P - t
    dist = np.concatenate([d0, d1], 1)
    window = np.where((dist >= 0) & (dist < 128), 0, NEG)
    inv = (1.0 / (f(10000.0) ** (np.arange(0, 64, 2, dtype=f) / f(64)))).astype(f)
    ang = (np.arange(S, dtype=f)[:, None] * inv[None, :]).astype(f)
    ang = np.concatenate([ang, ang], 1)
    cos, sin = np.cos(ang).T, np.sin(ang).T
    rot = np.zeros((P, P))
    for h in (0, 64):
        for i in range(32):
            rot[h + 32 + i, h + i] = -1.0
            rot[h + i, h + 32 + i] = 1.0
    n = np.arange(511) - 255
    d = np.maximum(-n, 0)
    nf = np.maximum(d, 1).astype(f)
    large = 16 + (np.log(nf / f(16)) / f(np.log(2048 / 16)) * f(16)).astype(np.int32)
    bucket = np.where(d < 16, d, np.minimum(large, 31))
    rel = np.zeros((P, 511))
    rel[bucket, np.arange(511)] = 1.0
    rel[:, n > 0] = 0.0
    rel[32, n > 0] = NEG
    e, j = np.arange(8)[:, None], np.arange(8)[None, :]
    hsel = np.zeros((P, MH, P))
    for h in range(MH):
        hsel[h, h] = 1.0
    parts = {
        "ident": np.eye(P), "ones": np.ones((P, P)),
        "upto": np.concatenate([p <= t, p + P <= t], 1), "before": np.concatenate([p < t, p + P < t], 1),
        "after": p > t[:, :P], "causal": causal, "chunk": chunk,
        "earlier": np.concatenate([p < t, p + P < t[:, P:]], 1), "dist": np.maximum(dist, 0), "window": window,
        "block4": np.repeat(p // 4 == np.arange(32)[None, :], 4, 1), "half": (p // 64) == (np.arange(P)[None, :] // 64),
        "rot": rot, "cos": np.tile(cos, (2, 1)), "sin": np.tile(sin, (2, 1)), "rel": rel, "hsel": hsel.reshape(P, -1),
        "iota": np.broadcast_to(np.arange(P)[None, :], (P, P)), "lower": np.broadcast_to((j < e).reshape(1, 64), (P, 64)),
        "eid": np.broadcast_to(np.arange(8)[None, :], (P, 8)), "slots": np.broadcast_to(np.arange(4)[None, :], (P, 4)),
        "eps": np.broadcast_to(np.array([[RMS_EPS, LN_EPS]]), (P, 2)),
    }
    at, out, n = {}, [], 0
    for k, a in parts.items():
        at[k] = (n, n + a.shape[1])
        n += a.shape[1]
        out.append(np.asarray(a, f))
    return np.ascontiguousarray(np.concatenate(out, 1)), at


class Signal:
    def __init__(self, name, sem, val, base):
        self.name, self.sem, self.val, self.base = name, sem, val, base


class Count:

    def __init__(self, known=None):
        self.known, self.seen, self.n, self.sems = known, {}, {}, {}
        self.loop, self.start, self.per = None, {}, {}

    def sem(self, name):
        if name not in self.sems:
            self.sems[name] = self.make(name)
        return self.sems[name]

    def enter(self, r):
        self.loop, self.start = r, dict(self.n)

    def leave(self):
        for b in range(4):
            self.per[f"filled{b}"] = self.per[f"drained{b}"] = ROUND_JOBS // 4
        for k, v in self.n.items():
            if v != self.start.get(k, 0) and k not in self.per:
                self.per[k] = v - self.start.get(k, 0)
        self.loop = None

    def value(self, name, v):
        per = self.known.per.get(name, 0) if self.known else 0
        return v if self.loop is None or per == 0 else self.loop * per + v

    def sig(self, name, *key, by=1):
        self.n[name] = self.n.get(name, 0) + by
        self.seen[(name,) + key] = self.n[name]
        return Signal(name, self.sem(name), self.value(name, self.n[name]), self.n[name])

    def at(self, name, *key):
        v = self.known.seen[(name,) + key] if self.known else 1
        return self.sem(name), self.value(name, v)

    def before(self, name, *key):
        v = self.known.seen[(name,) + key] - self.known.per[name] if self.known else 1
        return self.sem(name), self.value(name, v)


class Jobs:

    def __init__(self, count, known=None):
        self.c, self.known, self.n, self.seen = count, known, 0, {}

    def number(self, *key):
        return self.known.seen[key] if self.known else self.seen.get(key, 0)

    def bank(self, *key):
        return self.number(*key) % 4

    def fill(self, pe, *key):
        n = self.n
        self.seen[key] = n
        self.n += 1
        if n >= 4:
            name = f"drained{n % 4}"
            pe.wait_ge(self.c.sem(name), self.c.value(name, n // 4))
        return n % 4

    def filled(self, *key):
        n = self.number(*key)
        name = f"filled{n % 4}"
        self.c.n[name] = max(self.c.n.get(name, 0), n // 4 + 1)
        return Signal(name, self.c.sem(name), self.c.value(name, n // 4 + 1), n // 4 + 1)

    def full(self, *key):
        n = self.number(*key)
        name = f"filled{n % 4}"
        return self.c.sem(name), self.c.value(name, n // 4 + 1)

    def free(self, *key):
        n = self.number(*key)
        name = f"drained{n % 4}"
        self.c.n[name] = max(self.c.n.get(name, 0), n // 4 + 1)
        return Signal(name, self.c.sem(name), self.c.value(name, n // 4 + 1), n // 4 + 1)

    def emptied(self, *key):
        n = self.number(*key)
        name = f"drained{n % 4}"
        return self.c.sem(name), self.c.value(name, n // 4 + 1)


class Stream:

    def __init__(self, count, known=None):
        self.c, self.known, self.n, self.number, self.freed = count, known, 0, {}, {}
        self.slot, self.landing = [0] * RING, {}

    def free(self, key, signal):
        n = self.number[key]
        self.freed[n] = (signal.name, signal.base)


def program(nc, A, out, const_at, known=None, upto=9):
    c = Count(known[0] if known else None)
    J = Jobs(c, known[1] if known else None)
    W = Stream(c, known[2] if known else None)
    ctx = ExitStack()
    with ctx:
        c.make = lambda name: ctx.enter_context(nc.semaphore(name))
        if known:
            for name in known[0].sems:
                c.sem(name)

        def sb(name, *shape, dt=F32):
            return ctx.enter_context(nc.sbuf_tensor(name, [P, *shape], dt))

        consts = sb("consts", max(b for _, b in const_at.values()))

        def C(name, n=0):
            a, b = const_at[name]
            v = consts[:, a:b]
            return v.rearrange("p (a b) -> p a b", a=n) if n else v

        ident, ones = C("ident"), C("ones")
        ring = sb("ring", RING, PIECE)
        arena = sb("arena", 16 * 1024)
        xres = sb("xres", NT, D)
        nrm = sb("nrm", NT, D)
        hT = sb("hT", KC, S)
        logit = sb("logit", 4, 512)
        probT = sb("probT", 2, 512)
        junk = sb("junk", D)
        bd = sb("bd", 24, P)
        wide = sb("wide", D)
        vcol = sb("vcol", 4, P)
        st = sb("st", 64)
        smx = sb("smx", 4, 8)
        gl = sb("gl", 2, 8)
        lg = sb("lg", 2, 24)
        aT = sb("aT", 512)
        fcol = sb("fcol", 2, 4)
        mcol = sb("mcol", 4, 16)
        half_c = sb("half_c", 16)
        relb = sb("relb", HEADS1)
        brow = sb("brow", 8)
        sinkb = sb("sinkb", SWAH)
        fsink = sb("fsink", SWAH)
        lamv = sb("lamv", 4, H64)
        lam = sb("lam", 4)
        wif = sb("wif", 24, 8)
        wraw = sb("wraw", 24, 4)
        rw = sb("rw", KC, NEXP)
        modc = sb("modc", 32)
        rt = sb("rt", 6, NT, NEXP)
        cmp = sb("cmp", 2, NT * 64)
        pos = sb("pos", 3, NT, NROUND + 1)
        xtr = sb("xtr", 8, 8)
        rid = sb("rid", 16)
        ridi = sb("ridi", 16, dt=I32)
        ps = [ctx.enter_context(nc.psum_tensor(f"bank{i}", [P, 512], F32)) for i in range(4)]
        acc = [ctx.enter_context(nc.psum_tensor(f"sum{i}", [P, 512], F32)) for i in range(4)]
        relrow = nc.dram_tensor("relrow", (P, HEADS1, 511), F32, kind="Internal").ap()

        def U(unit, *dims, off=0):
            n = int(np.prod(dims))
            v = arena[:, unit * 1024 + off:unit * 1024 + off + n]
            return v.rearrange("p (a b) -> p a b", a=dims[0]) if len(dims) == 2 else v

        relrep = U(0, HEADS1, 512)
        relw = logit[:, 0:2, :].rearrange("p a (b n) -> p (a b) n", n=P)
        mix1 = U(0, 16, S)
        relbias = U(4, HEADS1, 384)
        qT, kT, vt = U(8, 8, S), U(10, 8, S), U(12, NT, D)
        xmT, xcT, vm = U(14, 8, S), U(4, 8, S), U(6, NT, D)
        qmT, kmT, vmT = U(8, 8, S), U(10, 8, S), U(12, 8, S)
        vrows = [U(15, P, off=P * g) for g in range(4)]
        qraw = U(10, 4, 512)
        qdT, kdT, vd = U(0, 4, S), U(1, 4, S), U(2, NT, 512)
        sqT, skT, sv = U(3, 4, S), U(4, 4, S), U(5, NT, 512)
        mix2, fT = U(6, 8, S), U(0, 32, S)
        gm, gf = U(8, D), U(9, D)
        sbw = U(12, 2, 2048)
        cact = U(10, KC, P)
        memkT, memv = U(15, 2, S), U(15, NT, 256, off=512)
        memx = U(12, NT, D)
        uT, cT = U(0, CC, S), U(2, CC, S)
        mqT, mq2 = U(4, 2, S), U(4, 512, off=512)
        sg3 = U(8, 4, 512)
        lnw = U(10, 4, S)
        sq3 = U(13, CC, S)
        mix3 = U(6, 8, S)
        actd = U(0, 22, S)
        rsw = U(11, 2, 512)
        swq, swk = U(0, 6, S), U(2, 2, S)
        swv = U(3, NT, 256)
        hgT, eact, actT, ey = U(0, KC, P), U(1, 2, 512), U(2, 28, P), U(6, D)
        Pm, PG, pgT, esg = U(7, NT, P), U(7, NT, P, off=256), U(8, S), U(9, 2, 512)

        vgroups = [
            [("g_pre", 8), ("conv_w", 32), ("conv_b", 8), ("mh_norm", 8), ("skip", 8), ("mix_norm_g_2", 8),
             ("ffn_norm_g_2", 8), ("ada_b_2", 48)],
            [("c_2", 8), ("mem_norm_g_3", 8), ("cv_attn_norm_g_3", 8), ("cv_b_glu_3", 12), ("cv_dw_b_3", 6),
             ("cv_ln_g_3", 6), ("cv_ln_b_3", 6), ("cv_ffn_norm_g_3", 8), ("sw_attn_norm_g_3", 8),
             ("sw_ffn_norm_g_3", 8), ("diff_subln_g_2", 1), ("cv_memq_norm_g_3", 0), ("sw_q_norm_g_3", 0),
             ("sw_memq_norm_g_3", 0), ("mem_k_norm_g_3", 0), ("sw_k_norm_g_3", 0)],
            [("cv_dw_w_3", 96)], [("cv_dw_w_3", 90)],
        ]
        vat, vload = {}, []
        for g, group in enumerate(vgroups):
            r, loads = 0, []
            for name, n in group:
                src = A[name]
                src = src.rearrange({1: "a -> a", 2: "a b -> (a b)", 3: "a b c -> (a b c)"}[len(src.shape)])
                if n == 0:
                    for h in range(2):
                        loads.append((vrows[g][r:r + 1, h * H64:(h + 1) * H64], src.rearrange("(a b) -> a b", a=1)))
                else:
                    first = 96 if g == 3 else 0
                    loads.append((vrows[g][r:r + n, :], src.rearrange("(a b) -> a b", b=P)[first:first + n, :]))
                vat.setdefault(name, (g, r))
                r += n or 1
            vload.append((r, loads))

        def vec(name, i=0):
            g, r = vat[name]
            if name == "cv_dw_w_3" and i >= 96:
                g, r, i = 3, 0, i - 96
            return vcol[:, g, r + i:r + i + 1]

        def everywhere(src, n):
            return bass.AP(tensor=src.tensor, offset=src.offset, ap=[[0, P], [1, n]])

        block = ctx.enter_context(nc.Block())

        @block.sync
        def _(sp):
            sp.dma_start(xres[:, :, :], A["x"].rearrange("a (t p) d -> p (a t) d", p=P)).then_inc(c.sem("x_in"), 16)
            sp.dma_start(consts[:, :], A["consts"]).then_inc(c.sem("consts_in"), 16)
            base = [None]

            def piece(key, *loads):
                n = W.n
                W.n += 1
                W.number[key] = n
                s = n % RING
                if base[0] is not None and n - RING < base[0]:
                    name, v = W.known.freed[n - RING + 6 * RING] if W.known else ("piece_used", 1)
                    sp.wait_ge(c.sem(name), c.value(name, v - (c.known.per[name] if c.known else 0)))
                elif n >= RING:
                    name, v = W.known.freed[n - RING] if W.known else ("piece_used", 1)
                    sp.wait_ge(c.sem(name), c.value(name, v))
                for dst, src in loads:
                    sp.dma_start(dst(ring[:, s, :]), src).then_inc(c.sem(f"landed{s}"), 16)
                    W.slot[s] += 16
                W.landing[key] = (s, W.slot[s])

            def shaped(a, b, lo=0, hi=None):
                return lambda slot: slot[:, 0:a * b].rearrange("p (a b) -> p a b", a=a)[:, :, lo:b if hi is None else hi]

            def columns(name, w, col, cols=512):
                v = w.rearrange("(k p) n -> p k n", p=P)
                if cols == 256:
                    piece((name, col, 0), (shaped(KC, 256), v[:, :, col:col + 256]))
                    return
                for h in range(2):
                    piece((name, col, h), (shaped(4, 512), v[:, 4 * h:4 * h + 4, col:col + 512]))

            def chunk_rows(name, w, k):
                piece((name, k), (shaped(2, D), w.rearrange("(k p) n -> p k n", p=P)[:, 2 * k:2 * k + 2, :]))

            for g in range(0, 6144, 512):
                columns("w_in", A["w_in"][0], g)
            for k in range(8):
                chunk_rows("w_out", A["w_out"][0], k)
            for g in range(0, 6144, 512):
                columns("ada", A["ada_w_2"][0], g)
            if upto >= 2:
                for g in range(0, 3072, 512):
                    columns("w_in2", A["w_in_2"][0], g)
                for k in range(4):
                    chunk_rows("w_out2", A["w_out_2"][0], k)
                for g in range(0, FF2, 512):
                    columns("ff1", A["w_ff1_2"][0], g)
                for k in range(16):
                    chunk_rows("ff2", A["w_ff2_2"][0], k)
            if upto >= 3:
                columns("mem", A["w_mem_kv_3"], 0)
                for g in (0, 256, 512):
                    columns("cv_in", A["cv_w_in_3"][0], g, 256)
                    columns("cv_in", A["cv_w_in_3"][0], CONV + g, 256)
                columns("cv_in", A["cv_w_in_3"][0], 2 * CONV, 256)
                for k in range(4):
                    chunk_rows("cv_out", A["cv_w_out_3"][0], k)
                for g in range(0, FFD, 256):
                    columns("gate", A["cv_w_gate_3"][0], g, 256)
                    columns("up", A["cv_w_up_3"][0], g, 256)
                for k in range(11):
                    chunk_rows("down", A["cv_w_down_3"][0], k)
            if upto >= 4:
                v = A["sw_w_in_3"][0].rearrange("(k p) n -> p k n", p=P)

                for g in range(2):
                    for h in range(2):
                        piece(("sw_in", g, h),
                              *((shaped(4, 512, P * x + H64 * y, P * x + H64 * (y + 1)),
                                 v[:, 4 * h:4 * h + 4, 384 * g + 192 * y + H64 * x:384 * g + 192 * y + H64 * (x + 1)])
                                for x in range(3) for y in range(2)),
                              (shaped(4, 512, 384), v[:, 4 * h:4 * h + 4, 768 + P * g:768 + P * (g + 1)]))
                columns("sw_in", A["sw_w_in_3"][0], 1024)
                for k in range(4):
                    chunk_rows("sw_out", A["sw_w_out_3"][0], k)
            if upto >= 5:
                for n in range(W.n - RING, W.n):
                    sp.wait_ge(*((c.sem(W.known.freed[n][0]), W.known.freed[n][1]) if W.known else (c.sem("piece_used"), 1)))
                base[0], slot0 = W.n, list(W.slot)
                gate, up, down = (A[f"sw_we_{x}_3"].rearrange("a e (k p) n -> (a e) p k n", p=P) for x in ("gate", "up", "down"))

                def expert(e):
                    W.n, W.slot = base[0], list(slot0)
                    for g in range(FFE // 512):
                        for name, w in (("xgate", gate), ("xup", up)):
                            for h in range(2):
                                piece((name, g, h), (shaped(4, 512), w[e, :, 4 * h:4 * h + 4, g * 512:(g + 1) * 512]))
                    for k in range(FFE // 256):
                        piece(("xdown", k), (shaped(2, D), down[e, :, 2 * k:2 * k + 2, :]))
                    assert W.n - base[0] == 6 * RING

                with sp.Fori(0, NEXP) as r:
                    c.loop = r
                    expert(r)
                    c.loop = None
                sp.wait_ge(*c.at("rounds_ready"))
                n_rounds = sp.value_load(ridi[0:1, 15:16], min_val=NEXP, max_val=NROUND)
                with sp.If(n_rounds > NEXP):
                    with sp.Fori(NEXP, n_rounds) as r:
                        e = sp.value_load(ridi[0:1, bass.ds(r, 1)], min_val=0, max_val=NEXP - 1)
                        c.loop = r
                        expert(e)
                        c.loop = None
            sp.wait_ge(*c.at("x_ready", min(upto, 5)))
            sp.dma_start(out.rearrange("a (t p) d -> p (a t) d", p=P), xres[:, :, :]).then_inc(c.sem("out_stored"), 16)
            sp.wait_ge(c.sem("out_stored"), 16)

        @block.tensor
        def _(pe):
            mm = nc.tensor.matmul

            def landed(key):
                s, v = W.known.landing[key] if W.known else (0, 16)
                pe.wait_ge(c.sem(f"landed{s}"), v if c.loop is None else c.loop * 96 + v)
                return ring[:, s, :]

            def chunks(name, col, cols=512):
                if cols == 256:
                    v = landed((name, col, 0)).rearrange("p (k n) -> p k n", k=KC)
                    return [v[:, k, :] for k in range(KC)], [(name, col, 0)]
                w = []
                for h in range(2):
                    v = landed((name, col, h)).rearrange("p (k n) -> p k n", k=4)
                    w += [v[:, k, :] for k in range(4)]
                return w, [(name, col, 0), (name, col, 1)]

            def done(last, *key):
                s = J.filled(*key)
                last.then_inc(s.sem, 1)
                return s

            def free(keys, signal):
                for k in keys:
                    W.free(k, signal)

            def turn(stage, src, n=KC):
                for q in range(n // 2):
                    b = J.fill(pe, stage, q)
                    for j in range(2):
                        for t in range(NT):
                            last = nc.tensor.transpose(ps[b][:, j * S + t * P:j * S + (t + 1) * P],
                                                       src[:, t, (2 * q + j) * P:(2 * q + j + 1) * P], ident)
                    done(last, stage, q)

            def turned(stage, n=4):
                for q in range(n):
                    pe.wait_ge(*J.emptied(stage, q))

            def proj_T(stage, w, c0, q):
                b = J.fill(pe, stage, q)
                for j in range(2):
                    for k in range(KC):
                        last = mm(ps[b][:, j * S:(j + 1) * S], w[k][:, c0 + j * P:c0 + (j + 1) * P], hT[:, k, :],
                                  start=(k == 0), stop=(k == KC - 1))
                return done(last, stage, q)

            def cols_T(stage, name, col, cols=512):
                w, keys = chunks(name, col, cols)
                for q in range(cols // 256):
                    s = proj_T(stage, w, q * 256, col // 256 + q)
                free(keys, s)

            def cols_tok(stage, name, col):
                w, keys = chunks(name, col)
                for t in range(NT):
                    b = J.fill(pe, stage, col, t)
                    for k in range(KC):
                        last = mm(ps[b][:, :], hT[:, k, t * P:(t + 1) * P], w[k], start=(k == 0), stop=(k == KC - 1))
                    s = done(last, stage, col, t)
                free(keys, s)

            def sum_rows(stage, name, n, mixT, ready=lambda k: None):
                for k in range(n):
                    w = landed((name, k)).rearrange("p (k n) -> p k n", k=2)
                    ready(k)
                    for j in range(2):
                        kk = 2 * k + j
                        for t in range(NT):
                            for h in range(2):
                                last = mm(acc[2 * t + h][:, :], mixT[:, kk, t * P:(t + 1) * P],
                                          w[:, j, h * 512:(h + 1) * 512], start=(kk == 0), stop=(kk == 2 * n - 1))
                    s = c.sig("piece_used", stage, k)
                    last.then_inc(s.sem, 1)
                    free([(name, k)], s)

            def scores(stage, i, segs, score):
                b = J.fill(pe, stage + "S", i)
                for t, col, nk in segs:
                    last = score(i, t, ps[b][:, col:col + nk * P], nk)
                done(last, stage + "S", i)

            def turn_probs(stage, h, segs, buf):
                pe.wait_ge(*c.at("probs_ready", stage, h))
                b = J.fill(pe, stage + "T", h)
                for x in range(sum(nk for _, _, nk in segs)):
                    last = nc.tensor.transpose(ps[b][:, x * P:(x + 1) * P], logit[:, buf, x * P:(x + 1) * P], ident)
                done(last, stage + "T", h)

            def out_T(stage, h, segs, v, base, width):
                pe.wait_ge(*J.emptied(stage + "T", h))
                b = J.fill(pe, stage + "O", h)
                x = 0
                for t, col, nk in segs:
                    for k in range(nk):
                        last = mm(ps[b][base:base + width, t * P:(t + 1) * P], v(k), probT[:, h % 2, x * P:(x + 1) * P],
                                  start=(k == 0), stop=(k == nk - 1))
                        x += 1
                done(last, stage + "O", h)

            def attend(stage, H, segs, score, v, place, between=lambda i: None):
                for i in range(H + 2):
                    if i < H:
                        scores(stage, i, segs, score)
                    between(i)
                    if 1 <= i <= H:
                        turn_probs(stage, i - 1, segs, (i - 1) % 4)
                    if i >= 2:
                        out_T(stage, i - 2, segs, v(i - 2), *place(i - 2))

            def head_rms(stage, n, ready=None):
                for q in range(n):
                    pe.wait_ge(*c.at("squares", stage, q))
                    b = J.fill(pe, stage, q)
                    done(mm(ps[b][:, :], C("half"), logit[:, q % 2, :], start=True, stop=True), stage, q)

            pe.wait_ge(c.sem("consts_in"), 16)
            for g, (r, loads) in enumerate(vload):
                pe.wait_ge(c.sem(f"vrows_in{g}"), 16 * len(loads))
                b = J.fill(pe, "vec", g)
                done(nc.tensor.transpose(ps[b][:, 0:r], vrows[g][0:r, :], ident[0:r, 0:r]), "vec", g)
            pe.wait_ge(*c.at("rel_wide"))
            for h in range(HEADS1):
                b = J.fill(pe, "rel", h)
                done(mm(ps[b][:, 0:511], relw[0:33, h, :], C("rel")[0:33, :], start=True, stop=True), "rel", h)

            pe.wait_ge(*c.at("normed", "pre"))
            turn("pre", nrm)
            turned("pre")
            for g in (0, 512, 1024, 1536):
                cols_T("b1p", "w_in", g)
            for g in (2048, 2560):
                cols_tok("b1v", "w_in", g)
            for q in range(8):
                pe.wait_ge(*J.emptied("b1p", q))
            for col in (2048, 2560):
                for t in range(NT):
                    pe.wait_ge(*J.emptied("b1v", col, t))

            def b1_between(i):
                if i in B1_BETWEEN:
                    cols_T("b1p", "w_in", B1_BETWEEN[i])

            attend("b1", HEADS1, T384,
                   lambda h, t, dst, nk: mm(dst, qT[:, h, t * P:(t + 1) * P], kT[:, h, 0:nk * P], start=True, stop=True),
                   lambda h: lambda k: vt[:, k, h * P:(h + 1) * P], lambda h: (0, P), b1_between)

            pe.wait_ge(*c.at("bd_ready"))
            for q in range(16, 20):
                pe.wait_ge(*J.emptied("b1p", q))
            for m, (key, src) in enumerate((("qm", xcT), ("km", xcT), ("vmT", xmT))):
                for q in range(4):
                    if m == 0:
                        pe.wait_ge(*c.at("conv_ready", 2 * q + 1))
                    b = J.fill(pe, key, q)
                    for j in range(2):
                        last = mm(ps[b][:, j * S:(j + 1) * S], bd[:, 8 * m + 2 * q + j, :], src[:, 2 * q + j, :],
                                  start=True, stop=True)
                    done(last, key, q)
            for t in range(NT):
                for q in range(2):
                    b = J.fill(pe, "vm", t, q)
                    for j in range(4):
                        last = mm(ps[b][:, j * P:(j + 1) * P], xmT[:, 4 * q + j, t * P:(t + 1) * P], bd[:, 16 + 4 * q + j, :],
                                  start=True, stop=True)
                    done(last, "vm", t, q)
            pe.wait_ge(c.sem("wif_in"), 32)
            for key in ("qm", "km", "vmT"):
                for q in range(4):
                    pe.wait_ge(*J.emptied(key, q))
            b = J.fill(pe, "gates")
            for t in range(NT):
                o = ps[b][:, t * 8:t * 8 + 8]
                for m, src in enumerate((qmT, kmT, vmT)):
                    for k in range(KC):
                        mm(o, src[:, k, t * P:(t + 1) * P], wif[:, 8 * m + k, :], start=(m + k == 0), stop=False)
                last = mm(o, ones[0:1, :], brow[0:1, 0:8], start=False, stop=True)
            done(last, "gates")
            pe.wait_ge(*c.at("loggates"))
            b = J.fill(pe, "Frow")
            for k in range(NT):
                mm(ps[b][0:MH, 0:S], gl[:, k, 4:8], C("upto", 2)[:, k, :], start=(k == 0), stop=(k == 1))
            for k in range(NT):
                last = mm(ps[b][0:MH, S + k * P:S + (k + 1) * P], gl[:, k, 0:4], ident, start=True, stop=True)
            done(last, "Frow")
            b = J.fill(pe, "Fcol")
            for t in range(NT):
                for k in range(t + 1):
                    last = mm(ps[b][:, t * 4:t * 4 + 4], C("upto", 2)[:, k, t * P:(t + 1) * P], gl[:, k, 4:8],
                              start=(k == 0), stop=(k == t))
            done(last, "Fcol")
            pe.wait_ge(*c.at("a_rows"))
            for t in range(NT):
                for q in range(2):
                    pe.wait_ge(*J.emptied("vm", t, q))
            for i in range(MH + 2):
                if i < MH:
                    b = J.fill(pe, "mA", i)
                    for t, col, nk in T384:
                        last = mm(ps[b][:, col:col + nk * P], C("hsel", MH)[0:MH, i, :], aT[0:MH, 0:nk * P], start=True, stop=True)
                    done(last, "mA", i)
                    b = J.fill(pe, "mS", i)
                    for t, col, nk in T384:
                        for k in range(2):
                            last = mm(ps[b][:, col:col + nk * P], qmT[:, 2 * i + k, t * P:(t + 1) * P], kmT[:, 2 * i + k, 0:nk * P],
                                      start=(k == 0), stop=(k == 1))
                    done(last, "mS", i)
                if 1 <= i <= MH:
                    turn_probs("m", i - 1, T384, (i - 1) % 4)
                if i >= 2:
                    h = i - 2
                    pe.wait_ge(*J.emptied("mT", h))
                    b = J.fill(pe, "mO", h)
                    for t, x, k, stop in ((0, 0, 0, True), (1, 1, 0, False), (1, 2, 1, True)):
                        last = mm(ps[b][:, t * S:(t + 1) * S], probT[:, h % 2, x * P:(x + 1) * P], vm[:, k, h * MD:(h + 1) * MD],
                                  start=(k == 0), stop=stop)
                    done(last, "mO", h)
            pe.wait_ge(*c.at("normed", "mlstm"))
            turn("mlstm", nrm)
            turned("mlstm")
            sum_rows("b1", "w_out", 8, mix1)

            pe.wait_ge(*c.at("c_ready"))
            for g in range(12):
                w, keys = chunks("ada", g * 512)
                b = J.fill(pe, "ada", g)
                if g // 2 in (2, 5):
                    for k in range(KC):
                        last = mm(ps[b][:, :], cact[:, k, :], w[k], start=(k == 0), stop=(k == KC - 1))
                else:
                    for j in range(4):
                        for k in range(KC):
                            last = mm(ps[b][:, j:j + 1], w[k][:, j * P:(j + 1) * P], cact[:, k, 0:1],
                                      start=(k == 0), stop=(k == KC - 1))
                free(keys, done(last, "ada", g))
            if upto < 2:
                return
            pe.wait_ge(*c.at("normed", "mix2"))
            turn("mix2", nrm)
            turned("mix2")
            for x, col in enumerate((0, 512)):
                cols_T("dqk", "w_in2", col)
            cols_tok("b2v", "w_in2", 1024)
            for q in range(4):
                pe.wait_ge(*J.emptied("dqk", q))
                b = J.fill(pe, "rot", q)
                done(mm(ps[b][:, :], C("rot"), qraw[:, q, :], start=True, stop=True), "rot", q)
            for col in (1536, 2048):
                cols_T("sqk", "w_in2", col)
            cols_tok("b2v", "w_in2", 2560)
            for q in range(4):
                pe.wait_ge(*c.at("roped", q))
            for t in range(NT):
                pe.wait_ge(*J.emptied("b2v", 1024, t))

            def diff_score(i, t, dst, nk):
                h, m = i // 2, 64 * (i % 2)
                return mm(dst, qdT[m:m + 64, h, t * P:(t + 1) * P], kdT[m:m + 64, h, 0:nk * P], start=True, stop=True)

            for i in range(NDIFF + 2):
                if i < NDIFF:
                    scores("d", 2 * i, T384, diff_score)
                    scores("d", 2 * i + 1, T384, diff_score)
                if 1 <= i <= NDIFF:
                    turn_probs("dd", i - 1, T384, 2 * ((i - 1) % 2))
                if i >= 2:
                    h = i - 2
                    pe.wait_ge(*J.emptied("ddT", h))
                    b = J.fill(pe, "ddO", h)
                    for t, x, k, stop in ((0, 0, 0, True), (1, 1, 0, False), (1, 2, 1, True)):
                        last = mm(ps[b][:, t * P:(t + 1) * P], probT[:, h % 2, x * P:(x + 1) * P], vd[:, k, h * P:(h + 1) * P],
                                  start=(k == 0), stop=stop)
                    done(last, "ddO", h)
            for q in range(6, 10):
                pe.wait_ge(*J.emptied("sqk", q))
            for t in range(NT):
                pe.wait_ge(*J.emptied("b2v", 2560, t))
            for i in range(NSB + 2):
                if i < NSB:
                    m, ch = 64 * (i % 2), i // 2
                    b = J.fill(pe, "sbz", i)
                    mm(ps[b][:, 0:S], skT[m:m + 64, ch, 0:P], sqT[m:m + 64, ch, :], start=True, stop=True)
                    done(mm(ps[b][:, S:S + P], skT[m:m + 64, ch, P:S], sqT[m:m + 64, ch, P:S], start=True, stop=True), "sbz", i)
                if 1 <= i <= NSB:
                    h = i - 1
                    pe.wait_ge(*c.at("log1m_ready", h))
                    l1 = sbw[:, h % 2, 768:1152]
                    b = J.fill(pe, "sbs", h)
                    mm(ps[b][:, 0:S], C("after"), l1[:, 0:S], start=True, stop=False)
                    mm(ps[b][:, P:S], ones, l1[:, S:S + P], start=False, stop=True)
                    done(mm(ps[b][:, S:S + P], C("after"), l1[:, S:S + P], start=True, stop=True), "sbs", h)
                if i >= 2:
                    h = i - 2
                    m = 64 * (h % 2)
                    pe.wait_ge(*c.at("sticks_ready", h))
                    a = sbw[:, h % 2, 1152:1536]
                    b = J.fill(pe, "sbo", h)
                    mm(ps[b][m:m + 64, 0:S], sv[:, 0, h * 64:(h + 1) * 64], a[:, 0:S], start=True, stop=False)
                    done(mm(ps[b][m:m + 64, P:S], sv[:, 1, h * 64:(h + 1) * 64], a[:, S:S + P], start=False, stop=True), "sbo", h)
            pe.wait_ge(*c.at("normed", "subln"))
            turn("subln", nrm, 4)
            turned("subln", 2)
            for h in range(NSB):
                pe.wait_ge(*J.emptied("sbo", h))
            sum_rows("b2", "w_out2", 4, mix2)
            pe.wait_ge(*c.at("normed", "ffn2"))
            turn("ffn2", nrm)
            turned("ffn2")
            for g in range(0, FF2, 512):
                cols_T("ff1", "ff1", g)

            def ff_ready(k):
                pe.wait_ge(*c.at("relu2_ready", k))
                if k == 13 and upto >= 3:
                    pe.wait_ge(*c.at("normed", "mem"))
                    turn("mem", nrm)

            sum_rows("ff", "ff2", 16, fT, ff_ready)
            if upto < 3:
                return

            turned("mem")
            w, keys = chunks("mem", 0)
            proj_T("memk", w, 0, 0)
            b = J.fill(pe, "memv")
            for t in range(NT):
                for k in range(KC):
                    last = mm(ps[b][:, t * 256:(t + 1) * 256], hT[:, k, t * P:(t + 1) * P], w[k][:, 256:512],
                              start=(k == 0), stop=(k == KC - 1))
            free(keys, done(last, "memv"))
            head_rms("memk2", 1)

            def mem_attend(stage, qsrc):
                attend(stage, MEMH, T512,
                       lambda h, t, dst, nk: mm(dst, qsrc[64 * (h % 2):64 * (h % 2) + 64, h // 2, t * P:(t + 1) * P],
                                                memkT[64 * (h % 2):64 * (h % 2) + 64, h // 2, :], start=True, stop=True),
                       lambda h: lambda k: memv[:, k, h * 64:(h + 1) * 64], lambda h: (64 * (h % 2), 64))

            pe.wait_ge(*c.at("normed", "cv"))
            turn("cv", nrm)
            turned("cv")
            for g in range(3):
                cols_T("cvp", "cv_in", CONV + 256 * g, 256)
                cols_T("cvp", "cv_in", 256 * g, 256)
            cols_T("cvp", "cv_in", 2 * CONV, 256)
            head_rms("cvq2", 1)
            pe.wait_ge(*c.at("head_normed", "memk2", 0))
            pe.wait_ge(*J.emptied("memv"))
            pe.wait_ge(*c.at("head_normed", "cvq2", 0))
            mem_attend("cm", mqT)
            for key, src in (("cmean", cT), ("cvar", sq3)):
                for k in range(CC):
                    if k == 0 or key == "cmean":
                        pe.wait_ge(*(c.at("cmean_in", k) if key == "cmean" else c.at("cvar_in")))
                    if k == 0:
                        b = J.fill(pe, key)
                    last = mm(ps[b][:, 0:S], ones, src[:, k, :], start=(k == 0), stop=(k == CC - 1))
                done(last, key)
            pe.wait_ge(*c.at("conv_act"))
            for h in range(MEMH):
                pe.wait_ge(*J.emptied("cmO", h))
            sum_rows("cv", "cv_out", 4, mix3)
            pe.wait_ge(*c.at("normed", "cvf"))
            turn("cvf", nrm)
            turned("cvf")
            for g in range(11):
                cols_T("fg", "gate", 256 * g, 256)
                cols_T("fu", "up", 256 * g, 256)
            sum_rows("dn", "down", 11, actd, lambda k: pe.wait_ge(*J.emptied("fu", k)))
            if upto < 4:
                return

            pe.wait_ge(*c.at("normed", "sw"))
            turn("sw", nrm)
            turned("sw")
            for g in range(2):
                w, keys = [], []
                for h in range(2):
                    v = landed(("sw_in", g, h)).rearrange("p (k n) -> p k n", k=4)
                    w += [v[:, k, :] for k in range(4)]
                    keys.append(("sw_in", g, h))
                for q in range(2):
                    b = J.fill(pe, "swp", 2 * g + q)
                    for j in range(2):
                        x = 2 * q + j
                        for k in range(KC):
                            last = mm(ps[b][:, j * S:(j + 1) * S], w[k][:, x * P:(x + 1) * P], hT[:, k, :],
                                      start=(k == 0), stop=(k == KC - 1))
                    s = done(last, "swp", 2 * g + q)
                free(keys, s)
            w, keys = chunks("sw_in", 1024)
            b = J.fill(pe, "swv")
            for t in range(NT):
                for k in range(KC):
                    last = mm(ps[b][:, t * 256:(t + 1) * 256], hT[:, k, t * P:(t + 1) * P], w[k][:, 0:256],
                              start=(k == 0), stop=(k == KC - 1))
            done(last, "swv")
            free(keys, proj_T("swm", w, 256, 0))
            head_rms("swn", 5)
            pe.wait_ge(*J.emptied("swv"))
            pe.wait_ge(*c.at("head_normed", "swn", 4))

            def swa_score(h, t, dst, nk):
                g, y, x = h // 6, 64 * (h % 6 // 3), h % 3
                return mm(dst, swq[y:y + 64, 3 * g + x, t * P:(t + 1) * P], swk[y:y + 64, g, 0:nk * P], start=True, stop=True)

            attend("sw", SWAH, T384, swa_score, lambda h: lambda k: swv[:, k, (h // 3) * 64:(h // 3 + 1) * 64],
                   lambda h: (64 * (h % 2), 64))
            mem_attend("sm", mqT)
            for st_, n in (("sw", SWAH), ("sm", MEMH)):
                for h in range(n):
                    pe.wait_ge(*J.emptied(st_ + "O", h))
            sum_rows("so", "sw_out", 4, mix3)
            if upto < 5:
                return

            pe.wait_ge(*c.at("normed", "moe"))
            turn("moe", nrm)
            turned("moe")
            pe.wait_ge(c.sem("rw_in"), 16)
            b = J.fill(pe, "router")
            for t in range(NT):
                for k in range(KC):
                    last = mm(ps[b][:, t * 8:t * 8 + 8], hT[:, k, t * P:(t + 1) * P], rw[:, k, :], start=(k == 0), stop=(k == KC - 1))
            done(last, "router")
            pe.wait_ge(*c.at("selected"))
            b = J.fill(pe, "slots")
            for t in range(NT):
                for k in range(t + 1):
                    mm(ps[b][:, t * 8:t * 8 + 8], C("before", 2)[:, k, t * P:(t + 1) * P], rt[:, 1, k, :], start=(k == 0), stop=(k == t))
            for k in range(NT):
                last = mm(ps[b][:, 16:24], ones, rt[:, 1, k, :], start=(k == 0), stop=(k == NT - 1))
            done(last, "slots")

            def gather(turn_):
                pe.wait_ge(*c.at("dispatch_ready", turn_))
                for q in range(2):
                    b = J.fill(pe, "hg" + turn_, q)
                    for j in range(4):
                        for t in range(NT):
                            last = mm(ps[b][:, j * P:(j + 1) * P], nrm[:, t, (4 * q + j) * P:(4 * q + j + 1) * P], Pm[:, t, :],
                                      start=(t == 0), stop=(t == NT - 1))
                    done(last, "hg" + turn_, q)

            def turn_gates(turn_):
                b = J.fill(pe, "pgT" + turn_)
                for t in range(NT):
                    last = nc.tensor.transpose(ps[b][:, t * P:(t + 1) * P], PG[:, t, :], ident)
                done(last, "pgT" + turn_)

            gather("first")
            turn_gates("first")
            pe.wait_ge(*c.at("rounds_ready"))
            n_rounds = pe.value_load(ridi[0:1, 15:16], min_val=NEXP, max_val=NROUND)
            with pe.Fori(0, n_rounds) as r:
                c.enter(r)
                pe.wait_ge(*c.before("gathered", "next", 1))

                def turn_act(g):
                    pe.wait_ge(*c.at("act_ready", g))
                    b = J.fill(pe, "xt", g)
                    for j in range(4):
                        last = nc.tensor.transpose(ps[b][:, j * P:(j + 1) * P], eact[:, g % 2, j * P:(j + 1) * P], ident)
                    done(last, "xt", g)

                for g in range(FFE // 512):
                    for name, key in (("xgate", "xg"), ("xup", "xu")):
                        w, keys = chunks(name, g)
                        b = J.fill(pe, key, g)
                        for k in range(KC):
                            last = mm(ps[b][:, :], hgT[:, k, :], w[k], start=(k == 0), stop=(k == KC - 1))
                        free(keys, done(last, key, g))
                    if g >= 1:
                        turn_act(g - 1)
                turn_act(FFE // 512 - 1)
                for k in range(FFE // 256):
                    w = landed(("xdown", k)).rearrange("p (k n) -> p k n", k=2)
                    pe.wait_ge(*J.emptied("xt", k // 2))
                    for j in range(2):
                        for h in range(2):
                            kk = 2 * k + j
                            last = mm(acc[h][:, :], actT[:, kk, :], w[:, j, h * 512:(h + 1) * 512],
                                      start=(kk == 0), stop=(kk == FFE // P - 1))
                    s = c.sig("piece_used", "xdown", k)
                    last.then_inc(s.sem, 1)
                    free([("xdown", k)], s)
                gather("next")
                pe.wait_ge(*c.before("gates_turned", "next"))
                pe.wait_ge(*c.at("expert_out", 0))
                pe.wait_ge(*c.at("expert_out1", 0))
                for t in range(NT):
                    for h in range(2):
                        b = J.fill(pe, "xs", t, h)
                        done(mm(ps[b][:, :], pgT[:, t * P:(t + 1) * P], ey[:, h * 512:(h + 1) * 512], start=True, stop=True), "xs", t, h)
                turn_gates("next")
                c.leave()

        @block.scalar
        def _(act):
            def do(ins, s=None):
                s = s or c.sig("act_step")
                ins.then_inc(s.sem, 1)
                act.wait_ge(s.sem, s.val)

            def go(ins, s):
                ins.then_inc(s.sem, 1)

            f = nc.scalar.activation

            act.dma_start(relb[0:32, :], A["rel_bias"]).then_inc(c.sem("rel_in"), 16)
            for g, (r, loads) in enumerate(vload):
                for dst, src in loads:
                    act.dma_start(dst, src).then_inc(c.sem(f"vrows_in{g}"), 16)
            act.dma_start(wif[:, :, :], A["w_if"][0].rearrange("(k p) n -> p k n", p=P)).then_inc(c.sem("wif_in"), 16)
            act.dma_start(brow[0:1, :], A["b_if"]).then_inc(c.sem("wif_in"), 16)
            for m, name in enumerate(("wq_m", "wk_m", "wv_m")):
                act.dma_start(wraw[:, 8 * m:8 * m + 8, :], A[name][0].rearrange("(k n) i o -> (n i) k o", k=8))\
                    .then_inc(c.sem("wraw_in"), 16)
            act.dma_start(wide[:, :], everywhere(A["g_post"], D)).then_inc(c.sem("wide_in"), 16)
            act.dma_start(sinkb[:, :], everywhere(A["sw_sinks_3"], SWAH)).then_inc(c.sem("small_in"), 16)
            for i, name in enumerate(("lambda_q1_2", "lambda_k1_2", "lambda_q2_2", "lambda_k2_2")):
                act.dma_start(lamv[:, i, :], everywhere(A[name], H64)).then_inc(c.sem("small_in"), 16)
            act.dma_start(rw[:, :, :], A["sw_router_3"][0].rearrange("(k p) n -> p k n", p=P)).then_inc(c.sem("rw_in"), 16)

            def copy(dst, key, cols=512, lo=0, rows=slice(0, P), func=ACT.Copy):
                act.wait_ge(*J.full(*key))
                do(f(dst, ps[J.bank(*key)][rows, lo:lo + cols], func), J.free(*key))

            def pair(buf, q):
                return buf[:, 2 * q:2 * q + 2, :].rearrange("p a b -> p (a b)")

            def exps(stage, i, segs, buf, sink=None):
                act.wait_ge(*c.at("max_ready", stage, i))
                for t, col, nk in segs:
                    x = logit[:, buf, col:col + nk * P]
                    do(f(x, x, ACT.Exp, bias=smx[:, buf, t:t + 1], accum_out=smx[:, buf, 2 + t:3 + t]),
                       c.sig("exp_done", stage, i) if t == 1 and sink is None else None)
                if sink is not None:
                    for t in range(NT):
                        do(f(smx[:, buf, 6 + t:7 + t], sink, ACT.Exp, bias=smx[:, buf, t:t + 1]),
                           c.sig("exp_done", stage, i) if t == 1 else None)

            def probs_T(stage, h, segs, prev):
                if h >= 2:
                    act.wait_ge(*J.full(prev, h - 2))
                copy(probT[:, h % 2, 0:P * sum(nk for _, _, nk in segs)], (stage + "T", h), P * sum(nk for _, _, nk in segs))

            def head_rms(stage, raws):
                for q, raw in enumerate(raws):
                    if q >= 2:
                        act.wait_ge(*J.full(stage, q - 2))
                    do(f(logit[:, q % 2, :], raw, ACT.Square), c.sig("squares", stage, q))
                    act.wait_ge(*J.full(stage, q))
                    if q >= 2:
                        act.wait_ge(*c.at("head_normed", stage, q - 2))
                    do(f(rsw[:, q % 2, :], ps[J.bank(stage, q)][:, :], ACT.Sqrt, scale=1.0 / H64, bias=C("eps")[:, 0:1]),
                       J.free(stage, q))

            for g, (r, _) in enumerate(vload):
                copy(vcol[:, g, 0:r], ("vec", g), r)
            for h in range(HEADS1):
                copy(relrep[:, h, 0:511], ("rel", h), 511)
            act.dma_start(relrow, relrep[:, :, 0:511]).then_inc(c.sem("relrow_out"), 16)
            act.wait_ge(c.sem("relrow_out"), 16)
            for first, lo, n in ((255, 0, P), (127, P, S)):
                act.dma_start(relbias[:, :, lo:lo + n],
                              bass.AP(tensor=relrow.tensor, offset=first, ap=[[HEADS1 * 511 - 1, P], [511, HEADS1], [1, n]]))\
                    .then_inc(c.sem("relbias_in"), 16)
            for q in range(8):
                copy(pair(qT if q < 4 else kT, q % 4), ("b1p", q))
            for i in range(HEADS1 + 2):
                if i < HEADS1:
                    exps("b1", i, T384, i % 4)
                if i in B1_BETWEEN:
                    for q in (B1_BETWEEN[i] // 256, B1_BETWEEN[i] // 256 + 1):
                        if q < 16:
                            copy(pair(mix1, q - 12), ("b1p", q), func=ACT.Silu)
                        elif q < 20:
                            copy(pair(xmT, q - 16), ("b1p", q))
                        else:
                            copy(pair(mix1, q - 20 + 4), ("b1p", q), func=ACT.Silu)
                if 1 <= i <= HEADS1:
                    probs_T("b1", i - 1, T384, "b1O")
            for k in range(KC):
                act.wait_ge(*c.at("conv", k))
                do(f(xcT[:, k, :], xcT[:, k, :], ACT.Silu), c.sig("conv_ready", k))
            for key, dst in (("qm", qmT), ("km", kmT)):
                for q in range(4):
                    copy(pair(dst, q), (key, q))
            act.wait_ge(*c.at("gates_in"))
            do(f(lg[:, :, 0:4], gl[:, :, 4:8], ACT.Abs))
            do(f(lg[:, :, 4:8], lg[:, :, 0:4], ACT.Exp, scale=-1.0))
            do(f(lg[:, :, 8:12], lg[:, :, 4:8], ACT.Ln, bias=ones[:, 0:1]), c.sig("softplus", "gates"))
            for i in range(MH + 2):
                if i < MH:
                    act.wait_ge(*c.at("max_ready", "m", i))
                    for t, col, nk in T384:
                        x = logit[:, i % 4, col:col + nk * P]
                        do(f(x, x, ACT.Exp, bias=mcol[:, i, 2 + t:3 + t]))
                    do(f(mcol[:, i, 6:8], mcol[:, i, 4:6], ACT.Exp, scale=-1.0), c.sig("exp_done", "m", i))
                if 1 <= i <= MH:
                    probs_T("m", i - 1, T384, "mO")
            do(f(lg[:, 0, 0:8], vcol[:, vat["c_2"][0], vat["c_2"][1]:vat["c_2"][1] + 8], ACT.Silu), c.sig("c_act"))
            act.wait_ge(*c.at("piece_used", "b1", 7))
            for t in range(NT):
                for h in range(2):
                    do(f(junk[:, 0:512], acc[2 * t + h][:, :], ACT.Square, accum_out=st[:, 4 + 2 * t + h:5 + 2 * t + h]),
                       c.sig("squares", "post1") if t + h == 2 else None)
            if upto < 2:
                return
            for q in range(4):
                copy(qraw[:, q, :], ("dqk", q))
                if q == 3:
                    for t in range(NT):
                        copy(vd[:, t, :], ("b2v", 1024, t))
            for q in range(6, 10):
                copy(pair(sqT if q < 8 else skT, q % 2), ("sqk", q))
            for t in range(NT):
                copy(sv[:, t, :], ("b2v", 2560, t))
            for i in range(2):
                act.wait_ge(*c.at("lambda_dots"))
                do(f(lam[:, i:i + 1], lam[:, i:i + 1], ACT.Exp), c.sig("lambda_exp") if i else None)
            for i in range(NDIFF + 1):
                if i < NDIFF:
                    exps("d", 2 * i, T384, 2 * i % 4)
                    exps("d", 2 * i + 1, T384, (2 * i + 1) % 4)
                if i >= 1:
                    probs_T("dd", i - 1, T384, "ddO")
            for i in range(NSB + 2):
                if i < NSB:
                    act.wait_ge(*c.at("z_ready", i))
                    z, x = sbw[:, i % 2, 0:384], sbw[:, i % 2, 384:768]
                    do(f(x, z, ACT.Abs))
                    do(f(x, x, ACT.Exp, scale=-1.0))
                    do(f(x, x, ACT.Ln, bias=ones[:, 0:1]), c.sig("softplus", i))
                if i >= 2:
                    h = i - 2
                    act.wait_ge(*c.at("stick_log", h))
                    x = sbw[:, h % 2, 1152:1536]
                    do(f(x, x, ACT.Exp), c.sig("exp_done", "sb", h))
                    m = 64 * (h % 2)
                    copy(mix2[m:m + 64, 4 + h // 2, :], ("sbo", h), S, rows=slice(m, m + 64))
            for k in range(16):
                act.wait_ge(*J.full("ff1", k))
                do(f(pair(fT, k), ps[J.bank("ff1", k)][:, :], ACT.Relu), J.free("ff1", k))
            if upto < 3:
                return

            copy(pair(memkT, 0), ("memk", 0))
            copy(memv[:, :, :].rearrange("p a b -> p (a b)"), ("memv",))
            head_rms("memk2", [pair(memkT, 0)])

            def memory(stage, between=lambda i: None):
                for i in range(MEMH + 2):
                    if i < MEMH:
                        exps(stage, i, T512, i % 4)
                    if 1 <= i <= MEMH:
                        probs_T(stage, i - 1, T512, stage + "O")
                    if i >= 2:
                        m, h = 64 * (i % 2), i - 2
                        copy(mix3[m:m + 64, 6 + h // 2, :], (stage + "O", h), S, rows=slice(m, m + 64))

            for g in range(3):
                key = ("cvp", 3 + g)
                act.wait_ge(*J.full(*key))
                for j in range(2):
                    do(f(sg3[:, g, j * S:(j + 1) * S], ps[J.bank(*key)][:, j * S:(j + 1) * S], ACT.Sigmoid,
                         bias=vec("cv_b_glu_3", CC + 2 * g + j)), J.free(*key) if j else None)
            copy(pair(mqT, 0), ("cvp", 6))
            head_rms("cvq2", [pair(mqT, 0)])
            memory("cm")
            act.wait_ge(*c.at("centred"))
            flat = lambda v: v.rearrange("p a b -> p (a b)")
            do(f(flat(sq3), flat(cT), ACT.Square), c.sig("cvar_in"))
            act.wait_ge(*J.full("cvar"))
            do(f(lnw[:, 1, :], ps[J.bank("cvar")][:, 0:S], ACT.Sqrt, scale=1.0 / CONV, bias=C("eps")[:, 1:2]), J.free("cvar"))
            act.wait_ge(*c.at("conv_normed"))
            for k in range(CC):
                do(f(mix3[:, k, :], cT[:, k, :], ACT.Silu, scale=vec("cv_ln_g_3", k), bias=vec("cv_ln_b_3", k)),
                   c.sig("conv_act") if k == CC - 1 else None)
            for g in range(11):
                if g >= 4:
                    act.wait_ge(*J.emptied("fu", g - 4))
                copy(sg3[:, g % 4, :], ("fg", g), func=ACT.Silu)
            if upto < 4:
                return
            for g in range(2):
                copy(flat(swq[:, 3 * g:3 * g + 2, :]), ("swp", 2 * g))
                key = ("swp", 2 * g + 1)
                act.wait_ge(*J.full(*key))
                do(f(swq[:, 3 * g + 2, :], ps[J.bank(*key)][:, 0:S], ACT.Copy))
                do(f(swk[:, g, :], ps[J.bank(*key)][:, S:2 * S], ACT.Copy), J.free(*key))
            copy(flat(swv), ("swv",))
            copy(pair(mqT, 0), ("swm", 0))
            head_rms("swn", [pair(swq, 0), pair(swq, 1), pair(swq, 2), pair(swk, 0), pair(mqT, 0)])
            for i in range(SWAH + 2):
                if i < SWAH:
                    exps("sw", i, T384, i % 4, sinkb[:, i:i + 1])
                if 1 <= i <= SWAH:
                    probs_T("sw", i - 1, T384, "swO")
                if i >= 2:
                    m, h = 64 * (i % 2), i - 2
                    copy(mix3[m:m + 64, h // 2, :], ("swO", h), S, rows=slice(m, m + 64))
            memory("sm")
            if upto < 5:
                return

            act.wait_ge(*c.at("router_max"))
            for t in range(NT):
                do(f(rt[:, 2, t, :], rt[:, 0, t, :], ACT.Exp, bias=xtr[:, t, 0:1]), c.sig("exp_done", "router") if t else None)

            def gates_T(turn_):
                copy(pgT[:, :], ("pgT" + turn_,), S)
                go_last = c.sig("gates_turned", turn_)
                do(f(xtr[:, 7, 0:1], ones[:, 0:1], ACT.Copy), go_last)

            gates_T("first")
            act.wait_ge(*c.at("rounds_ready"))
            n_rounds = act.value_load(ridi[0:1, 15:16], min_val=NEXP, max_val=NROUND)
            with act.Fori(0, n_rounds) as r:
                c.enter(r)
                n = FFE // 512
                for g in range(n + 1):
                    if g < n:
                        if g >= 2:
                            act.wait_ge(*c.at("act_ready", g - 2))
                        copy(esg[:, g % 2, :], ("xg", g), func=ACT.Silu)
                    if g >= 1:
                        copy(flat(actT[:, 4 * (g - 1):4 * g, :]), ("xt", g - 1))
                act.wait_ge(*c.at("piece_used", "xdown", FFE // 256 - 1))
                do(f(ey[:, 0:512], acc[0][:, :], ACT.Copy), c.sig("expert_out", 0))
                gates_T("next")
                c.leave()

        @block.vector
        def _(dve):
            v = nc.vector

            def do(ins, s=None):
                s = s or c.sig("vec_step")
                ins.then_inc(s.sem, 1)
                dve.wait_ge(s.sem, s.val)

            def rep(ap, n):
                return bass.AP(tensor=ap.tensor, offset=ap.offset, ap=[ap.ap[0], [0, n], ap.ap[1]])

            def spread(ap, n):
                return bass.AP(tensor=ap.tensor, offset=ap.offset, ap=[ap.ap[0], ap.ap[1], [0, n]])

            def bank(*key):
                dve.wait_ge(*J.full(*key))
                return ps[J.bank(*key)]

            def pair(buf, q):
                return buf[:, 2 * q:2 * q + 2, :].rearrange("p a b -> p (a b)")

            def flat(x):
                return x.rearrange("p a b -> p (a b)")

            def norm(stage, src, dst=nrm):
                s0 = 4 * NORMS.index(stage)
                for t in range(NT):
                    do(v.tensor_tensor_reduce(junk[:, :], src[:, t, :], src[:, t, :], 1.0, 0.0, ALU.mult, ALU.add,
                                              st[:, s0 + t:s0 + t + 1]), c.sig("squares_v", stage) if t else None)
                dve.wait_ge(*c.at("rstd", stage))
                for t in range(NT):
                    do(v.tensor_scalar(dst[:, t, :], src[:, t, :], st[:, s0 + 2 + t:s0 + 3 + t], None, ALU.mult),
                       c.sig("normed", stage) if t else None)

            def gains(stage, gain, shift=None, n=KC, dst=hT, k0=0):
                for q in range(n // 2):
                    b = bank(stage, q)
                    for j in range(2):
                        k = 2 * q + j
                        do(v.tensor_scalar(dst[:, k0 + k, :], b[:, j * S:(j + 1) * S], gain(k), shift(k) if shift else None,
                                           ALU.mult, ALU.add if shift else ALU.bypass), J.free(stage, q) if j else None)

            def logits(stage, i, segs, buf, scale, bias, slope=None, sink=None):
                b = bank(stage + "S", i)
                n = P * sum(nk for _, _, nk in segs)
                x = logit[:, buf, 0:n]
                if bias is None:
                    do(v.tensor_scalar(x, b[:, 0:n], scale, None, ALU.mult), J.free(stage + "S", i))
                else:
                    do(v.scalar_tensor_tensor(x, b[:, 0:n], scale, bias, ALU.mult, ALU.add), J.free(stage + "S", i))
                if slope is not None:
                    do(v.scalar_tensor_tensor(x, C("dist"), slope, x, ALU.mult, ALU.add))
                for t, col, nk in segs:
                    do(v.tensor_reduce(smx[:, buf, t:t + 1], logit[:, buf, col:col + nk * P], AX, ALU.max, negate=True),
                       c.sig("max_ready", stage, i) if t and sink is None else None)
                if sink is not None:
                    do(v.tensor_scalar(smx[:, buf, 0:2], smx[:, buf, 0:2], sink, None, ALU.min), c.sig("max_ready", stage, i))

            def probs(stage, i, segs, buf, sink=False):
                dve.wait_ge(*c.at("exp_done", stage, i))
                if sink:
                    do(v.tensor_tensor(smx[:, buf, 2:4], smx[:, buf, 2:4], smx[:, buf, 6:8], ALU.add))
                do(v.reciprocal(smx[:, buf, 4:6], smx[:, buf, 2:4]))
                for t, col, nk in segs:
                    x = logit[:, buf, col:col + nk * P]
                    do(v.tensor_scalar(x, x, smx[:, buf, 4 + t:5 + t], None, ALU.mult), c.sig("probs_ready", stage, i) if t else None)

            def head_normed(stage, raws, gain):
                for q, raw in enumerate(raws):
                    dve.wait_ge(*J.emptied(stage, q))
                    do(v.reciprocal(rsw[:, q % 2, :], rsw[:, q % 2, :]))
                    do(v.scalar_tensor_tensor(raw, raw, gain[q], rsw[:, q % 2, :], ALU.mult, ALU.mult),
                       c.sig("head_normed", stage, q))

            def add_sums(stage, last, gate=None):
                dve.wait_ge(*c.at("piece_used", *last))
                for t in range(NT):
                    for h in range(2):
                        x, a = xres[:, t, h * 512:(h + 1) * 512], acc[2 * t + h][:, :]
                        if gate is not None:
                            do(v.tensor_tensor(junk[:, 0:512], a, gate[:, h * 512:(h + 1) * 512], ALU.mult))
                            a = junk[:, 0:512]
                        do(v.tensor_tensor(x, x, a, ALU.add))

            do(v.memset(relb[32:33, :], 1.0))
            dve.wait_ge(c.sem("rel_in"), 16)
            do(v.tensor_copy(relw[0:33, :, :], spread(relb[0:33, :], P)), c.sig("rel_wide"))
            do(v.memset(half_c[:, :], -0.5), c.sig("exponent"))
            dve.wait_ge(c.sem("x_in"), 16)
            norm("pre", xres)
            dve.wait_ge(c.sem("wraw_in"), 48)
            dve.wait_ge(c.sem("consts_in"), 16)
            for m in range(24):
                w = wraw[:, m, :]
                do(v.tensor_tensor(bd[:, m, :].rearrange("p (n o) -> p n o", o=4), rep(w, 32),
                                   C("block4").rearrange("p (n o) -> p n o", o=4), ALU.mult), c.sig("bd_ready") if m == 23 else None)
            for g in range(4):
                dve.wait_ge(*J.emptied("vec", g))
            gains("pre", lambda k: vec("g_pre", k))
            for col in (2048, 2560):
                for t in range(NT):
                    do(v.tensor_copy(vt[:, t, col - 2048:col - 2048 + 512], bank("b1v", col, t)[:, :]), J.free("b1v", col, t))
            dve.wait_ge(c.sem("relbias_in"), 32)
            for i in range(HEADS1 + 2):
                if i < HEADS1:
                    logits("b1", i, T384, i % 4, DH1 ** -0.5, relbias[:, i, :])
                if 1 <= i <= HEADS1:
                    probs("b1", i - 1, T384, (i - 1) % 4)
                if i >= 2:
                    h = i - 2
                    dve.wait_ge(*J.emptied("b1p", 12 + h // 2))
                    do(v.tensor_tensor(mix1[:, h, :], mix1[:, h, :], bank("b1O", h)[:, 0:S], ALU.mult), J.free("b1O", h))
            for k in range(KC):
                dve.wait_ge(*J.emptied("b1p", 16 + k // 2))
                y, x = xcT[:, k, :], xmT[:, k, :]
                do(v.tensor_scalar(y, x, vec("conv_w", 24 + k), vec("conv_b", k), ALU.mult, ALU.add))
                for d in (1, 2, 3):
                    do(v.scalar_tensor_tensor(y[:, d:S], x[:, 0:S - d], vec("conv_w", 8 * (3 - d) + k), y[:, d:S], ALU.mult, ALU.add),
                       c.sig("conv", k) if d == 3 else None)
            for q in range(4):
                do(v.tensor_copy(pair(vmT, q), bank("vmT", q)[:, :]), J.free("vmT", q))
            for t in range(NT):
                for q in range(2):
                    do(v.tensor_copy(vm[:, t, q * 512:(q + 1) * 512], bank("vm", t, q)[:, :]), J.free("vm", t, q))
            do(v.tensor_copy(flat(gl[:, :, :]), bank("gates")[:, 0:16]), J.free("gates"))
            go = c.sig("gates_in")
            do(v.tensor_scalar(lg[:, :, 12:16], gl[:, :, 4:8], 0.0, None, ALU.min), go)
            dve.wait_ge(*c.at("softplus", "gates"))
            do(v.tensor_tensor(gl[:, :, 4:8], lg[:, :, 12:16], lg[:, :, 8:12], ALU.subtract), c.sig("loggates"))
            b = bank("Frow")
            do(v.tensor_copy(aT[0:MH, S:2 * S], b[0:MH, 0:S]))
            do(v.tensor_tensor(aT[0:MH, 0:S], b[0:MH, S:2 * S], aT[0:MH, S:2 * S], ALU.subtract), J.free("Frow"))
            do(v.tensor_copy(flat(fcol[:, :, :]), bank("Fcol")[:, 0:8]), J.free("Fcol"))
            do(v.tensor_copy(mcol[:, 0, 0:1], ones[:, 0:1]), c.sig("a_rows"))
            stats = cmp[:, 0, :]
            moments = cmp[:, 1, :]
            for i in range(MH + 2):
                if i < MH:
                    x = logit[:, i % 4, 0:384]
                    do(v.tensor_tensor(x, bank("mA", i)[:, 0:384], C("causal"), ALU.add), J.free("mA", i))
                    for t, col, nk in T384:
                        do(v.tensor_reduce(mcol[:, i, t:t + 1], logit[:, i % 4, col:col + nk * P], AX, ALU.max))
                    do(v.tensor_scalar(mcol[:, i, 2:4], mcol[:, i, 0:2], 0.0, -1.0, ALU.max, ALU.mult))
                    do(v.tensor_tensor(mcol[:, i, 4:6], fcol[:, :, i], mcol[:, i, 2:4], ALU.subtract), c.sig("max_ready", "m", i))
                if 1 <= i <= MH:
                    h = i - 1
                    dve.wait_ge(*c.at("exp_done", "m", h))
                    b = bank("mS", h)
                    for t, col, nk in T384:
                        x = logit[:, h % 4, col:col + nk * P]
                        do(v.scalar_tensor_tensor(x, b[:, col:col + nk * P], MD ** -0.5, x, ALU.mult, ALU.mult,
                                                  accum_out=mcol[:, h, 8 + t:9 + t]), J.free("mS", h) if t else None)
                    m = mcol[:, h, :]
                    do(v.tensor_scalar(m[:, 10:12], m[:, 8:10], -1.0, None, ALU.mult), c.sig("probs_ready", "m", h))
                    do(v.tensor_tensor(m[:, 10:12], m[:, 8:10], m[:, 10:12], ALU.max))
                    do(v.tensor_tensor(m[:, 10:12], m[:, 10:12], m[:, 6:8], ALU.max))
                    do(v.reciprocal(m[:, 12:14], m[:, 10:12]))
                if i >= 2:
                    h = i - 2
                    b = bank("mO", h)
                    for t in range(NT):
                        x = nrm[:, t, h * MD:(h + 1) * MD]
                        do(v.tensor_scalar(x, b[:, t * S:(t + 1) * S], mcol[:, h, 12 + t:13 + t], None, ALU.mult),
                           J.free("mO", h) if t else None)
                        do(v.bn_stats(stats[:, 0:6], x))
                        do(v.bn_aggr(moments[:, 2 * (NT * h + t):2 * (NT * h + t) + 2], stats[:, 0:6]),
                           c.sig("moments") if h == MH - 1 and t else None)
            dve.wait_ge(*c.at("rstd", "mlstm"))
            for h in range(MH):
                for t in range(NT):
                    x, j = nrm[:, t, h * MD:(h + 1) * MD], 2 * (NT * h + t)
                    do(v.tensor_scalar(x, x, moments[:, j:j + 1], moments[:, j + 1:j + 2], ALU.subtract, ALU.mult),
                       c.sig("normed", "mlstm") if h == MH - 1 and t else None)
            for q in range(4):
                b = bank("mlstm", q)
                for j in range(2):
                    k = 2 * q + j
                    x = junk[:, j * S:(j + 1) * S]
                    do(v.tensor_scalar(x, xcT[:, k, :], vec("skip", k), None, ALU.mult))
                    do(v.scalar_tensor_tensor(x, b[:, j * S:(j + 1) * S], vec("mh_norm", k), x, ALU.mult, ALU.add))
                    do(v.tensor_tensor(mix1[:, 8 + k, :], mix1[:, 8 + k, :], x, ALU.mult), J.free("mlstm", q) if j else None)
            dve.wait_ge(*c.at("c_act"))
            for k in range(KC):
                do(v.tensor_scalar(cact[:, k, :], ones, lg[:, 0, k:k + 1], None, ALU.mult), c.sig("c_ready") if k == KC - 1 else None)
            dve.wait_ge(c.sem("wide_in"), 16)
            dve.wait_ge(*c.at("rstd", "post1"))
            for t in range(NT):
                for h in range(2):
                    cs = slice(h * 512, (h + 1) * 512)
                    do(v.scalar_tensor_tensor(nrm[:, t, cs], acc[2 * t + h][:, :], st[:, 40 + t:41 + t], wide[:, cs], ALU.mult, ALU.mult))
                    do(v.tensor_tensor(xres[:, t, cs], xres[:, t, cs], nrm[:, t, cs], ALU.add), c.sig("x_ready", 1) if t + h == 2 else None)

            if upto >= 2:
                norm("mix2", xres)
            ga, ra = vat["ada_b_2"]
            for g in range(12):
                b, part, half = bank("ada", g), g // 2, g % 2
                if part in (2, 5):
                    if half == 0:
                        dve.wait_ge(c.sem("gates_bias_in"), 32)
                    x = (gm if part == 2 else gf)[:, half * 512:(half + 1) * 512]
                    do(v.tensor_tensor(x, x, b[:, :], ALU.add), J.free("ada", g))
                else:
                    o = 8 * {0: 0, 1: 1, 3: 2, 4: 3}[part] + 4 * half
                    do(v.tensor_tensor(modc[:, o:o + 4], b[:, 0:4], vcol[:, ga, ra + 4 * g:ra + 4 * g + 4], ALU.add), J.free("ada", g))
            for o, name in ((8, "mix_norm_g_2"), (24, "ffn_norm_g_2")):
                gg, rr = vat[name]
                do(v.scalar_tensor_tensor(modc[:, o:o + 8], modc[:, o:o + 8], 1.0, vcol[:, gg, rr:rr + 8], ALU.add, ALU.mult))
            if upto < 2:
                return
            dve.wait_ge(c.sem("small_in"), 80)
            for i in range(2):
                do(v.tensor_tensor_reduce(junk[:, 0:H64], lamv[:, 2 * i, :], lamv[:, 2 * i + 1, :], 1.0, 0.0, ALU.mult, ALU.add,
                                          lam[:, i:i + 1]), c.sig("lambda_dots") if i else None)
            gains("mix2", lambda k: modc[:, 8 + k:9 + k], lambda k: modc[:, k:k + 1])
            for q in range(4):
                dve.wait_ge(*J.emptied("dqk", q))
                x = qraw[:, q, :].rearrange("p (a b) -> p a b", a=2)
                a, d = (junk[:, o:o + 512].rearrange("p (a b) -> p a b", a=2) for o in (0, 512))
                do(v.tensor_tensor(a, x, rep(C("cos"), 2), ALU.mult))
                do(v.tensor_tensor(d, bank("rot", q)[:, :].rearrange("p (a b) -> p a b", a=2), rep(C("sin"), 2), ALU.mult), J.free("rot", q))
                do(v.tensor_tensor(pair(qdT if q < 2 else kdT, q % 2), junk[:, 0:512], junk[:, 512:1024], ALU.add), c.sig("roped", q))
            dve.wait_ge(*c.at("lambda_exp"))
            do(v.tensor_scalar(lam[:, 2:3], lam[:, 0:1], lam[:, 1:2], LAMBDA_INIT, ALU.subtract, ALU.add))
            do(v.tensor_scalar(lam[:, 2:3], lam[:, 2:3], -1.0, None, ALU.mult))
            for i in range(NDIFF + 2):
                if i < NDIFF:
                    for j in (2 * i, 2 * i + 1):
                        logits("d", j, T384, j % 4, H64 ** -0.5, C("chunk"))
                if 1 <= i <= NDIFF:
                    h = i - 1
                    p0, p1 = 2 * h % 4, (2 * h + 1) % 4
                    dve.wait_ge(*c.at("exp_done", "d", 2 * h + 1))
                    for p in (p0, p1):
                        do(v.reciprocal(smx[:, p, 4:6], smx[:, p, 2:4]))
                    do(v.tensor_scalar(smx[:, p1, 4:6], smx[:, p1, 4:6], lam[:, 2:3], None, ALU.mult))
                    for t, col, nk in T384:
                        x, y = logit[:, p0, col:col + nk * P], logit[:, p1, col:col + nk * P]
                        do(v.tensor_scalar(x, x, smx[:, p0, 4 + t:5 + t], None, ALU.mult))
                        do(v.scalar_tensor_tensor(x, y, smx[:, p1, 4 + t:5 + t], x, ALU.mult, ALU.add),
                           c.sig("probs_ready", "dd", h) if t else None)
                if i >= 2:
                    h = i - 2
                    do(v.tensor_copy(nrm[:, :, h * P:(h + 1) * P], bank("ddO", h)[:, 0:S].rearrange("p (t d) -> p t d", t=NT)),
                       J.free("ddO", h))
            for t in range(NT):
                do(v.tensor_tensor(junk[:, t * 512:(t + 1) * 512], nrm[:, t, 0:512], nrm[:, t, 0:512], ALU.mult))
            do(v.tensor_reduce(st[:, 44:52], junk[:, :].rearrange("p (a b) -> p a b", b=P), AX, ALU.add), c.sig("squares_v", "subln"))
            dve.wait_ge(*c.at("rstd", "subln"))
            for t in range(NT):
                x = nrm[:, t, 0:512].rearrange("p (a b) -> p a b", b=P)
                do(v.tensor_tensor(x, x, spread(st[:, 52 + 4 * t:56 + 4 * t], P), ALU.mult), c.sig("normed", "subln") if t else None)
            for i in range(NSB + 2):
                if i < NSB:
                    do(v.tensor_scalar(sbw[:, i % 2, 0:384], bank("sbz", i)[:, 0:384], H64 ** -0.5, None, ALU.mult), J.free("sbz", i))
                    do(v.tensor_copy(smx[:, 0, 0:1], ones[:, 0:1]), c.sig("z_ready", i))
                if 1 <= i <= NSB:
                    h = i - 1
                    w = sbw[:, h % 2, :]
                    z, sp_, l1, lb = w[:, 0:384], w[:, 384:768], w[:, 768:1152], w[:, 1536:1920]
                    dve.wait_ge(*c.at("softplus", h))
                    do(v.scalar_tensor_tensor(lb, z, 0.0, sp_, ALU.min, ALU.subtract))
                    do(v.tensor_tensor(l1, lb, z, ALU.subtract))
                    do(v.tensor_tensor(l1, l1, C("earlier"), ALU.mult), c.sig("log1m_ready", h))
                    a = w[:, 1152:1536]
                    do(v.tensor_tensor(a, bank("sbs", h)[:, 0:384], lb, ALU.add), J.free("sbs", h))
                    do(v.tensor_copy(smx[:, 0, 0:1], ones[:, 0:1]), c.sig("stick_log", h))
                if i >= 2:
                    h = i - 2
                    a = sbw[:, h % 2, 1152:1536]
                    dve.wait_ge(*c.at("exp_done", "sb", h))
                    do(v.tensor_tensor(a, a, C("earlier"), ALU.mult), c.sig("sticks_ready", h))
            for q in range(2):
                b = bank("subln", q)
                for j in range(2):
                    do(v.tensor_scalar(mix2[:, 2 * q + j, :], b[:, j * S:(j + 1) * S], vec("diff_subln_g_2"), 1.0 - LAMBDA_INIT,
                                       ALU.mult, ALU.mult), J.free("subln", q) if j else None)
            add_sums("b2", ("b2", 3), gm)
            norm("ffn2", xres)
            gains("ffn2", lambda k: modc[:, 24 + k:25 + k], lambda k: modc[:, 16 + k:17 + k])
            for k in range(16):
                dve.wait_ge(*J.emptied("ff1", k))
                do(v.tensor_tensor(pair(fT, k), pair(fT, k), pair(fT, k), ALU.mult), c.sig("relu2_ready", k))
            if upto >= 3:
                dve.wait_ge(c.sem("mem_in"), 16)
                norm("mem", memx)
                gains("mem", lambda k: vec("mem_norm_g_3", k))
            add_sums("ff", ("ff", 15), gf)
            norm("final2", xres)
            dve.wait_ge(c.sem("final_gain_in"), 16)
            for t in range(NT):
                do(v.tensor_tensor(xres[:, t, :], nrm[:, t, :], wide[:, :], ALU.mult), c.sig("x_ready", 2) if t else None)
            if upto < 3:
                return

            head_normed("memk2", [pair(memkT, 0)], [vec("mem_k_norm_g_3")])
            norm("cv", xres)
            gains("cv", lambda k: vec("cv_attn_norm_g_3", k))
            for g in range(3):
                b = bank("cvp", g)
                dve.wait_ge(*J.emptied("cvp", 3 + g))
                for j in range(2):
                    do(v.scalar_tensor_tensor(uT[:, 2 * g + j, :], b[:, j * S:(j + 1) * S], vec("cv_b_glu_3", 2 * g + j),
                                              sg3[:, g, j * S:(j + 1) * S], ALU.add, ALU.mult), J.free("cvp", g) if j else None)
            head_normed("cvq2", [pair(mqT, 0)], [vec("cv_memq_norm_g_3")])

            def conv(k):
                y, x = cT[:, k, :], uT[:, k, :]
                do(v.tensor_scalar(y, x, vec("cv_dw_w_3", CC * (CONVW - 1) + k), vec("cv_dw_b_3", k), ALU.mult, ALU.add))
                for d in range(1, CONVW):
                    do(v.scalar_tensor_tensor(y[:, d:S], x[:, 0:S - d], vec("cv_dw_w_3", CC * (CONVW - 1 - d) + k), y[:, d:S],
                                              ALU.mult, ALU.add), c.sig("cmean_in", k) if d == CONVW - 1 else None)

            def memory(stage, between=lambda i: None):
                for i in range(MEMH + 1):
                    if i < MEMH:
                        logits(stage, i, T512, i % 4, H64 ** -0.5, None)
                    between(i)
                    if i >= 1:
                        probs(stage, i - 1, T512, (i - 1) % 4)

            memory("cm", conv)
            conv(5)
            do(v.tensor_scalar(lnw[:, 0, :], bank("cmean")[:, 0:S], 1.0 / CONV, None, ALU.mult), J.free("cmean"))
            do(v.tensor_tensor(cT[:, :, :], cT[:, :, :], rep(lnw[:, 0, :], CC), ALU.subtract), c.sig("centred"))
            dve.wait_ge(*J.emptied("cvar"))
            do(v.reciprocal(lnw[:, 1, :], lnw[:, 1, :]))
            do(v.tensor_tensor(cT[:, :, :], cT[:, :, :], rep(lnw[:, 1, :], CC), ALU.mult), c.sig("conv_normed"))
            add_sums("cv", ("cv", 3))
            norm("cvf", xres)
            gains("cvf", lambda k: vec("cv_ffn_norm_g_3", k))
            for g in range(11):
                b = bank("fu", g)
                dve.wait_ge(*J.emptied("fg", g))
                do(v.tensor_tensor(pair(actd, g), sg3[:, g % 4, :], b[:, :], ALU.mult), J.free("fu", g))
            add_sums("dn", ("dn", 10))
            do(v.tensor_copy(mcol[:, 0, 0:1], ones[:, 0:1]), c.sig("x_ready", 3))
            if upto < 4:
                return
            norm("sw", xres)
            gains("sw", lambda k: vec("sw_attn_norm_g_3", k))
            head_normed("swn", [pair(swq, 0), pair(swq, 1), pair(swq, 2), pair(swk, 0), pair(mqT, 0)],
                        [vec("sw_q_norm_g_3")] * 3 + [vec("sw_k_norm_g_3"), vec("sw_memq_norm_g_3")])
            do(v.tensor_scalar(fsink[:, :], sinkb[:, :], -1.0, None, ALU.mult))
            for i in range(SWAH + 1):
                if i < SWAH:
                    logits("sw", i, T384, i % 4, H64 ** -0.5, C("window"), -(2.0 ** (-8.0 * (i + 1) / SWAH)), fsink[:, i:i + 1])
                if i >= 1:
                    probs("sw", i - 1, T384, (i - 1) % 4, sink=True)
            memory("sm")
            add_sums("so", ("so", 3))
            do(v.tensor_copy(mcol[:, 0, 0:1], ones[:, 0:1]), c.sig("x_ready", 4))
            if upto < 5:
                return

            norm("moe", xres)
            gains("moe", lambda k: vec("sw_ffn_norm_g_3", k))
            do(v.tensor_copy(flat(rt[:, 0, :, :]), bank("router")[:, 0:16]), J.free("router"))
            for t in range(NT):
                l = rt[:, 0, t, :]
                above, below = (cmp[:, x, 0:64].rearrange("p (e j) -> p e j", e=8) for x in range(2))
                lower = C("lower").rearrange("p (e j) -> p e j", e=8)
                do(v.tensor_tensor(above, rep(l, 8), spread(l, 8), ALU.is_gt))
                do(v.tensor_tensor(below, rep(l, 8), spread(l, 8), ALU.is_equal))
                do(v.tensor_tensor(below, below, lower, ALU.mult))
                do(v.tensor_tensor(above, above, below, ALU.add))
                do(v.tensor_reduce(rt[:, 3, t, :], above, AX, ALU.add))
                do(v.tensor_scalar(rt[:, 1, t, :], rt[:, 3, t, :], 2.0, None, ALU.is_lt), c.sig("selected") if t else None)
            for t in range(NT):
                do(v.tensor_reduce(xtr[:, t, 0:1], rt[:, 0, t, :], AX, ALU.max, negate=True), c.sig("router_max") if t else None)
            dve.wait_ge(*c.at("exp_done", "router"))
            for t in range(NT):
                do(v.tensor_tensor_reduce(rt[:, 4, t, :], rt[:, 2, t, :], rt[:, 1, t, :], 1.0, 0.0, ALU.mult, ALU.add, xtr[:, t, 1:2]))
                do(v.reciprocal(xtr[:, t, 2:3], xtr[:, t, 1:2]))
            b = bank("slots")
            do(v.memset(pos[:, :, :, :].rearrange("p a t r -> p (a t r)"), 0.0))
            do(v.tensor_copy(pos[:, 0, :, 0:NEXP], b[:, 0:16].rearrange("p (t e) -> p t e", t=NT)))
            do(v.tensor_copy(xtr[:, 3, :], b[:, 16:24]), J.free("slots"))
            do(v.tensor_copy(pos[:, 1, :, 0:NEXP], rt[:, 1, :, :]))
            for t in range(NT):
                do(v.tensor_scalar(pos[:, 2, t, 0:NEXP], rt[:, 4, t, :], xtr[:, t, 2:3], None, ALU.mult))
            big, rank = xtr[:, 4, :], xtr[:, 5, :]
            before_ = cmp[:, 0, 0:64].rearrange("p (e j) -> p e j", e=8)
            do(v.tensor_scalar(big, xtr[:, 3, :], float(P), None, ALU.is_gt))
            do(v.tensor_tensor(before_, rep(big, 8), C("lower").rearrange("p (e j) -> p e j", e=8), ALU.mult))
            do(v.tensor_reduce(rank, before_, AX, ALU.add))
            do(v.memset(rid[:, :], 0.0))
            do(v.tensor_copy(rid[:, 0:8], C("eid")))
            do(v.tensor_reduce(rid[:, 15:16], big, AX, ALU.add))
            do(v.tensor_scalar(rid[:, 15:16], rid[:, 15:16], float(NEXP), None, ALU.add))
            one = xtr[:, 6, :]
            six = cmp[:, 1, 0:48].rearrange("p (a e) -> p a e", e=8)
            for x in range(EXTRA):
                do(v.tensor_scalar(one, rank, float(x), None, ALU.is_equal))
                do(v.tensor_tensor(one, one, big, ALU.mult))
                do(v.tensor_tensor_reduce(cmp[:, 0, 0:8], one, C("eid"), 1.0, 0.0, ALU.mult, ALU.add, rid[:, 8 + x:9 + x]))
                for a in range(3):
                    do(v.tensor_tensor(six[:, 2 * a:2 * a + 2, :], pos[:, a, :, 0:NEXP], rep(one, 2), ALU.mult))
                    do(v.tensor_reduce(pos[:, a, :, NEXP + x], six[:, 2 * a:2 * a + 2, :], AX, ALU.add))
                do(v.tensor_scalar(pos[:, 0, :, NEXP + x], pos[:, 0, :, NEXP + x], float(-P), None, ALU.add))
            do(v.tensor_copy(ridi[:, :], rid[:, :]), c.sig("rounds_ready"))

            def dispatch(at_, key):
                for m, a in ((Pm, 1), (PG, 2)):
                    for t in range(NT):
                        do(v.tensor_scalar(m[:, t, :], C("iota"), pos[:, 0, t, at_], pos[:, a, t, at_], ALU.is_equal, ALU.mult),
                           c.sig("dispatch_ready", key) if a == 2 and t else None)

            gs, rs = vat["sw_ffn_norm_g_3"]

            def gathered(key):
                for q in range(2):
                    b = bank("hg" + key, q)
                    do(v.tensor_tensor(hgT[:, 4 * q:4 * q + 4, :], b[:, :].rearrange("p (a b) -> p a b", a=4),
                                       spread(vcol[:, gs, rs + 4 * q:rs + 4 * q + 4], P), ALU.mult), J.free("hg" + key, q))
                do(v.tensor_copy(xtr[:, 7, 1:2], ones[:, 0:1]), c.sig("gathered", key, 1))

            dispatch(slice(0, 1), "first")
            gathered("first")
            n_rounds = dve.value_load(ridi[0:1, 15:16], min_val=NEXP, max_val=NROUND)
            with dve.Fori(0, n_rounds) as r:
                c.enter(r)
                for g in range(FFE // 512):
                    b = bank("xu", g)
                    dve.wait_ge(*J.emptied("xg", g))
                    if g >= 2:
                        dve.wait_ge(*J.full("xt", g - 2))
                    do(v.tensor_tensor(eact[:, g % 2, :], esg[:, g % 2, :], b[:, :], ALU.mult), J.free("xu", g))
                    do(v.tensor_copy(xtr[:, 7, 1:2], ones[:, 0:1]), c.sig("act_ready", g))
                    if g == 3:
                        dispatch(bass.ds(r + 1, 1), "next")
                dve.wait_ge(*c.at("piece_used", "xdown", FFE // 256 - 1))
                do(v.tensor_copy(ey[:, 512:1024], acc[1][:, :]), c.sig("expert_out1", 0))
                gathered("next")
                for t in range(NT):
                    for h in range(2):
                        x = xres[:, t, h * 512:(h + 1) * 512]
                        do(v.tensor_tensor(x, x, bank("xs", t, h)[:, :], ALU.add), J.free("xs", t, h))
                c.leave()
            do(v.tensor_copy(mcol[:, 0, 0:1], ones[:, 0:1]), c.sig("x_ready", 5))

        @block.gpsimd
        def _(pool):
            g = nc.gpsimd

            def do(ins, s=None):
                s = s or c.sig("pool_step")
                ins.then_inc(s.sem, 1)
                pool.wait_ge(s.sem, s.val)

            def rstd(stage, src, dst, n, width, eps=RMS_EPS):
                do(g.tensor_scalar(dst, src, 1.0 / width, eps, ALU.mult, ALU.add))
                do(g.tensor_tensor(dst, dst, half_c[:, 0:n], ALU.pow), c.sig("rstd", stage))

            def norm(stage):
                s0 = 4 * NORMS.index(stage)
                pool.wait_ge(*c.at("squares_v", stage))
                rstd(stage, st[:, s0:s0 + 2], st[:, s0 + 2:s0 + 4], NT, D)

            pool.wait_ge(*c.at("exponent"))
            norm("pre")
            pool.wait_ge(*c.at("moments"))
            var = cmp[:, 1, 1:1 + 4 * MH:2]
            do(g.tensor_scalar(var, var, LN_EPS, None, ALU.add))
            do(g.tensor_tensor(var, var, half_c[:, 0:2 * MH], ALU.pow), c.sig("rstd", "mlstm"))
            pool.wait_ge(*c.at("normed", "mlstm"))
            for dst, col in ((gm, 2 * D), (gf, 5 * D)):
                pool.dma_start(dst, everywhere(A["ada_b_2"][:, col:col + D], D)).then_inc(c.sem("gates_bias_in"), 16)
            pool.wait_ge(*c.at("squares", "post1"))
            for t in range(NT):
                do(g.tensor_tensor(st[:, 4 + 2 * t:5 + 2 * t], st[:, 4 + 2 * t:5 + 2 * t], st[:, 5 + 2 * t:6 + 2 * t], ALU.add))
            rstd("post1", st[:, 4:8:2], st[:, 40:42], NT, D)
            if upto < 2:
                return
            norm("mix2")
            pool.wait_ge(*c.at("x_ready", 1))
            pool.dma_start(wide[:, :], everywhere(A["final_norm_g_2"], D)).then_inc(c.sem("final_gain_in"), 16)
            pool.wait_ge(*c.at("squares_v", "subln"))
            rstd("subln", st[:, 44:52], st[:, 52:60], 8, P)
            norm("ffn2")
            if upto >= 3:
                pool.dma_start(memx, A["mem_3"].rearrange("a (t p) d -> p (a t) d", p=P)).then_inc(c.sem("mem_in"), 16)
                norm("mem")
            norm("final2")
            if upto < 3:
                return
            norm("cv")
            norm("cvf")
            if upto < 4:
                return
            norm("sw")
            if upto < 5:
                return
            norm("moe")

        del block
    return c, J, W


NORMS = ["pre", "post1", "mix2", "ffn2", "mem", "final2", "cv", "cvf", "sw", "moe"]
_INS = ["x", "rel_bias", "g_pre", "g_post", "w_in", "conv_w", "conv_b", "wq_m", "wk_m", "wv_m", "w_if", "b_if", "mh_norm",
        "skip", "w_out", "c_2", "ada_w_2", "ada_b_2", "mix_norm_g_2", "w_in_2", "lambda_q1_2", "lambda_k1_2",
        "lambda_q2_2", "lambda_k2_2", "diff_subln_g_2", "w_out_2", "ffn_norm_g_2", "w_ff1_2", "w_ff2_2",
        "final_norm_g_2", "mem_3", "mem_norm_g_3", "w_mem_kv_3", "mem_k_norm_g_3", "cv_attn_norm_g_3", "cv_w_in_3",
        "cv_b_glu_3", "cv_dw_w_3", "cv_dw_b_3", "cv_ln_g_3", "cv_ln_b_3", "cv_memq_norm_g_3", "cv_w_out_3",
        "cv_ffn_norm_g_3", "cv_w_gate_3", "cv_w_up_3", "cv_w_down_3", "sw_attn_norm_g_3", "sw_w_in_3", "sw_q_norm_g_3",
        "sw_k_norm_g_3", "sw_sinks_3", "sw_memq_norm_g_3", "sw_w_out_3", "sw_ffn_norm_g_3", "sw_router_3",
        "sw_we_gate_3", "sw_we_up_3", "sw_we_down_3"]


def build(core, inputs, upto=9):
    table, const_at = constants()
    known = None
    for _ in range(2):
        nc = core()
        arrays, A = {"consts": table}, {}
        for name in _INS:
            arrays[name] = np.ascontiguousarray(inputs[name])
        for name, a in arrays.items():
            A[name] = nc.dram_tensor(f"in_{name}", a.shape, F32, kind="ExternalInput").ap()
        out = nc.dram_tensor("out_dram", (1, S, D), F32, kind="ExternalOutput").ap()
        known = program(nc, A, out, const_at, known, upto)
    return nc, {f"in_{name}": a for name, a in arrays.items()}


def kernel(**inputs):
    import concourse.bacc as bacc
    from concourse.bass_utils import run_bass_kernel_spmd
    nc, arrays = build(lambda: bacc.Bacc("TRN2", target_bir_lowering=False, num_devices=1), inputs)
    r = run_bass_kernel_spmd(nc, [arrays], core_ids=[0])
    return r.results[0]["out_dram"]
```

```python
from contextlib import ExitStack

import numpy as np

import concourse.bass as bass
from concourse import mybir

F32 = mybir.dt.float32
F32R = mybir.dt.float32r
I32 = mybir.dt.int32
ALU = mybir.AluOpType
ACT = mybir.ActivationFunctionType
AX = mybir.AxisListType.X

P = 128
S = 256
NT = S // P
D = 1024
KC = D // P
HEADS1, DH1 = 8, 128
MH, MD = 4, 256
H64 = 64
NDIFF, NSB = 4, 8
FF2 = 4096
CONV, CONVW = 768, 31
CC = CONV // P
CONV_PE = (4, 5)
DIAGS = 16
MEMH = 4
SWAH, SWAKV = 12, 4
FFD = 2816
NEXP, FFE = 8, 3584
EXTRA = (2 * S) // (P + 1)
NROUND = NEXP + EXTRA
RING = 7
PIECE = 2048
NEG = -1e30
RMS_EPS, LN_EPS = 1e-6, 1e-5
LAMBDA_INIT = 0.2

ROUND_JOBS = 28
ROUND_PIECES = [(w, g, h) for g in range(FFE // 512) for w in ("xgate", "xup") for h in range(2)] \
    + [("xdown", k) for k in range(FFE // 256)]
HALVES = 2 * len(ROUND_PIECES)
POOL_PIECES = (0,)
SPLITS = 6
B1_BETWEEN = {0: 3072, 1: 3584, 3: 4096, 5: 4608, 7: 5120, 9: 5632}
ADA = [0, 1, 2, 3, 6, 7, 8, 9, 4, 5, 10, 11]
T384 = [(0, 0, 1), (1, 128, 2)]
T512 = [(0, 0, 2), (1, 256, 2)]


def constants():
    p = np.arange(P)[:, None]
    t = np.arange(S)[None, :]
    f = np.float32
    causal = np.concatenate([np.where(t[:, :P] <= p, 0, NEG), np.where(t <= p + P, 0, NEG)], 1)
    chunk = np.concatenate([np.where(t[:, :P] // 64 <= p // 64, 0, NEG), np.where(t // 64 <= (p + P) // 64, 0, NEG)], 1)
    d0, d1 = p - t[:, :P], p + P - t
    dist = np.concatenate([d0, d1], 1)
    window = np.where((dist >= 0) & (dist < 128), 0, NEG)
    inv = (1.0 / (f(10000.0) ** (np.arange(0, 64, 2, dtype=f) / f(64)))).astype(f)
    ang = (np.arange(S, dtype=f)[:, None] * inv[None, :]).astype(f)
    ang = np.concatenate([ang, ang], 1)
    cos, sin = np.cos(ang).T, np.sin(ang).T
    rot = np.zeros((P, P))
    for h in (0, 64):
        for i in range(32):
            rot[h + 32 + i, h + i] = -1.0
            rot[h + i, h + 32 + i] = 1.0
    n = np.arange(511) - 255
    d = np.maximum(-n, 0)
    nf = np.maximum(d, 1).astype(f)
    large = 16 + (np.log(nf / f(16)) / f(np.log(2048 / 16)) * f(16)).astype(np.int32)
    bucket = np.where(d < 16, d, np.minimum(large, 31))
    rel = np.zeros((P, 511))
    rel[bucket, np.arange(511)] = 1.0
    rel[:, n > 0] = 0.0
    rel[32, n > 0] = NEG
    e, j = np.arange(8)[:, None], np.arange(8)[None, :]
    hsel = np.zeros((P, MH, P))
    for h in range(MH):
        hsel[h, h] = 1.0
    parts = {
        "ident": np.eye(P), "ones": np.ones((P, P)),
        "upto": np.concatenate([p <= t, p + P <= t], 1), "before": np.concatenate([p < t, p + P < t], 1),
        "after": p > t[:, :P], "causal": causal, "chunk": chunk,
        "earlier": np.concatenate([p < t, p + P < t[:, P:]], 1), "dist": np.maximum(dist, 0), "window": window,
        "block4": np.repeat(p // 4 == np.arange(32)[None, :], 4, 1), "half": (p // 64) == (np.arange(P)[None, :] // 64),
        "rot": rot, "cos": np.tile(cos, (2, 1)), "sin": np.tile(sin, (2, 1)), "rel": rel, "hsel": hsel.reshape(P, -1),
        "iota": np.broadcast_to(np.arange(P)[None, :], (P, P)), "lower": np.broadcast_to((j < e).reshape(1, 64), (P, 64)),
        "eid": np.broadcast_to(np.arange(8)[None, :], (P, 8)), "slots": np.broadcast_to(np.arange(4)[None, :], (P, 4)),
        "eps": np.broadcast_to(np.array([[RMS_EPS, LN_EPS]]), (P, 2)),
    }
    at, out, n = {}, [], 0
    for k, a in parts.items():
        at[k] = (n, n + a.shape[1])
        n += a.shape[1]
        out.append(np.asarray(a, f))
    return np.ascontiguousarray(np.concatenate(out, 1)), at


class Signal:
    def __init__(self, name, sem, val, base):
        self.name, self.sem, self.val, self.base = name, sem, val, base


class Count:

    def __init__(self, known=None):
        self.known, self.seen, self.n, self.sems = known, {}, {}, {}
        self.loop, self.start, self.per = None, {}, {}

    def sem(self, name):
        if name not in self.sems:
            self.sems[name] = self.make(name)
        return self.sems[name]

    def enter(self, r):
        self.loop, self.start = r, dict(self.n)

    def leave(self):
        for b in range(4):
            self.per[f"filled{b}"] = self.per[f"drained{b}"] = ROUND_JOBS // 4
        for k, v in self.n.items():
            if v != self.start.get(k, 0) and k not in self.per:
                self.per[k] = v - self.start.get(k, 0)
        self.loop = None

    def value(self, name, v):
        per = self.known.per.get(name, 0) if self.known else 0
        return v if self.loop is None or per == 0 else self.loop * per + v

    def sig(self, name, *key, by=1):
        self.n[name] = self.n.get(name, 0) + by
        self.seen[(name,) + key] = self.n[name]
        return Signal(name, self.sem(name), self.value(name, self.n[name]), self.n[name])

    def at(self, name, *key):
        v = self.known.seen[(name,) + key] if self.known else 1
        return self.sem(name), self.value(name, v)

    def before(self, name, *key):
        v = self.known.seen[(name,) + key] - self.known.per[name] if self.known else 1
        return self.sem(name), self.value(name, v)


class Jobs:

    def __init__(self, count, known=None):
        self.c, self.known, self.n, self.seen = count, known, 0, {}

    def number(self, *key):
        return self.known.seen[key] if self.known else self.seen.get(key, 0)

    def bank(self, *key):
        return self.number(*key) % 4

    def fill(self, pe, *key):
        n = self.n
        self.seen[key] = n
        self.n += 1
        if n >= 4:
            name = f"drained{n % 4}"
            pe.wait_ge(self.c.sem(name), self.c.value(name, n // 4))
        return n % 4

    def filled(self, *key):
        n = self.number(*key)
        name = f"filled{n % 4}"
        self.c.n[name] = max(self.c.n.get(name, 0), n // 4 + 1)
        return Signal(name, self.c.sem(name), self.c.value(name, n // 4 + 1), n // 4 + 1)

    def full(self, *key):
        n = self.number(*key)
        name = f"filled{n % 4}"
        return self.c.sem(name), self.c.value(name, n // 4 + 1)

    def free(self, *key):
        n = self.number(*key)
        name = f"drained{n % 4}"
        self.c.n[name] = max(self.c.n.get(name, 0), n // 4 + 1)
        return Signal(name, self.c.sem(name), self.c.value(name, n // 4 + 1), n // 4 + 1)

    def emptied(self, *key):
        n = self.number(*key)
        name = f"drained{n % 4}"
        return self.c.sem(name), self.c.value(name, n // 4 + 1)


class Stream:

    def __init__(self, count, known=None):
        self.c, self.known, self.n, self.number, self.freed = count, known, 0, {}, {}
        self.slot, self.landing, self.halves = [0] * RING, {}, {}

    def free(self, key, signal):
        n = self.number[key]
        self.freed[n] = (signal.name, signal.base)

    def half_free(self, hp, signal):
        self.halves[hp] = (signal.name, signal.base)

    def half_wait(self, hp):
        name, v = self.known.halves[(hp - SPLITS) % HALVES] if self.known else ("piece_used", 1)
        if hp < SPLITS and self.known:
            v -= self.c.known.per[name]
        return self.c.sem(name), self.c.value(name, v)

    def place(self, key):
        return self.known.landing[key][0] if self.known else 0

    def landed(self, key):
        s, v = self.known.landing[key] if self.known else (0, 16)
        return self.c.sem(f"landed{s}"), self.c.loop * (16 * len(ROUND_PIECES) // RING) + v

    def low_name(self, hp):
        return "lo_ready_pool" if hp // 2 in POOL_PIECES else "lo_ready"

    def ready(self, key):
        s, v = self.known.landing[key] if self.known else (0, 16)
        return self.c.sem(f"landed{s}"), v


def program(nc, A, out, const_at, known=None, upto=9):
    c = Count(known[0] if known else None)
    J = Jobs(c, known[1] if known else None)
    W = Stream(c, known[2] if known else None)
    ctx = ExitStack()
    with ctx:
        c.make = lambda name: ctx.enter_context(nc.semaphore(name))
        if known:
            for name in known[0].sems:
                c.sem(name)

        def sb(name, *shape, dt=F32):
            return ctx.enter_context(nc.sbuf_tensor(name, [P, *shape], dt))

        consts = sb("consts", max(b for _, b in const_at.values()))

        def C(name, n=0):
            a, b = const_at[name]
            v = consts[:, a:b]
            return v.rearrange("p (a b) -> p a b", a=n) if n else v

        ident, ones = C("ident"), C("ones")
        ring = sb("ring", RING, PIECE)
        xres = sb("xres", NT, D)
        nrm = sb("nrm", NT, D)
        wide = sb("wide", D)
        vcol = sb("vcol", 4, P)
        st = sb("st", 64)
        smx = sb("smx", 4, 8)
        gl = sb("gl", 2, 8)
        lg = sb("lg", 2, 24)
        aT = sb("aT", 512)
        fcol = sb("fcol", 2, 4)
        mcol = sb("mcol", 4, 16)
        half_c = sb("half_c", 16)
        relb = sb("relb", HEADS1)
        brow = sb("brow", 8)
        sinkb = sb("sinkb", SWAH)
        fsink = sb("fsink", SWAH)
        lamv = sb("lamv", 4, H64)
        lam = sb("lam", 4)
        wif = sb("wif", 24, 8)
        wraw = sb("wraw", 24, 4)
        rw = sb("rw", KC, NEXP)
        ccol = sb("ccol", KC)
        modc = sb("modc", 32)
        rt = sb("rt", 6, NT, NEXP)
        cmp = sb("cmp", 2, NT * 64)
        pos = sb("pos", 3, NT, NROUND + 1)
        xtr = sb("xtr", 8, 8)
        rid = sb("rid", 16)
        ridi = sb("ridi", 16, dt=I32)
        with ExitStack() as phase:
            def sa(name, *shape):
                return phase.enter_context(nc.sbuf_tensor(name, [P, *shape], F32))

            arena = sa("arena", 16 * 1024)
            bd = sa("bd", 24, P)
            logit = sa("logit", 4, 512)
            probT = sa("probT", 2, 512)
            hT = sa("hT", KC, S)
            junk = sa("junk", D)
        with ExitStack() as phase:
            def se(name, *shape, dt=F32):
                return phase.enter_context(nc.sbuf_tensor(name, [P, *shape], dt))

            w_hi, w_lo = se("w_hi", SPLITS, PIECE // 2, dt=F32R), se("w_lo", SPLITS, PIECE // 2, dt=F32R)
            act_hi, act_lo = se("act_hi", 28, P, dt=F32R), se("act_lo", 28, P, dt=F32R)
            esg, ey = se("esg", 2, 512), se("ey", D)
            Pm, PG, pgT = se("Pm", NT, P), se("PG", NT, P), se("pgT", S)
            eact = se("eact", 2, 512)
            hg_hi, hg_lo = se("hg_hi", KC, P, dt=F32R), se("hg_lo", KC, P, dt=F32R)
        ps = [ctx.enter_context(nc.psum_tensor(f"bank{i}", [P, 512], F32)) for i in range(4)]
        acc = [ctx.enter_context(nc.psum_tensor(f"sum{i}", [P, 512], F32)) for i in range(4)]
        relrow = nc.dram_tensor("relrow", (P, HEADS1, 511), F32, kind="Internal").ap()

        def U(unit, *dims, off=0):
            n = int(np.prod(dims))
            v = arena[:, unit * 1024 + off:unit * 1024 + off + n]
            return v.rearrange("p (a b) -> p a b", a=dims[0]) if len(dims) == 2 else v

        relrep = U(0, HEADS1, 512)
        relw = logit[:, 0:2, :].rearrange("p a (b n) -> p (a b) n", n=P)
        mix1 = U(0, 16, S)
        relbias = U(4, HEADS1, 384)
        qT, kT, vt = U(8, 8, S), U(10, 8, S), U(12, NT, D)
        xmT, xcT, vm = U(14, 8, S), U(4, 8, S), U(6, NT, D)
        qmT, kmT, vmT = U(8, 8, S), U(10, 8, S), U(12, 8, S)
        vrows = [U(15, P, off=P * g) for g in range(4)]
        qraw = U(12, 4, 512)
        qdT, kdT, vd = U(0, 4, S), U(1, 4, S), U(2, NT, 512)
        sqT, skT, sv = U(3, 4, S), U(4, 4, S), U(5, NT, 512)
        mix2, fT = U(6, 8, S), U(0, 32, S)
        gm, gf = U(15, D), U(14, D)
        sbw = [U(8, 2, 1152), U(8, 2, 1152, off=2304), U(0, 2, 1152)]
        adasum = [probT[:, 0, :], probT[:, 1, :], junk[:, 0:512], junk[:, 512:1024]]
        cact = hT[:, 0:4, :].rearrange("p a (b n) -> p (a b) n", n=P)
        memkT, memv = U(15, 2, S), U(15, NT, 256, off=512)
        memx = U(12, NT, D)
        uT, cT = U(0, CC, S), U(2, CC, S)
        mqT, mq2 = U(4, 2, S), U(4, 512, off=512)
        sg3 = U(8, 4, 512)
        lnw, tap = U(10, 2, S), U(10, S, off=512)
        sq3 = U(13, CC, S)
        mix3 = U(6, 8, S)
        diag = U(12, DIAGS, P)
        actd = U(0, 22, S)
        rsw = U(11, 2, 512)
        swq, swk = U(0, 6, S), U(2, 2, S)
        swv = U(3, NT, 256)
        vgroups = [
            [("g_pre", 8), ("conv_w", 32), ("conv_b", 8), ("mh_norm", 8), ("skip", 8), ("mix_norm_g_2", 8),
             ("c_2", 8), ("ada_b_2", 48)],
            [("ffn_norm_g_2", 8), ("mem_norm_g_3", 8), ("cv_attn_norm_g_3", 8), ("cv_b_glu_3", 12), ("cv_dw_b_3", 6),
             ("cv_ln_g_3", 6), ("cv_ln_b_3", 6), ("cv_ffn_norm_g_3", 8), ("sw_attn_norm_g_3", 8),
             ("sw_ffn_norm_g_3", 8), ("diff_subln_g_2", 1), ("cv_memq_norm_g_3", 0), ("sw_q_norm_g_3", 0),
             ("sw_memq_norm_g_3", 0), ("mem_k_norm_g_3", 0), ("sw_k_norm_g_3", 0)],
            [("cv_dw_w_3", 96)], [("cv_dw_w_3", 90)],
        ]
        vat, vload = {}, []
        for g, group in enumerate(vgroups):
            r, loads = 0, []
            for name, n in group:
                src = A[name]
                src = src.rearrange({1: "a -> a", 2: "a b -> (a b)", 3: "a b c -> (a b c)"}[len(src.shape)])
                if n == 0:
                    for h in range(2):
                        loads.append((vrows[g][r:r + 1, h * H64:(h + 1) * H64], src.rearrange("(a b) -> a b", a=1)))
                else:
                    first = 96 if g == 3 else 0
                    loads.append((vrows[g][r:r + n, :], src.rearrange("(a b) -> a b", b=P)[first:first + n, :]))
                vat.setdefault(name, (g, r))
                r += n or 1
            vload.append((r, loads))

        def vec(name, i=0):
            g, r = vat[name]
            if name == "cv_dw_w_3" and i >= 96:
                g, r, i = 3, 0, i - 96
            return vcol[:, g, r + i:r + i + 1]

        def everywhere(src, n):
            return bass.AP(tensor=src.tensor, offset=src.offset, ap=[[0, P], [1, n]])

        block = ctx.enter_context(nc.Block())

        @block.sync
        def _(sp):
            for dst, src in vload[0][1]:
                sp.dma_start(dst, src).then_inc(c.sem("vrows_in0"), 16)
            sp.dma_start(xres[:, :, :], A["x"].rearrange("a (t p) d -> p (a t) d", p=P)).then_inc(c.sem("x_in"), 16)
            sp.dma_start(consts[:, 0:2 * P], A["consts"][:, 0:2 * P]).then_inc(c.sem("ident_in"), 16)
            base = [None]

            def piece(key, *loads):
                n = W.n
                W.n += 1
                W.number[key] = n
                s = n % RING
                if base[0] is not None:
                    i = n - base[0] - RING
                    hp = (2 * i + 1) % HALVES
                    sp.wait_ge(*(c.at if i >= 0 else c.before)(W.low_name(hp), hp))
                elif n >= RING:
                    name, v = W.known.freed[n - RING] if W.known else ("piece_used", 1)
                    sp.wait_ge(c.sem(name), c.value(name, v))
                for dst, src in loads:
                    sp.dma_start(dst(ring[:, s, :]), src).then_inc(c.sem(f"landed{s}"), 16)
                    W.slot[s] += 16
                W.landing[key] = (s, W.slot[s])

            def shaped(a, b, lo=0, hi=None):
                return lambda slot: slot[:, 0:a * b].rearrange("p (a b) -> p a b", a=a)[:, :, lo:b if hi is None else hi]

            def columns(name, w, col, cols=512):
                v = w.rearrange("(k p) n -> p k n", p=P)
                if cols == 256:
                    piece((name, col, 0), (shaped(KC, 256), v[:, :, col:col + 256]))
                    return
                for h in range(2):
                    piece((name, col, h), (shaped(4, 512), v[:, 4 * h:4 * h + 4, col:col + 512]))

            def chunk_rows(name, w, k):
                piece((name, k), (shaped(2, D), w.rearrange("(k p) n -> p k n", p=P)[:, 2 * k:2 * k + 2, :]))

            for i, beside in enumerate(((0,), (1,), (2,), (3, 4), (5, 6), (7,))):
                for x in beside:
                    columns("ada", A["ada_w_2"][0], 512 * ADA[x])
                columns("w_in", A["w_in"][0], 512 * i)
            for g in range(3072, 6144, 512):
                columns("w_in", A["w_in"][0], g)
            for name, i in (("w_out", 0), ("ada", 8), ("w_out", 1), ("w_out", 2), ("w_out", 3), ("ada", 9), ("ada", 10), ("ada", 11)):
                if name == "ada":
                    columns("ada", A["ada_w_2"][0], 512 * ADA[i])
                else:
                    chunk_rows("w_out", A["w_out"][0], i)
            for k in range(4, 8):
                chunk_rows("w_out", A["w_out"][0], k)
            if upto >= 2:
                for g in range(0, 3072, 512):
                    columns("w_in2", A["w_in_2"][0], g)
                for k in range(4):
                    chunk_rows("w_out2", A["w_out_2"][0], k)
                for g in range(0, FF2, 512):
                    columns("ff1", A["w_ff1_2"][0], g)
                for k in range(16):
                    chunk_rows("ff2", A["w_ff2_2"][0], k)
            if upto >= 3:
                columns("mem", A["w_mem_kv_3"], 0)
                for g in (0, 256, 512):
                    columns("cv_in", A["cv_w_in_3"][0], g, 256)
                    columns("cv_in", A["cv_w_in_3"][0], CONV + g, 256)
                columns("cv_in", A["cv_w_in_3"][0], 2 * CONV, 256)
                for k in (3, 0, 1, 2):
                    chunk_rows("cv_out", A["cv_w_out_3"][0], k)
                for g in range(0, FFD, 256):
                    columns("gate", A["cv_w_gate_3"][0], g, 256)
                    columns("up", A["cv_w_up_3"][0], g, 256)
                for k in range(11):
                    chunk_rows("down", A["cv_w_down_3"][0], k)
            if upto >= 4:
                v = A["sw_w_in_3"][0].rearrange("(k p) n -> p k n", p=P)

                for g in range(2):
                    for h in range(2):
                        piece(("sw_in", g, h),
                              *((shaped(4, 512, P * x + H64 * y, P * x + H64 * (y + 1)),
                                 v[:, 4 * h:4 * h + 4, 384 * g + 192 * y + H64 * x:384 * g + 192 * y + H64 * (x + 1)])
                                for x in range(3) for y in range(2)),
                              (shaped(4, 512, 384), v[:, 4 * h:4 * h + 4, 768 + P * g:768 + P * (g + 1)]))
                columns("sw_in", A["sw_w_in_3"][0], 1024)
                for k in range(4):
                    chunk_rows("sw_out", A["sw_w_out_3"][0], k)
            if upto >= 5:
                for n in range(W.n - RING, W.n):
                    sp.wait_ge(*((c.sem(W.known.freed[n][0]), W.known.freed[n][1]) if W.known else (c.sem("piece_used"), 1)))
                base[0], slot0 = W.n, list(W.slot)
                gate, up, down = (A[f"sw_we_{x}_3"].rearrange("a e (k p) n -> (a e) p k n", p=P) for x in ("gate", "up", "down"))

                def expert(e):
                    W.n, W.slot = base[0], list(slot0)
                    for key in ROUND_PIECES:
                        if key[0] == "xdown":
                            piece(key, (shaped(2, D), down[e, :, 2 * key[1]:2 * key[1] + 2, :]))
                        else:
                            w, (_, g, h) = gate if key[0] == "xgate" else up, key
                            piece(key, (shaped(4, 512), w[e, :, 4 * h:4 * h + 4, g * 512:(g + 1) * 512]))
                    assert W.n - base[0] == 6 * RING and HALVES % SPLITS == 0

                with sp.Fori(0, NEXP) as r:
                    c.loop = r
                    expert(r)
                    c.loop = None
                sp.wait_ge(*c.at("rounds_ready"))
                n_rounds = sp.value_load(ridi[0:1, 15:16], min_val=NEXP, max_val=NROUND)
                with sp.If(n_rounds > NEXP):
                    with sp.Fori(NEXP, n_rounds) as r:
                        e = sp.value_load(ridi[0:1, bass.ds(r, 1)], min_val=0, max_val=NEXP - 1)
                        c.loop = r
                        expert(e)
                        c.loop = None
            sp.wait_ge(*c.at("x_ready", min(upto, 5)))
            sp.dma_start(out.rearrange("a (t p) d -> p (a t) d", p=P), xres[:, :, :]).then_inc(c.sem("out_stored"), 16)
            sp.wait_ge(c.sem("out_stored"), 16)

        @block.tensor
        def _(pe):
            mm = nc.tensor.matmul

            def landed(key):
                s, v = W.known.landing[key] if W.known else (0, 16)
                pe.wait_ge(c.sem(f"landed{s}"), v if c.loop is None else c.loop * 96 + v)
                return ring[:, s, :]

            def chunks(name, col, cols=512):
                if cols == 256:
                    v = landed((name, col, 0)).rearrange("p (k n) -> p k n", k=KC)
                    return [v[:, k, :] for k in range(KC)], [(name, col, 0)]
                w = []
                for h in range(2):
                    v = landed((name, col, h)).rearrange("p (k n) -> p k n", k=4)
                    w += [v[:, k, :] for k in range(4)]
                return w, [(name, col, 0), (name, col, 1)]

            def done(last, *key):
                s = J.filled(*key)
                last.then_inc(s.sem, 1)
                return s

            def free(keys, signal):
                for k in keys:
                    W.free(k, signal)

            def turn(stage, src, n=KC):
                for q in range(n // 2):
                    b = J.fill(pe, stage, q)
                    for j in range(2):
                        for t in range(NT):
                            last = nc.tensor.transpose(ps[b][:, j * S + t * P:j * S + (t + 1) * P],
                                                       src[:, t, (2 * q + j) * P:(2 * q + j + 1) * P], ident)
                    done(last, stage, q)

            def turned(stage, n=4):
                for q in range(n):
                    pe.wait_ge(*J.emptied(stage, q))

            def proj_T(stage, w, c0, q):
                b = J.fill(pe, stage, q)
                for j in range(2):
                    for k in range(KC):
                        last = mm(ps[b][:, j * S:(j + 1) * S], w[k][:, c0 + j * P:c0 + (j + 1) * P], hT[:, k, :],
                                  start=(k == 0), stop=(k == KC - 1))
                return done(last, stage, q)

            def cols_T(stage, name, col, cols=512):
                w, keys = chunks(name, col, cols)
                for q in range(cols // 256):
                    s = proj_T(stage, w, q * 256, col // 256 + q)
                free(keys, s)

            def cols_tok(stage, name, col):
                w, keys = chunks(name, col)
                for t in range(NT):
                    b = J.fill(pe, stage, col, t)
                    for k in range(KC):
                        last = mm(ps[b][:, :], hT[:, k, t * P:(t + 1) * P], w[k], start=(k == 0), stop=(k == KC - 1))
                    s = done(last, stage, col, t)
                free(keys, s)

            def sum_rows(stage, name, n, mixT, ready=lambda k: None, ks=None, first=0, last_=None):
                last_ = n - 1 if last_ is None else last_
                for k in ks or range(n):
                    w = landed((name, k)).rearrange("p (k n) -> p k n", k=2)
                    ready(k)
                    for j in range(2):
                        kk = 2 * k + j
                        for t in range(NT):
                            for h in range(2):
                                last = mm(acc[2 * t + h][:, :], mixT[:, kk, t * P:(t + 1) * P],
                                          w[:, j, h * 512:(h + 1) * 512], start=(k == first and j == 0), stop=(k == last_ and j == 1))
                    s = c.sig("piece_used", stage, k)
                    last.then_inc(s.sem, 1)
                    free([(name, k)], s)

            def scores(stage, i, segs, score):
                b = J.fill(pe, stage + "S", i)
                for t, col, nk in segs:
                    last = score(i, t, ps[b][:, col:col + nk * P], nk)
                done(last, stage + "S", i)

            def turn_probs(stage, h, segs, buf):
                pe.wait_ge(*c.at("probs_ready", stage, h))
                b = J.fill(pe, stage + "T", h)
                for x in range(sum(nk for _, _, nk in segs)):
                    last = nc.tensor.transpose(ps[b][:, x * P:(x + 1) * P], logit[:, buf, x * P:(x + 1) * P], ident)
                done(last, stage + "T", h)

            def out_T(stage, h, segs, v, base, width):
                pe.wait_ge(*J.emptied(stage + "T", h))
                b = J.fill(pe, stage + "O", h)
                x = 0
                for t, col, nk in segs:
                    for k in range(nk):
                        last = mm(ps[b][base:base + width, t * P:(t + 1) * P], v(k), probT[:, h % 2, x * P:(x + 1) * P],
                                  start=(k == 0), stop=(k == nk - 1))
                        x += 1
                done(last, stage + "O", h)

            def attend(stage, H, segs, score, v, place, between=lambda i: None):
                for i in range(H + 3):
                    if i < H:
                        scores(stage, i, segs, score)
                    between(i)
                    if 2 <= i < H + 2:
                        turn_probs(stage, i - 2, segs, (i - 2) % 4)
                    if i >= 3:
                        out_T(stage, i - 3, segs, v(i - 3), *place(i - 3))

            def head_rms(stage, n, ready=None):
                for q in range(n):
                    pe.wait_ge(*c.at("squares", stage, q))
                    b = J.fill(pe, stage, q)
                    done(mm(ps[b][:, :], C("half"), logit[:, q % 2, :], start=True, stop=True), stage, q)

            def columns_of(g):
                pe.wait_ge(c.sem(f"vrows_in{g}"), 16 * len(vload[g][1]))
                b, r = J.fill(pe, "vec", g), vload[g][0]
                done(nc.tensor.transpose(ps[b][:, 0:r], vrows[g][0:r, :], ident[0:r, 0:r]), "vec", g)

            pe.wait_ge(c.sem("ident_in"), 16)
            columns_of(0)

            pe.wait_ge(*c.at("normed", "pre"))
            turn("pre", nrm)
            turned("pre")

            def ada_columns(*places):
                for x in places:
                    pe.wait_ge(*c.at("ada_sum", x, 1))
                    b = J.fill(pe, "ada", ADA[x])
                    for j in range(4):
                        last = mm(ps[b][:, j:j + 1], adasum[x % 4][:, j * P:(j + 1) * P], ones[:, 0:1], start=True, stop=True)
                    done(last, "ada", ADA[x])

            def ada_gates(*places):
                for g in (ADA[x] for x in places):
                    w, keys = chunks("ada", g * 512)
                    b = J.fill(pe, "ada", g)
                    for k in range(KC):
                        last = mm(ps[b][:, :], cact[:, k, :], w[k], start=(k == 0), stop=(k == KC - 1))
                    free(keys, done(last, "ada", g))

            cols_T("b1p", "w_in", 0)
            cols_T("b1p", "w_in", 512)
            ada_columns(0, 1)
            pe.wait_ge(*c.at("rel_wide"))
            pe.wait_ge(c.sem("consts_in"), 16)
            for h in range(HEADS1):
                b = J.fill(pe, "rel", h)
                done(mm(ps[b][:, 0:511], relw[0:33, h, :], C("rel")[0:33, :], start=True, stop=True), "rel", h)
            for g in range(1, 4):
                columns_of(g)
            cols_T("b1p", "w_in", 1024)
            ada_columns(2)
            cols_T("b1p", "w_in", 1536)
            ada_columns(3, 4)
            cols_tok("b1v", "w_in", 2048)
            ada_columns(5, 6)
            cols_tok("b1v", "w_in", 2560)
            ada_columns(7)
            for q in range(8):
                pe.wait_ge(*J.emptied("b1p", q))
            for col in (2048, 2560):
                for t in range(NT):
                    pe.wait_ge(*J.emptied("b1v", col, t))

            def b1_between(i):
                if i in B1_BETWEEN:
                    cols_T("b1p", "w_in", B1_BETWEEN[i])

            attend("b1", HEADS1, T384,
                   lambda h, t, dst, nk: mm(dst, qT[:, h, t * P:(t + 1) * P], kT[:, h, 0:nk * P], start=True, stop=True),
                   lambda h: lambda k: vt[:, k, h * P:(h + 1) * P], lambda h: (0, P), b1_between)

            pe.wait_ge(*c.at("bd_ready"))
            for q in range(16, 20):
                pe.wait_ge(*J.emptied("b1p", q))
            for m, (key, src) in enumerate((("qm", xcT), ("km", xcT), ("vmT", xmT))):
                for q in range(4):
                    if m == 0:
                        pe.wait_ge(*c.at("conv_ready", 2 * q + 1))
                    b = J.fill(pe, key, q)
                    for j in range(2):
                        last = mm(ps[b][:, j * S:(j + 1) * S], bd[:, 8 * m + 2 * q + j, :], src[:, 2 * q + j, :],
                                  start=True, stop=True)
                    done(last, key, q)
            for t in range(NT):
                for q in range(2):
                    b = J.fill(pe, "vm", t, q)
                    for j in range(4):
                        last = mm(ps[b][:, j * P:(j + 1) * P], xmT[:, 4 * q + j, t * P:(t + 1) * P], bd[:, 16 + 4 * q + j, :],
                                  start=True, stop=True)
                    done(last, "vm", t, q)
            def b1_out(*ks):
                sum_rows("b1", "w_out", 8, mix1, lambda k: pe.wait_ge(*J.emptied("mlstm", k - 4)) if k >= 4 else None, ks)

            for h in range(HEADS1):
                pe.wait_ge(*J.emptied("b1O", h))
            b1_out(0)
            pe.wait_ge(*c.at("c_ready"))
            ada_gates(8)
            pe.wait_ge(c.sem("wif_in"), 32)
            for key in ("qm", "km", "vmT"):
                for q in range(4):
                    pe.wait_ge(*J.emptied(key, q))
            b = J.fill(pe, "gates")
            for t in range(NT):
                o = ps[b][:, t * 8:t * 8 + 8]
                for m, src in enumerate((qmT, kmT, vmT)):
                    for k in range(KC):
                        mm(o, src[:, k, t * P:(t + 1) * P], wif[:, 8 * m + k, :], start=(m + k == 0), stop=False)
                last = mm(o, ones[0:1, :], brow[0:1, 0:8], start=False, stop=True)
            done(last, "gates")
            b1_out(1)
            pe.wait_ge(*c.at("loggates"))
            b = J.fill(pe, "Frow")
            for k in range(NT):
                mm(ps[b][0:MH, 0:S], gl[:, k, 4:8], C("upto", 2)[:, k, :], start=(k == 0), stop=(k == 1))
            for k in range(NT):
                last = mm(ps[b][0:MH, S + k * P:S + (k + 1) * P], gl[:, k, 0:4], ident, start=True, stop=True)
            done(last, "Frow")
            b = J.fill(pe, "Fcol")
            for t in range(NT):
                for k in range(t + 1):
                    last = mm(ps[b][:, t * 4:t * 4 + 4], C("upto", 2)[:, k, t * P:(t + 1) * P], gl[:, k, 4:8],
                              start=(k == 0), stop=(k == t))
            done(last, "Fcol")
            pe.wait_ge(*c.at("a_rows"))
            for t in range(NT):
                for q in range(2):
                    pe.wait_ge(*J.emptied("vm", t, q))
            for i in range(MH + 2):
                if i < MH:
                    b = J.fill(pe, "mA", i)
                    for t, col, nk in T384:
                        last = mm(ps[b][:, col:col + nk * P], C("hsel", MH)[0:MH, i, :], aT[0:MH, 0:nk * P], start=True, stop=True)
                    done(last, "mA", i)
                    b = J.fill(pe, "mS", i)
                    for t, col, nk in T384:
                        for k in range(2):
                            last = mm(ps[b][:, col:col + nk * P], qmT[:, 2 * i + k, t * P:(t + 1) * P], kmT[:, 2 * i + k, 0:nk * P],
                                      start=(k == 0), stop=(k == 1))
                    done(last, "mS", i)
                if i in (1, 3):
                    b1_out(2 + i // 2)
                if 1 <= i <= MH:
                    turn_probs("m", i - 1, T384, (i - 1) % 4)
                if i >= 2:
                    h = i - 2
                    pe.wait_ge(*J.emptied("mT", h))
                    b = J.fill(pe, "mO", h)
                    for t, x, k, stop in ((0, 0, 0, True), (1, 1, 0, False), (1, 2, 1, True)):
                        last = mm(ps[b][:, t * S:(t + 1) * S], probT[:, h % 2, x * P:(x + 1) * P], vm[:, k, h * MD:(h + 1) * MD],
                                  start=(k == 0), stop=stop)
                    done(last, "mO", h)
            ada_gates(9, 10, 11)
            pe.wait_ge(*c.at("normed", "mlstm"))
            turn("mlstm", nrm)
            b1_out(4, 5, 6, 7)

            if upto < 2:
                return
            pe.wait_ge(*c.at("normed", "mix2"))
            turn("mix2", nrm)
            turned("mix2")
            for x, col in enumerate((0, 512)):
                cols_T("dqk", "w_in2", col)
            cols_tok("b2v", "w_in2", 1024)
            for q in range(4):
                pe.wait_ge(*J.emptied("dqk", q))
                b = J.fill(pe, "rot", q)
                done(mm(ps[b][:, :], C("rot"), qraw[:, q, :], start=True, stop=True), "rot", q)
            for col in (1536, 2048):
                cols_T("sqk", "w_in2", col)
            cols_tok("b2v", "w_in2", 2560)
            for q in range(4):
                pe.wait_ge(*c.at("roped", q))
            for t in range(NT):
                pe.wait_ge(*J.emptied("b2v", 1024, t))

            def diff_score(i, t, dst, nk):
                h, m = i // 2, 64 * (i % 2)
                return mm(dst, qdT[m:m + 64, h, t * P:(t + 1) * P], kdT[m:m + 64, h, 0:nk * P], start=True, stop=True)

            for i in range(NDIFF + 2):
                if i < NDIFF:
                    scores("d", 2 * i, T384, diff_score)
                    scores("d", 2 * i + 1, T384, diff_score)
                if 1 <= i <= NDIFF:
                    turn_probs("dd", i - 1, T384, 2 * ((i - 1) % 2))
                if i >= 2:
                    h = i - 2
                    pe.wait_ge(*J.emptied("ddT", h))
                    b = J.fill(pe, "ddO", h)
                    for t, x, k, stop in ((0, 0, 0, True), (1, 1, 0, False), (1, 2, 1, True)):
                        last = mm(ps[b][:, t * P:(t + 1) * P], probT[:, h % 2, x * P:(x + 1) * P], vd[:, k, h * P:(h + 1) * P],
                                  start=(k == 0), stop=stop)
                    done(last, "ddO", h)
            for q in range(6, 10):
                pe.wait_ge(*J.emptied("sqk", q))
            for t in range(NT):
                pe.wait_ge(*J.emptied("b2v", 2560, t))
            for i in range(NSB // 2 + 2):
                for h in (2 * i, 2 * i + 1) if i < NSB // 2 else ():
                    m, ch = 64 * (h % 2), h // 2
                    b = J.fill(pe, "sbz", h)
                    mm(ps[b][:, 0:S], skT[m:m + 64, ch, 0:P], sqT[m:m + 64, ch, :], start=True, stop=True)
                    done(mm(ps[b][:, S:S + P], skT[m:m + 64, ch, P:S], sqT[m:m + 64, ch, P:S], start=True, stop=True), "sbz", h)
                if 1 <= i <= NSB // 2:
                    pe.wait_ge(*c.at("log1m_ready", i - 1))
                    for h in (2 * i - 2, 2 * i - 1):
                        l1 = sbw[h // 2 % 3][:, h % 2, 0:384]
                        b = J.fill(pe, "sbs", h)
                        mm(ps[b][:, 0:S], C("after"), l1[:, 0:S], start=True, stop=False)
                        mm(ps[b][:, P:S], ones, l1[:, S:S + P], start=False, stop=True)
                        done(mm(ps[b][:, S:S + P], C("after"), l1[:, S:S + P], start=True, stop=True), "sbs", h)
                if i >= 2:
                    pe.wait_ge(*c.at("sticks_ready", i - 2))
                    for h in (2 * i - 4, 2 * i - 3):
                        m, a = 64 * (h % 2), sbw[h // 2 % 3][:, h % 2, 384:768]
                        b = J.fill(pe, "sbo", h)
                        mm(ps[b][m:m + 64, 0:S], sv[:, 0, h * 64:(h + 1) * 64], a[:, 0:S], start=True, stop=False)
                        done(mm(ps[b][m:m + 64, P:S], sv[:, 1, h * 64:(h + 1) * 64], a[:, S:S + P], start=False, stop=True), "sbo", h)
            pe.wait_ge(*c.at("normed", "subln"))
            turn("subln", nrm, 4)
            turned("subln", 2)
            for h in range(NSB):
                pe.wait_ge(*J.emptied("sbo", h))
            sum_rows("b2", "w_out2", 4, mix2)
            pe.wait_ge(*c.at("normed", "ffn2"))
            turn("ffn2", nrm)
            turned("ffn2")
            for g in range(0, FF2, 512):
                cols_T("ff1", "ff1", g)

            def ff_ready(k):
                pe.wait_ge(*c.at("relu2_ready", k))
                if k == 13 and upto >= 3:
                    pe.wait_ge(*c.at("normed", "mem"))
                    turn("mem", nrm)

            sum_rows("ff", "ff2", 16, fT, ff_ready)
            if upto < 3:
                return

            turned("mem")
            w, keys = chunks("mem", 0)
            proj_T("memk", w, 0, 0)
            b = J.fill(pe, "memv")
            for t in range(NT):
                for k in range(KC):
                    last = mm(ps[b][:, t * 256:(t + 1) * 256], hT[:, k, t * P:(t + 1) * P], w[k][:, 256:512],
                              start=(k == 0), stop=(k == KC - 1))
            free(keys, done(last, "memv"))
            head_rms("memk2", 1)

            def mem_attend(stage, qsrc):
                attend(stage, MEMH, T512,
                       lambda h, t, dst, nk: mm(dst, qsrc[64 * (h % 2):64 * (h % 2) + 64, h // 2, t * P:(t + 1) * P],
                                                memkT[64 * (h % 2):64 * (h % 2) + 64, h // 2, :], start=True, stop=True),
                       lambda h: lambda k: memv[:, k, h * 64:(h + 1) * 64], lambda h: (64 * (h % 2), 64))

            pe.wait_ge(*c.at("normed", "cv"))
            turn("cv", nrm)
            turned("cv")
            for g in range(3):
                cols_T("cvp", "cv_in", CONV + 256 * g, 256)
                cols_T("cvp", "cv_in", 256 * g, 256)
            cols_T("cvp", "cv_in", 2 * CONV, 256)
            head_rms("cvq2", 1)
            pe.wait_ge(*J.emptied("cvp", 2))
            for x, k in enumerate(CONV_PE):
                for d in range(CONVW):
                    n = x * CONVW + d
                    pe.wait_ge(*c.at("tap_ready", n))
                    mm(acc[x][:, d:S], diag[:, n % DIAGS, :], uT[:, k, 0:S - d], start=(d == 0), stop=(d == CONVW - 1))\
                        .then_inc(c.sig("tap_used", n).sem, 1)
            pe.wait_ge(*c.at("head_normed", "memk2", 0))
            pe.wait_ge(*J.emptied("memv"))
            pe.wait_ge(*c.at("head_normed", "cvq2", 0))
            mem_attend("cm", mqT)
            for key, src in (("cmean", cT), ("cvar", sq3)):
                for k in range(CC):
                    if k == 0 or key == "cmean":
                        pe.wait_ge(*(c.at("conv_pool" if k < 1 else "cmean_in", k) if key == "cmean" else c.at("cvar_in")))
                    if k == 0:
                        b = J.fill(pe, key)
                    last = mm(ps[b][:, 0:S], ones, src[:, k, :], start=(k == 0), stop=(k == CC - 1))
                done(last, key)
                if key == "cmean":
                    for h in range(MEMH):
                        pe.wait_ge(*J.emptied("cmO", h))
                    sum_rows("cv", "cv_out", 4, mix3, ks=(3,), first=3, last_=2)
            sum_rows("cv", "cv_out", 4, mix3, lambda k: pe.wait_ge(*c.at("conv_act", 2 * k + 1)), (0, 1, 2), 3, 2)
            pe.wait_ge(*c.at("normed", "cvf"))
            turn("cvf", nrm)
            turned("cvf")
            for g in range(11):
                cols_T("fg", "gate", 256 * g, 256)
                cols_T("fu", "up", 256 * g, 256)
            sum_rows("dn", "down", 11, actd, lambda k: pe.wait_ge(*J.emptied("fu", k)))
            if upto < 4:
                return

            pe.wait_ge(*c.at("normed", "sw"))
            turn("sw", nrm)
            turned("sw")
            for g in range(2):
                w, keys = [], []
                for h in range(2):
                    v = landed(("sw_in", g, h)).rearrange("p (k n) -> p k n", k=4)
                    w += [v[:, k, :] for k in range(4)]
                    keys.append(("sw_in", g, h))
                for q in range(2):
                    b = J.fill(pe, "swp", 2 * g + q)
                    for j in range(2):
                        x = 2 * q + j
                        for k in range(KC):
                            last = mm(ps[b][:, j * S:(j + 1) * S], w[k][:, x * P:(x + 1) * P], hT[:, k, :],
                                      start=(k == 0), stop=(k == KC - 1))
                    s = done(last, "swp", 2 * g + q)
                free(keys, s)
            w, keys = chunks("sw_in", 1024)
            b = J.fill(pe, "swv")
            for t in range(NT):
                for k in range(KC):
                    last = mm(ps[b][:, t * 256:(t + 1) * 256], hT[:, k, t * P:(t + 1) * P], w[k][:, 0:256],
                              start=(k == 0), stop=(k == KC - 1))
            done(last, "swv")
            free(keys, proj_T("swm", w, 256, 0))
            head_rms("swn", 5)
            pe.wait_ge(*J.emptied("swv"))
            pe.wait_ge(*c.at("head_normed", "swn", 4))

            def swa_score(h, t, dst, nk):
                g, y, x = h // 6, 64 * (h % 6 // 3), h % 3
                return mm(dst, swq[y:y + 64, 3 * g + x, t * P:(t + 1) * P], swk[y:y + 64, g, 0:nk * P], start=True, stop=True)

            attend("sw", SWAH, T384, swa_score, lambda h: lambda k: swv[:, k, (h // 3) * 64:(h // 3 + 1) * 64],
                   lambda h: (64 * (h % 2), 64))
            mem_attend("sm", mqT)
            for st_, n in (("sw", SWAH), ("sm", MEMH)):
                for h in range(n):
                    pe.wait_ge(*J.emptied(st_ + "O", h))
            sum_rows("so", "sw_out", 4, mix3)
            if upto < 5:
                return

            pe.wait_ge(*c.at("normed", "moe"))
            turn("moe", nrm)
            turned("moe")
            pe.wait_ge(c.sem("rw_in"), 16)
            b = J.fill(pe, "router")
            for t in range(NT):
                for k in range(KC):
                    last = mm(ps[b][:, t * 8:t * 8 + 8], hT[:, k, t * P:(t + 1) * P], rw[:, k, :], start=(k == 0), stop=(k == KC - 1))
            done(last, "router")
            pe.wait_ge(*c.at("selected"))
            b = J.fill(pe, "slots")
            for t in range(NT):
                for k in range(t + 1):
                    mm(ps[b][:, t * 8:t * 8 + 8], C("before", 2)[:, k, t * P:(t + 1) * P], rt[:, 1, k, :], start=(k == 0), stop=(k == t))
            for k in range(NT):
                last = mm(ps[b][:, 16:24], ones, rt[:, 1, k, :], start=(k == 0), stop=(k == NT - 1))
            done(last, "slots")

            def gather(turn_):
                pe.wait_ge(*c.at("dispatch_ready", turn_))
                for q in range(2):
                    b = J.fill(pe, "hg" + turn_, q)
                    for j in range(4):
                        for t in range(NT):
                            last = mm(ps[b][:, j * P:(j + 1) * P], nrm[:, t, (4 * q + j) * P:(4 * q + j + 1) * P], Pm[:, t, :],
                                      start=(t == 0), stop=(t == NT - 1))
                    done(last, "hg" + turn_, q)

            def turn_gates():
                b = J.fill(pe, "pgT")
                for t in range(NT):
                    last = nc.tensor.transpose(ps[b][:, t * P:(t + 1) * P], PG[:, t, :], ident)
                done(last, "pgT")

            gather("first")
            pe.wait_ge(*c.at("rounds_ready"))
            n_rounds = pe.value_load(ridi[0:1, 15:16], min_val=NEXP, max_val=NROUND)
            with pe.Fori(0, n_rounds) as r:
                c.enter(r)

                def split(hp):
                    pe.wait_ge(*c.at(W.low_name(hp), hp))
                    return w_hi[:, hp % SPLITS, :], w_lo[:, hp % SPLITS, :]

                def turn_act(g):
                    pe.wait_ge(*J.emptied("xu", g))
                    b = J.fill(pe, "xt", g)
                    for j in range(4):
                        last = nc.tensor.transpose(ps[b][:, j * P:(j + 1) * P], eact[:, g % 2, j * P:(j + 1) * P], ident)
                    done(last, "xt", g)

                pe.wait_ge(*c.before("gathered", "next", 1))
                for g in range(FFE // 512):
                    for x, key in enumerate(("xg", "xu")):
                        b = J.fill(pe, key, g)
                        for q in range(4):
                            hp = 8 * g + 4 * x + q
                            hi, lo = split(hp)
                            for j in range(2):
                                k = 2 * q + j
                                cols = slice(j * 512, (j + 1) * 512)
                                mm(ps[b][:, :], hg_hi[:, k, :], hi[:, cols], start=(k == 0), stop=False)
                                mm(ps[b][:, :], hg_hi[:, k, :], lo[:, cols], start=False, stop=False)
                                last = mm(ps[b][:, :], hg_lo[:, k, :], hi[:, cols], start=False, stop=(k == KC - 1))
                            if q < 3:
                                s = c.sig("half_used", hp)
                                last.then_inc(s.sem, 1)
                            else:
                                s = done(last, key, g)
                            W.half_free(hp, s)
                    if g == 0:
                        turn_gates()
                    if g >= 1:
                        turn_act(g - 1)
                gather("next")
                turn_act(FFE // 512 - 1)
                for k in range(FFE // P):
                    hp = 8 * (FFE // 512) + k
                    if k % 4 == 0:
                        pe.wait_ge(*J.emptied("xt", k // 4))
                    hi, lo = split(hp)
                    for a, w in ((act_hi, hi), (act_hi, lo), (act_lo, hi)):
                        for h in range(2):
                            last = mm(acc[h][:, :], a[:, k, :], w[:, h * 512:(h + 1) * 512],
                                      start=(k == 0 and a is act_hi and w is hi), stop=(k == FFE // P - 1 and a is act_lo))
                    s = c.sig("piece_used", "xdown", k)
                    last.then_inc(s.sem, 1)
                    W.half_free(hp, s)
                pe.wait_ge(*J.emptied("pgT"))
                pe.wait_ge(*c.at("expert_out", 0))
                pe.wait_ge(*c.at("expert_out1", 0))
                for t in range(NT):
                    for h in range(2):
                        b = J.fill(pe, "xs", t, h)
                        done(mm(ps[b][:, :], pgT[:, t * P:(t + 1) * P], ey[:, h * 512:(h + 1) * 512], start=True, stop=True), "xs", t, h)
                c.leave()
        @block.scalar
        def _(act):
            def do(ins, s=None):
                s = s or c.sig("act_step")
                ins.then_inc(s.sem, 1)
                act.wait_ge(s.sem, s.val)

            def go(ins, s):
                ins.then_inc(s.sem, 1)

            f = nc.scalar.activation

            for g, (r, loads) in enumerate(vload):
                for dst, src in loads if g else ():
                    act.dma_start(dst, src).then_inc(c.sem(f"vrows_in{g}"), 16)
                if g == 0:
                    act.dma_start(relb[0:32, :], A["rel_bias"]).then_inc(c.sem("rel_in"), 16)
                    act.dma_start(consts[:, 2 * P:], A["consts"][:, 2 * P:]).then_inc(c.sem("consts_in"), 16)
            act.dma_start(wif[:, :, :], A["w_if"][0].rearrange("(k p) n -> p k n", p=P)).then_inc(c.sem("wif_in"), 16)
            act.dma_start(brow[0:1, :], A["b_if"]).then_inc(c.sem("wif_in"), 16)
            for m, name in enumerate(("wq_m", "wk_m", "wv_m")):
                act.dma_start(wraw[:, 8 * m:8 * m + 8, :], A[name][0].rearrange("(k n) i o -> (n i) k o", k=8))\
                    .then_inc(c.sem("wraw_in"), 16)
            act.dma_start(wide[:, :], everywhere(A["g_post"], D)).then_inc(c.sem("wide_in"), 16)
            act.dma_start(sinkb[:, :], everywhere(A["sw_sinks_3"], SWAH)).then_inc(c.sem("small_in"), 16)
            for i, name in enumerate(("lambda_q1_2", "lambda_k1_2", "lambda_q2_2", "lambda_k2_2")):
                act.dma_start(lamv[:, i, :], everywhere(A[name], H64)).then_inc(c.sem("small_in"), 16)
            act.dma_start(rw[:, :, :], A["sw_router_3"][0].rearrange("(k p) n -> p k n", p=P)).then_inc(c.sem("rw_in"), 16)

            def copy(dst, key, cols=512, lo=0, rows=slice(0, P), func=ACT.Copy):
                act.wait_ge(*J.full(*key))
                do(f(dst, ps[J.bank(*key)][rows, lo:lo + cols], func), J.free(*key))

            def pair(buf, q):
                return buf[:, 2 * q:2 * q + 2, :].rearrange("p a b -> p (a b)")

            def exps(stage, i, segs, buf, sink=None):
                act.wait_ge(*c.at("max_ready", stage, i))
                for t, col, nk in segs:
                    x = logit[:, buf, col:col + nk * P]
                    do(f(x, x, ACT.Exp, bias=smx[:, buf, t:t + 1], accum_out=smx[:, buf, 2 + t:3 + t]),
                       c.sig("exp_done", stage, i) if t == 1 and sink is None else None)
                if sink is not None:
                    for t in range(NT):
                        do(f(smx[:, buf, 6 + t:7 + t], sink, ACT.Exp, bias=smx[:, buf, t:t + 1]),
                           c.sig("exp_done", stage, i) if t == 1 else None)

            def probs_T(stage, h, segs, prev):
                if h >= 2:
                    act.wait_ge(*J.full(prev, h - 2))
                copy(probT[:, h % 2, 0:P * sum(nk for _, _, nk in segs)], (stage + "T", h), P * sum(nk for _, _, nk in segs))

            def head_rms(stage, raws):
                for q, raw in enumerate(raws):
                    if q >= 2:
                        act.wait_ge(*J.full(stage, q - 2))
                    do(f(logit[:, q % 2, :], raw, ACT.Square), c.sig("squares", stage, q))
                    act.wait_ge(*J.full(stage, q))
                    if q >= 2:
                        act.wait_ge(*c.at("head_normed", stage, q - 2))
                    do(f(rsw[:, q % 2, :], ps[J.bank(stage, q)][:, :], ACT.Sqrt, scale=1.0 / H64, bias=C("eps")[:, 0:1]),
                       J.free(stage, q))

            def columns_of(g):
                copy(vcol[:, g, 0:vload[g][0]], ("vec", g), vload[g][0])

            act.wait_ge(*J.emptied("vec", 0))
            do(f(ccol[:, :], vcol[:, vat["c_2"][0], vat["c_2"][1]:vat["c_2"][1] + KC], ACT.Silu), c.sig("c_act"))
            for q in range(4):
                copy(pair(qT, q), ("b1p", q))
            for h in range(HEADS1):
                copy(relrep[:, h, 0:511], ("rel", h), 511)
            act.dma_start(relrow, relrep[:, :, 0:511]).then_inc(c.sem("relrow_out"), 16)
            act.wait_ge(c.sem("relrow_out"), 16)
            for first, lo, n in ((255, 0, P), (127, P, S)):
                act.dma_start(relbias[:, :, lo:lo + n],
                              bass.AP(tensor=relrow.tensor, offset=first, ap=[[HEADS1 * 511 - 1, P], [511, HEADS1], [1, n]]))\
                    .then_inc(c.sem("relbias_in"), 16)
            for g in range(1, 4):
                columns_of(g)
            for q in range(4):
                copy(pair(kT, q), ("b1p", 4 + q))
            for i in range(HEADS1 + 3):
                if i < HEADS1:
                    exps("b1", i, T384, i % 4)
                if i in B1_BETWEEN:
                    for q in (B1_BETWEEN[i] // 256, B1_BETWEEN[i] // 256 + 1):
                        if q < 16:
                            copy(pair(mix1, q - 12), ("b1p", q), func=ACT.Silu)
                        elif q < 20:
                            copy(pair(xmT, q - 16), ("b1p", q))
                        else:
                            copy(pair(mix1, q - 20 + 4), ("b1p", q), func=ACT.Silu)
                if 2 <= i < HEADS1 + 2:
                    probs_T("b1", i - 2, T384, "b1O")
            for k in range(KC):
                act.wait_ge(*c.at("conv", k))
                do(f(xcT[:, k, :], xcT[:, k, :], ACT.Silu), c.sig("conv_ready", k))
            for key, dst in (("qm", qmT), ("km", kmT)):
                for q in range(4):
                    copy(pair(dst, q), (key, q))
            act.wait_ge(*c.at("gates_in"))
            do(f(lg[:, :, 0:4], gl[:, :, 4:8], ACT.Abs))
            do(f(lg[:, :, 4:8], lg[:, :, 0:4], ACT.Exp, scale=-1.0))
            do(f(lg[:, :, 8:12], lg[:, :, 4:8], ACT.Ln, bias=ones[:, 0:1]), c.sig("softplus", "gates"))
            for i in range(MH + 2):
                if i < MH:
                    act.wait_ge(*c.at("max_ready", "m", i))
                    for t, col, nk in T384:
                        x = logit[:, i % 4, col:col + nk * P]
                        do(f(x, x, ACT.Exp, bias=mcol[:, i, 2 + t:3 + t]))
                    do(f(mcol[:, i, 6:8], mcol[:, i, 4:6], ACT.Exp, scale=-1.0), c.sig("exp_done", "m", i))
                if 1 <= i <= MH:
                    probs_T("m", i - 1, T384, "mO")
            act.wait_ge(*c.at("piece_used", "b1", 7))
            for t in range(NT):
                for h in range(2):
                    do(f(junk[:, 0:512], acc[2 * t + h][:, :], ACT.Square, accum_out=st[:, 4 + 2 * t + h:5 + 2 * t + h]),
                       c.sig("squares", "post1") if t + h == 2 else None)
            if upto < 2:
                return
            for q in range(4):
                copy(qraw[:, q, :], ("dqk", q))
                if q == 3:
                    for t in range(NT):
                        copy(vd[:, t, :], ("b2v", 1024, t))
            for q in range(6, 10):
                copy(pair(sqT if q < 8 else skT, q % 2), ("sqk", q))
            for t in range(NT):
                copy(sv[:, t, :], ("b2v", 2560, t))
            for i in range(2):
                act.wait_ge(*c.at("lambda_dots"))
                do(f(lam[:, i:i + 1], lam[:, i:i + 1], ACT.Exp), c.sig("lambda_exp") if i else None)
            for i in range(NDIFF + 1):
                if i < NDIFF:
                    exps("d", 2 * i, T384, 2 * i % 4)
                    exps("d", 2 * i + 1, T384, (2 * i + 1) % 4)
                if i >= 1:
                    probs_T("dd", i - 1, T384, "ddO")
            for i in range(NSB // 2 + 2):
                if i >= 2:
                    for h in (2 * i - 4, 2 * i - 3):
                        act.wait_ge(*J.emptied("sbs", h))
                    x = sbw[(i - 2) % 3][:, :, 384:768]
                    do(f(x, x, ACT.Exp), c.sig("exp_done", "sb", i - 2))
                if i < NSB // 2:
                    for h in (2 * i, 2 * i + 1):
                        act.wait_ge(*J.emptied("sbz", h))
                    z, x = sbw[i % 3][:, :, 0:384], sbw[i % 3][:, :, 384:768]
                    do(f(x, z, ACT.Abs))
                    do(f(x, x, ACT.Exp, scale=-1.0))
                    do(f(x, x, ACT.Ln, bias=ones[:, 0:1]), c.sig("softplus", i))
                if i >= 2:
                    for h in (2 * i - 4, 2 * i - 3):
                        m = 64 * (h % 2)
                        copy(mix2[m:m + 64, 4 + h // 2, :], ("sbo", h), S, rows=slice(m, m + 64))
            for k in range(16):
                act.wait_ge(*J.full("ff1", k))
                do(f(pair(fT, k), ps[J.bank("ff1", k)][:, :], ACT.Relu), J.free("ff1", k))
            if upto < 3:
                return

            copy(pair(memkT, 0), ("memk", 0))
            copy(memv[:, :, :].rearrange("p a b -> p (a b)"), ("memv",))
            head_rms("memk2", [pair(memkT, 0)])

            def memory(stage):
                for i in range(MEMH + 3):
                    if i < MEMH:
                        exps(stage, i, T512, i % 4)
                    if 2 <= i < MEMH + 2:
                        probs_T(stage, i - 2, T512, stage + "O")
                    if i >= 3:
                        m, h = 64 * ((i - 3) % 2), i - 3
                        copy(mix3[m:m + 64, 6 + h // 2, :], (stage + "O", h), S, rows=slice(m, m + 64))

            def taps(first, end):
                for n in range(first, end):
                    if n >= DIAGS:
                        act.wait_ge(*c.at("tap_used", n - DIAGS))
                    col = vec("cv_dw_w_3", CC * (CONVW - 1 - n % CONVW) + CONV_PE[n // CONVW])
                    go(f(diag[:, n % DIAGS, :], ident, ACT.Copy, scale=col), c.sig("tap_ready", n))

            act.wait_ge(*c.at("normed", "cv"))
            taps(0, DIAGS)
            for g in range(3):
                key = ("cvp", 3 + g)
                act.wait_ge(*J.full(*key))
                for j in range(2):
                    do(f(sg3[:, g, j * S:(j + 1) * S], ps[J.bank(*key)][:, j * S:(j + 1) * S], ACT.Sigmoid,
                         bias=vec("cv_b_glu_3", CC + 2 * g + j)), J.free(*key) if j else None)
            copy(pair(mqT, 0), ("cvp", 6))
            head_rms("cvq2", [pair(mqT, 0)])
            taps(DIAGS, CONVW * len(CONV_PE))
            memory("cm")
            act.wait_ge(*c.at("centred"))
            flat = lambda v: v.rearrange("p a b -> p (a b)")
            do(f(flat(sq3), flat(cT), ACT.Square), c.sig("cvar_in"))
            act.wait_ge(*J.full("cvar"))
            do(f(lnw[:, 1, :], ps[J.bank("cvar")][:, 0:S], ACT.Sqrt, scale=1.0 / CONV, bias=C("eps")[:, 1:2]), J.free("cvar"))
            act.wait_ge(*c.at("conv_normed"))
            for k in range(CC):
                do(f(mix3[:, k, :], cT[:, k, :], ACT.Silu, scale=vec("cv_ln_g_3", k), bias=vec("cv_ln_b_3", k)),
                   c.sig("conv_act", k))
            for g in range(11):
                if g >= 4:
                    act.wait_ge(*J.emptied("fu", g - 4))
                copy(sg3[:, g % 4, :], ("fg", g), func=ACT.Silu)
            if upto < 4:
                return
            for g in range(2):
                copy(flat(swq[:, 3 * g:3 * g + 2, :]), ("swp", 2 * g))
                key = ("swp", 2 * g + 1)
                act.wait_ge(*J.full(*key))
                do(f(swq[:, 3 * g + 2, :], ps[J.bank(*key)][:, 0:S], ACT.Copy))
                do(f(swk[:, g, :], ps[J.bank(*key)][:, S:2 * S], ACT.Copy), J.free(*key))
            copy(flat(swv), ("swv",))
            copy(pair(mqT, 0), ("swm", 0))
            head_rms("swn", [pair(swq, 0), pair(swq, 1), pair(swq, 2), pair(swk, 0), pair(mqT, 0)])
            for i in range(SWAH + 3):
                if i < SWAH:
                    exps("sw", i, T384, i % 4, sinkb[:, i:i + 1])
                if 2 <= i < SWAH + 2:
                    probs_T("sw", i - 2, T384, "swO")
                if i >= 3:
                    m, h = 64 * ((i - 3) % 2), i - 3
                    copy(mix3[m:m + 64, h // 2, :], ("swO", h), S, rows=slice(m, m + 64))
            memory("sm")
            if upto < 5:
                return

            act.wait_ge(*c.at("router_max"))
            for t in range(NT):
                do(f(rt[:, 2, t, :], rt[:, 0, t, :], ACT.Exp, bias=xtr[:, t, 0:1]), c.sig("exp_done", "router") if t else None)

            act.wait_ge(*c.at("rounds_ready"))
            n_rounds = act.value_load(ridi[0:1, 15:16], min_val=NEXP, max_val=NROUND)
            with act.Fori(0, n_rounds) as r:
                c.enter(r)
                n, at_ = FFE // 512, [0]

                def high(upto):
                    for hp in range(at_[0], upto):
                        if hp % 2 == 0:
                            act.wait_ge(*W.landed(ROUND_PIECES[hp // 2]))
                        act.wait_ge(*W.half_wait(hp))
                        s, lo = W.place(ROUND_PIECES[hp // 2]), (hp % 2) * (PIECE // 2)
                        go(f(w_hi[:, hp % SPLITS, :], ring[:, s, lo:lo + PIECE // 2], ACT.Copy), c.sig("hi_ready", hp))
                    at_[0] = upto

                high(SPLITS)
                for g in range(n + 1):
                    if g < n:
                        high(8 * g + 9)
                        if g >= 2:
                            act.wait_ge(*J.emptied("xu", g - 2))
                        copy(esg[:, g % 2, :], ("xg", g), func=ACT.Silu)
                        high(8 * g + 13)
                    if g == 0:
                        copy(pgT[:, :], ("pgT",), S)
                    if g >= 1:
                        act.wait_ge(*J.full("xt", g - 1))
                        do(f(flat(act_hi[:, 4 * (g - 1):4 * g, :]), ps[J.bank("xt", g - 1)][:, :], ACT.Copy), c.sig("act_high", g - 1))
                high(HALVES)
                act.wait_ge(*c.at("piece_used", "xdown", FFE // P - 1))
                do(f(ey[:, 0:512], acc[0][:, :], ACT.Copy), c.sig("expert_out", 0))
                c.leave()
        @block.vector
        def _(dve):
            v = nc.vector

            def do(ins, s=None):
                s = s or c.sig("vec_step")
                ins.then_inc(s.sem, 1)
                dve.wait_ge(s.sem, s.val)

            def rep(ap, n):
                return bass.AP(tensor=ap.tensor, offset=ap.offset, ap=[ap.ap[0], [0, n], ap.ap[1]])

            def spread(ap, n):
                return bass.AP(tensor=ap.tensor, offset=ap.offset, ap=[ap.ap[0], ap.ap[1], [0, n]])

            def bank(*key):
                dve.wait_ge(*J.full(*key))
                return ps[J.bank(*key)]

            def pair(buf, q):
                return buf[:, 2 * q:2 * q + 2, :].rearrange("p a b -> p (a b)")

            def flat(x):
                return x.rearrange("p a b -> p (a b)")

            def norm(stage, src, dst=nrm):
                s0 = 4 * NORMS.index(stage)
                for t in range(NT):
                    do(v.tensor_tensor_reduce(junk[:, :], src[:, t, :], src[:, t, :], 1.0, 0.0, ALU.mult, ALU.add,
                                              st[:, s0 + t:s0 + t + 1]), c.sig("squares_v", stage) if t else None)
                dve.wait_ge(*c.at("rstd", stage))
                for t in range(NT):
                    do(v.tensor_scalar(dst[:, t, :], src[:, t, :], st[:, s0 + 2 + t:s0 + 3 + t], None, ALU.mult),
                       c.sig("normed", stage) if t else None)

            def gains(stage, gain, shift=None, n=KC, dst=hT, k0=0):
                for q in range(n // 2):
                    b = bank(stage, q)
                    for j in range(2):
                        k = 2 * q + j
                        do(v.tensor_scalar(dst[:, k0 + k, :], b[:, j * S:(j + 1) * S], gain(k), shift(k) if shift else None,
                                           ALU.mult, ALU.add if shift else ALU.bypass), J.free(stage, q) if j else None)

            def logits(stage, i, segs, buf, scale, bias, slope=None, sink=None):
                b = bank(stage + "S", i)
                n = P * sum(nk for _, _, nk in segs)
                x = logit[:, buf, 0:n]
                if bias is None:
                    do(v.tensor_scalar(x, b[:, 0:n], scale, None, ALU.mult), J.free(stage + "S", i))
                else:
                    do(v.scalar_tensor_tensor(x, b[:, 0:n], scale, bias, ALU.mult, ALU.add), J.free(stage + "S", i))
                if slope is not None:
                    do(v.scalar_tensor_tensor(x, C("dist"), slope, x, ALU.mult, ALU.add))
                for t, col, nk in segs:
                    do(v.tensor_reduce(smx[:, buf, t:t + 1], logit[:, buf, col:col + nk * P], AX, ALU.max, negate=True),
                       c.sig("max_ready", stage, i) if t and sink is None else None)
                if sink is not None:
                    do(v.tensor_scalar(smx[:, buf, 0:2], smx[:, buf, 0:2], sink, None, ALU.min), c.sig("max_ready", stage, i))

            def probs(stage, i, segs, buf, sink=False):
                dve.wait_ge(*c.at("exp_done", stage, i))
                if sink:
                    do(v.tensor_tensor(smx[:, buf, 2:4], smx[:, buf, 2:4], smx[:, buf, 6:8], ALU.add))
                do(v.reciprocal(smx[:, buf, 4:6], smx[:, buf, 2:4]))
                for t, col, nk in segs:
                    x = logit[:, buf, col:col + nk * P]
                    do(v.tensor_scalar(x, x, smx[:, buf, 4 + t:5 + t], None, ALU.mult), c.sig("probs_ready", stage, i) if t else None)

            def head_normed(stage, raws, gain):
                for q, raw in enumerate(raws):
                    dve.wait_ge(*J.emptied(stage, q))
                    do(v.reciprocal(rsw[:, q % 2, :], rsw[:, q % 2, :]))
                    do(v.scalar_tensor_tensor(raw, raw, gain[q], rsw[:, q % 2, :], ALU.mult, ALU.mult),
                       c.sig("head_normed", stage, q))

            def add_sums(stage, last, gate=None):
                dve.wait_ge(*c.at("piece_used", *last))
                for t in range(NT):
                    for h in range(2):
                        x, a = xres[:, t, h * 512:(h + 1) * 512], acc[2 * t + h][:, :]
                        if gate is not None:
                            do(v.tensor_tensor(junk[:, 0:512], a, gate[:, h * 512:(h + 1) * 512], ALU.mult))
                            a = junk[:, 0:512]
                        do(v.tensor_tensor(x, x, a, ALU.add))

            do(v.memset(half_c[:, :], -0.5), c.sig("exponent"))
            dve.wait_ge(c.sem("x_in"), 16)
            norm("pre", xres)
            def ada_sum(*places):
                for x in places:
                    if x >= 4:
                        dve.wait_ge(*J.full("ada", ADA[x - 4]))
                    for h in range(2):
                        key, y = ("ada", 512 * ADA[x], h), adasum[x % 4]
                        dve.wait_ge(*W.ready(key))
                        w = ring[:, W.place(key), :].rearrange("p (k n) -> p k n", k=4)
                        for k in range(4):
                            cond, s = ccol[:, 4 * h + k:4 * h + k + 1], c.sig("ada_sum", x, h) if k == 3 else None
                            if h + k == 0:
                                do(v.tensor_scalar(y, w[:, k, :], cond, None, ALU.mult))
                            else:
                                do(v.scalar_tensor_tensor(y, w[:, k, :], cond, y, ALU.mult, ALU.add), s)
                        W.free(key, s)

            def ada(*places):
                ga, ra = vat["ada_b_2"]
                for g in (ADA[x] for x in places):
                    b, part, half = bank("ada", g), g // 2, g % 2
                    if part in (2, 5):
                        if half == 0:
                            dve.wait_ge(c.sem("gates_bias_in"), 32)
                        x = (gm if part == 2 else gf)[:, half * 512:(half + 1) * 512]
                        do(v.tensor_tensor(x, x, b[:, :], ALU.add), J.free("ada", g))
                    else:
                        o = 8 * {0: 0, 1: 1, 3: 2, 4: 3}[part] + 4 * half
                        do(v.tensor_tensor(modc[:, o:o + 4], b[:, 0:4], vcol[:, ga, ra + 4 * g:ra + 4 * g + 4], ALU.add), J.free("ada", g))

            def values(col):
                for t in range(NT):
                    do(v.tensor_copy(vt[:, t, col - 2048:col - 2048 + 512], bank("b1v", col, t)[:, :]), J.free("b1v", col, t))

            do(v.tensor_copy(vcol[:, 0, 0:vload[0][0]], bank("vec", 0)[:, 0:vload[0][0]]), J.free("vec", 0))
            gains("pre", lambda k: vec("g_pre", k))
            dve.wait_ge(*c.at("c_act"))
            ada_sum(0)
            do(v.memset(relb[32:33, :], 1.0))
            dve.wait_ge(c.sem("rel_in"), 16)
            do(v.tensor_copy(relw[0:33, :, :], spread(relb[0:33, :], P)), c.sig("rel_wide"))
            ada_sum(1)
            ada(0, 1)
            ada_sum(2)
            ada(2)
            ada_sum(3, 4)
            ada(3, 4)
            ada_sum(5, 6)
            values(2048)
            ada(5, 6)
            ada_sum(7)
            values(2560)
            ada(7)
            dve.wait_ge(c.sem("wraw_in"), 48)
            dve.wait_ge(c.sem("consts_in"), 16)
            for m in range(24):
                w = wraw[:, m, :]
                do(v.tensor_tensor(bd[:, m, :].rearrange("p (n o) -> p n o", o=4), rep(w, 32),
                                   C("block4").rearrange("p (n o) -> p n o", o=4), ALU.mult), c.sig("bd_ready") if m == 23 else None)
            dve.wait_ge(c.sem("relbias_in"), 32)
            for i in range(HEADS1 + 3):
                if i < HEADS1:
                    logits("b1", i, T384, i % 4, DH1 ** -0.5, relbias[:, i, :])
                if 1 <= i <= HEADS1:
                    probs("b1", i - 1, T384, (i - 1) % 4)
                if i >= 3:
                    h = i - 3
                    dve.wait_ge(*J.emptied("b1p", 12 + h // 2))
                    do(v.tensor_tensor(mix1[:, h, :], mix1[:, h, :], bank("b1O", h)[:, 0:S], ALU.mult), J.free("b1O", h))
            for k in range(KC):
                dve.wait_ge(*J.emptied("b1p", 16 + k // 2))
                y, x = xcT[:, k, :], xmT[:, k, :]
                do(v.tensor_scalar(y, x, vec("conv_w", 24 + k), vec("conv_b", k), ALU.mult, ALU.add))
                for d in (1, 2, 3):
                    do(v.scalar_tensor_tensor(y[:, d:S], x[:, 0:S - d], vec("conv_w", 8 * (3 - d) + k), y[:, d:S], ALU.mult, ALU.add),
                       c.sig("conv", k) if d == 3 else None)
            dve.wait_ge(*J.full("b1p", 23))
            for k in range(KC):
                do(v.tensor_scalar(cact[:, k, :], ones, ccol[:, k:k + 1], None, ALU.mult), c.sig("c_ready") if k == KC - 1 else None)
            for q in range(4):
                do(v.tensor_copy(pair(vmT, q), bank("vmT", q)[:, :]), J.free("vmT", q))
            for t in range(NT):
                for q in range(2):
                    do(v.tensor_copy(vm[:, t, q * 512:(q + 1) * 512], bank("vm", t, q)[:, :]), J.free("vm", t, q))
            ada(8)
            do(v.tensor_copy(flat(gl[:, :, :]), bank("gates")[:, 0:16]), J.free("gates"))
            go = c.sig("gates_in")
            do(v.tensor_scalar(lg[:, :, 12:16], gl[:, :, 4:8], 0.0, None, ALU.min), go)
            dve.wait_ge(*c.at("softplus", "gates"))
            do(v.tensor_tensor(gl[:, :, 4:8], lg[:, :, 12:16], lg[:, :, 8:12], ALU.subtract), c.sig("loggates"))
            b = bank("Frow")
            do(v.tensor_copy(aT[0:MH, S:2 * S], b[0:MH, 0:S]))
            do(v.tensor_tensor(aT[0:MH, 0:S], b[0:MH, S:2 * S], aT[0:MH, S:2 * S], ALU.subtract), J.free("Frow"))
            do(v.tensor_copy(flat(fcol[:, :, :]), bank("Fcol")[:, 0:8]), J.free("Fcol"))
            do(v.tensor_copy(mcol[:, 0, 0:1], ones[:, 0:1]), c.sig("a_rows"))
            stats = cmp[:, 0, :]
            moments = cmp[:, 1, :]
            for i in range(MH + 2):
                if i < MH:
                    x = logit[:, i % 4, 0:384]
                    do(v.tensor_tensor(x, bank("mA", i)[:, 0:384], C("causal"), ALU.add), J.free("mA", i))
                    for t, col, nk in T384:
                        do(v.tensor_reduce(mcol[:, i, t:t + 1], logit[:, i % 4, col:col + nk * P], AX, ALU.max))
                    do(v.tensor_scalar(mcol[:, i, 2:4], mcol[:, i, 0:2], 0.0, -1.0, ALU.max, ALU.mult))
                    do(v.tensor_tensor(mcol[:, i, 4:6], fcol[:, :, i], mcol[:, i, 2:4], ALU.subtract), c.sig("max_ready", "m", i))
                if 1 <= i <= MH:
                    h = i - 1
                    dve.wait_ge(*c.at("exp_done", "m", h))
                    b = bank("mS", h)
                    for t, col, nk in T384:
                        x = logit[:, h % 4, col:col + nk * P]
                        do(v.scalar_tensor_tensor(x, b[:, col:col + nk * P], MD ** -0.5, x, ALU.mult, ALU.mult,
                                                  accum_out=mcol[:, h, 8 + t:9 + t]), J.free("mS", h) if t else None)
                    m = mcol[:, h, :]
                    do(v.tensor_scalar(m[:, 10:12], m[:, 8:10], -1.0, None, ALU.mult), c.sig("probs_ready", "m", h))
                    do(v.tensor_tensor(m[:, 10:12], m[:, 8:10], m[:, 10:12], ALU.max))
                    do(v.tensor_tensor(m[:, 10:12], m[:, 10:12], m[:, 6:8], ALU.max))
                    do(v.reciprocal(m[:, 12:14], m[:, 10:12]))
                if i >= 2:
                    h = i - 2
                    b = bank("mO", h)
                    for t in range(NT):
                        x = nrm[:, t, h * MD:(h + 1) * MD]
                        do(v.tensor_scalar(x, b[:, t * S:(t + 1) * S], mcol[:, h, 12 + t:13 + t], None, ALU.mult),
                           J.free("mO", h) if t else None)
                        do(v.bn_stats(stats[:, 0:6], x))
                        do(v.bn_aggr(moments[:, 2 * (NT * h + t):2 * (NT * h + t) + 2], stats[:, 0:6]),
                           c.sig("moments") if h == MH - 1 and t else None)
            ada(9, 10, 11)
            for o, name in ((8, "mix_norm_g_2"), (24, "ffn_norm_g_2")):
                gg, rr = vat[name]
                do(v.scalar_tensor_tensor(modc[:, o:o + 8], modc[:, o:o + 8], 1.0, vcol[:, gg, rr:rr + 8], ALU.add, ALU.mult))
            dve.wait_ge(*c.at("rstd", "mlstm"))
            for h in range(MH):
                for t in range(NT):
                    x, j = nrm[:, t, h * MD:(h + 1) * MD], 2 * (NT * h + t)
                    do(v.tensor_scalar(x, x, moments[:, j:j + 1], moments[:, j + 1:j + 2], ALU.subtract, ALU.mult),
                       c.sig("normed", "mlstm") if h == MH - 1 and t else None)
            for q in range(4):
                b = bank("mlstm", q)
                for j in range(2):
                    k = 2 * q + j
                    x = junk[:, j * S:(j + 1) * S]
                    do(v.tensor_scalar(x, xcT[:, k, :], vec("skip", k), None, ALU.mult))
                    do(v.scalar_tensor_tensor(x, b[:, j * S:(j + 1) * S], vec("mh_norm", k), x, ALU.mult, ALU.add))
                    do(v.tensor_tensor(mix1[:, 8 + k, :], mix1[:, 8 + k, :], x, ALU.mult), J.free("mlstm", q) if j else None)
            dve.wait_ge(c.sem("wide_in"), 16)
            dve.wait_ge(*c.at("rstd", "post1"))
            for t in range(NT):
                for h in range(2):
                    cs = slice(h * 512, (h + 1) * 512)
                    do(v.scalar_tensor_tensor(nrm[:, t, cs], acc[2 * t + h][:, :], st[:, 40 + t:41 + t], wide[:, cs], ALU.mult, ALU.mult))
                    do(v.tensor_tensor(xres[:, t, cs], xres[:, t, cs], nrm[:, t, cs], ALU.add), c.sig("x_ready", 1) if t + h == 2 else None)

            if upto >= 2:
                norm("mix2", xres)
            if upto < 2:
                return
            dve.wait_ge(c.sem("small_in"), 80)
            for i in range(2):
                do(v.tensor_tensor_reduce(junk[:, 0:H64], lamv[:, 2 * i, :], lamv[:, 2 * i + 1, :], 1.0, 0.0, ALU.mult, ALU.add,
                                          lam[:, i:i + 1]), c.sig("lambda_dots") if i else None)
            gains("mix2", lambda k: modc[:, 8 + k:9 + k], lambda k: modc[:, k:k + 1])
            for q in range(4):
                dve.wait_ge(*J.emptied("dqk", q))
                x = qraw[:, q, :].rearrange("p (a b) -> p a b", a=2)
                a, d = (junk[:, o:o + 512].rearrange("p (a b) -> p a b", a=2) for o in (0, 512))
                do(v.tensor_tensor(a, x, rep(C("cos"), 2), ALU.mult))
                do(v.tensor_tensor(d, bank("rot", q)[:, :].rearrange("p (a b) -> p a b", a=2), rep(C("sin"), 2), ALU.mult), J.free("rot", q))
                do(v.tensor_tensor(pair(qdT if q < 2 else kdT, q % 2), junk[:, 0:512], junk[:, 512:1024], ALU.add), c.sig("roped", q))
            dve.wait_ge(*c.at("lambda_exp"))
            do(v.tensor_scalar(lam[:, 2:3], lam[:, 0:1], lam[:, 1:2], LAMBDA_INIT, ALU.subtract, ALU.add))
            do(v.tensor_scalar(lam[:, 2:3], lam[:, 2:3], -1.0, None, ALU.mult))
            for i in range(NDIFF + 2):
                if i < NDIFF:
                    for j in (2 * i, 2 * i + 1):
                        logits("d", j, T384, j % 4, H64 ** -0.5, C("chunk"))
                if 1 <= i <= NDIFF:
                    h = i - 1
                    p0, p1 = 2 * h % 4, (2 * h + 1) % 4
                    dve.wait_ge(*c.at("exp_done", "d", 2 * h + 1))
                    for p in (p0, p1):
                        do(v.reciprocal(smx[:, p, 4:6], smx[:, p, 2:4]))
                    do(v.tensor_scalar(smx[:, p1, 4:6], smx[:, p1, 4:6], lam[:, 2:3], None, ALU.mult))
                    for t, col, nk in T384:
                        x, y = logit[:, p0, col:col + nk * P], logit[:, p1, col:col + nk * P]
                        do(v.tensor_scalar(x, x, smx[:, p0, 4 + t:5 + t], None, ALU.mult))
                        do(v.scalar_tensor_tensor(x, y, smx[:, p1, 4 + t:5 + t], x, ALU.mult, ALU.add),
                           c.sig("probs_ready", "dd", h) if t else None)
                if i >= 2:
                    h = i - 2
                    do(v.tensor_copy(nrm[:, :, h * P:(h + 1) * P], bank("ddO", h)[:, 0:S].rearrange("p (t d) -> p t d", t=NT)),
                       J.free("ddO", h))
            for t in range(NT):
                do(v.tensor_tensor(junk[:, t * 512:(t + 1) * 512], nrm[:, t, 0:512], nrm[:, t, 0:512], ALU.mult))
            do(v.tensor_reduce(st[:, 44:52], junk[:, :].rearrange("p (a b) -> p a b", b=P), AX, ALU.add), c.sig("squares_v", "subln"))
            dve.wait_ge(*c.at("rstd", "subln"))
            for t in range(NT):
                x = nrm[:, t, 0:512].rearrange("p (a b) -> p a b", b=P)
                do(v.tensor_tensor(x, x, spread(st[:, 52 + 4 * t:56 + 4 * t], P), ALU.mult), c.sig("normed", "subln") if t else None)
            earlier = rep(C("earlier"), 2)
            for i in range(NSB // 2 + 2):
                if i >= 2:
                    for h in (2 * i - 4, 2 * i - 3):
                        w = sbw[(i - 2) % 3][:, h % 2, :]
                        do(v.tensor_tensor(w[:, 384:768], bank("sbs", h)[:, 0:384], w[:, 768:1152], ALU.add), J.free("sbs", h))
                for h in (2 * i, 2 * i + 1) if i < NSB // 2 else ():
                    do(v.tensor_scalar(sbw[i % 3][:, h % 2, 0:384], bank("sbz", h)[:, 0:384], H64 ** -0.5, None, ALU.mult), J.free("sbz", h))
                if 1 <= i <= NSB // 2:
                    z, sp_, lb = (sbw[(i - 1) % 3][:, :, o:o + 384] for o in (0, 384, 768))
                    dve.wait_ge(*c.at("softplus", i - 1))
                    do(v.scalar_tensor_tensor(lb, z, 0.0, sp_, ALU.min, ALU.subtract))
                    do(v.tensor_tensor(z, lb, z, ALU.subtract))
                    do(v.tensor_tensor(z, z, earlier, ALU.mult), c.sig("log1m_ready", i - 1))
                if i >= 2:
                    a = sbw[(i - 2) % 3][:, :, 384:768]
                    dve.wait_ge(*c.at("exp_done", "sb", i - 2))
                    do(v.tensor_tensor(a, a, earlier, ALU.mult), c.sig("sticks_ready", i - 2))
            for q in range(2):
                b = bank("subln", q)
                for j in range(2):
                    do(v.tensor_scalar(mix2[:, 2 * q + j, :], b[:, j * S:(j + 1) * S], vec("diff_subln_g_2"), 1.0 - LAMBDA_INIT,
                                       ALU.mult, ALU.mult), J.free("subln", q) if j else None)
            add_sums("b2", ("b2", 3), gm)
            norm("ffn2", xres)
            gains("ffn2", lambda k: modc[:, 24 + k:25 + k], lambda k: modc[:, 16 + k:17 + k])
            for k in range(16):
                dve.wait_ge(*J.emptied("ff1", k))
                do(v.tensor_tensor(pair(fT, k), pair(fT, k), pair(fT, k), ALU.mult), c.sig("relu2_ready", k))
            if upto >= 3:
                dve.wait_ge(c.sem("mem_in"), 16)
                norm("mem", memx)
                gains("mem", lambda k: vec("mem_norm_g_3", k))
            add_sums("ff", ("ff", 15), gf)
            norm("final2", xres)
            dve.wait_ge(c.sem("final_gain_in"), 16)
            for t in range(NT):
                do(v.tensor_tensor(xres[:, t, :], nrm[:, t, :], wide[:, :], ALU.mult), c.sig("x_ready", 2) if t else None)
            if upto < 3:
                return

            norm("cv", xres)
            gains("cv", lambda k: vec("cv_attn_norm_g_3", k))
            head_normed("memk2", [pair(memkT, 0)], [vec("mem_k_norm_g_3")])
            def glu(g):
                b = bank("cvp", g)
                dve.wait_ge(*J.emptied("cvp", 3 + g))
                for j in range(2):
                    do(v.scalar_tensor_tensor(uT[:, 2 * g + j, :], b[:, j * S:(j + 1) * S], vec("cv_b_glu_3", 2 * g + j),
                                              sg3[:, g, j * S:(j + 1) * S], ALU.add, ALU.mult), J.free("cvp", g) if j else None)

            def conv(k):
                y, x = cT[:, k, :], uT[:, k, :]
                do(v.tensor_scalar(y, x, vec("cv_dw_w_3", CC * (CONVW - 1) + k), vec("cv_dw_b_3", k), ALU.mult, ALU.add))
                for d in range(1, CONVW):
                    do(v.scalar_tensor_tensor(y[:, d:S], x[:, 0:S - d], vec("cv_dw_w_3", CC * (CONVW - 1 - d) + k), y[:, d:S],
                                              ALU.mult, ALU.add), c.sig("cmean_in", k) if d == CONVW - 1 else None)

            glu(0)
            conv(1)
            glu(1)
            glu(2)
            conv(2)
            conv(3)
            head_normed("cvq2", [pair(mqT, 0)], [vec("cv_memq_norm_g_3")])

            def memory(stage, between=lambda i: None):
                for i in range(MEMH + 1):
                    if i < MEMH:
                        logits(stage, i, T512, i % 4, H64 ** -0.5, None)
                    between(i)
                    if i >= 1:
                        probs(stage, i - 1, T512, (i - 1) % 4)

            memory("cm")
            for x, k in enumerate(CONV_PE):
                dve.wait_ge(*c.at("tap_used", (x + 1) * CONVW - 1))
                do(v.tensor_scalar(cT[:, k, :], acc[x][:, 0:S], vec("cv_dw_b_3", k), None, ALU.add), c.sig("cmean_in", k))
            do(v.tensor_scalar(lnw[:, 0, :], bank("cmean")[:, 0:S], 1.0 / CONV, None, ALU.mult), J.free("cmean"))
            do(v.tensor_tensor(cT[:, :, :], cT[:, :, :], rep(lnw[:, 0, :], CC), ALU.subtract), c.sig("centred"))
            dve.wait_ge(*J.emptied("cvar"))
            do(v.reciprocal(lnw[:, 1, :], lnw[:, 1, :]))
            do(v.tensor_tensor(cT[:, :, :], cT[:, :, :], rep(lnw[:, 1, :], CC), ALU.mult), c.sig("conv_normed"))
            add_sums("cv", ("cv", 2))
            norm("cvf", xres)
            gains("cvf", lambda k: vec("cv_ffn_norm_g_3", k))
            for g in range(11):
                b = bank("fu", g)
                dve.wait_ge(*J.emptied("fg", g))
                do(v.tensor_tensor(pair(actd, g), sg3[:, g % 4, :], b[:, :], ALU.mult), J.free("fu", g))
            add_sums("dn", ("dn", 10))
            do(v.tensor_copy(mcol[:, 0, 0:1], ones[:, 0:1]), c.sig("x_ready", 3))
            if upto < 4:
                return
            norm("sw", xres)
            gains("sw", lambda k: vec("sw_attn_norm_g_3", k))
            head_normed("swn", [pair(swq, 0), pair(swq, 1), pair(swq, 2), pair(swk, 0), pair(mqT, 0)],
                        [vec("sw_q_norm_g_3")] * 3 + [vec("sw_k_norm_g_3"), vec("sw_memq_norm_g_3")])
            do(v.tensor_scalar(fsink[:, :], sinkb[:, :], -1.0, None, ALU.mult))
            for i in range(SWAH + 1):
                if i < SWAH:
                    logits("sw", i, T384, i % 4, H64 ** -0.5, C("window"), -(2.0 ** (-8.0 * (i + 1) / SWAH)), fsink[:, i:i + 1])
                if i >= 1:
                    probs("sw", i - 1, T384, (i - 1) % 4, sink=True)
            memory("sm")
            add_sums("so", ("so", 3))
            do(v.tensor_copy(mcol[:, 0, 0:1], ones[:, 0:1]), c.sig("x_ready", 4))
            if upto < 5:
                return

            norm("moe", xres)
            gains("moe", lambda k: vec("sw_ffn_norm_g_3", k))
            do(v.tensor_copy(flat(rt[:, 0, :, :]), bank("router")[:, 0:16]), J.free("router"))
            for t in range(NT):
                l = rt[:, 0, t, :]
                above, below = (cmp[:, x, 0:64].rearrange("p (e j) -> p e j", e=8) for x in range(2))
                lower = C("lower").rearrange("p (e j) -> p e j", e=8)
                do(v.tensor_tensor(above, rep(l, 8), spread(l, 8), ALU.is_gt))
                do(v.tensor_tensor(below, rep(l, 8), spread(l, 8), ALU.is_equal))
                do(v.tensor_tensor(below, below, lower, ALU.mult))
                do(v.tensor_tensor(above, above, below, ALU.add))
                do(v.tensor_reduce(rt[:, 3, t, :], above, AX, ALU.add))
                do(v.tensor_scalar(rt[:, 1, t, :], rt[:, 3, t, :], 2.0, None, ALU.is_lt), c.sig("selected") if t else None)
            for t in range(NT):
                do(v.tensor_reduce(xtr[:, t, 0:1], rt[:, 0, t, :], AX, ALU.max, negate=True), c.sig("router_max") if t else None)
            dve.wait_ge(*c.at("exp_done", "router"))
            for t in range(NT):
                do(v.tensor_tensor_reduce(rt[:, 4, t, :], rt[:, 2, t, :], rt[:, 1, t, :], 1.0, 0.0, ALU.mult, ALU.add, xtr[:, t, 1:2]))
                do(v.reciprocal(xtr[:, t, 2:3], xtr[:, t, 1:2]))
            b = bank("slots")
            do(v.memset(pos[:, :, :, :].rearrange("p a t r -> p (a t r)"), 0.0))
            do(v.tensor_copy(pos[:, 0, :, 0:NEXP], b[:, 0:16].rearrange("p (t e) -> p t e", t=NT)))
            do(v.tensor_copy(xtr[:, 3, :], b[:, 16:24]), J.free("slots"))
            do(v.tensor_copy(pos[:, 1, :, 0:NEXP], rt[:, 1, :, :]))
            for t in range(NT):
                do(v.tensor_scalar(pos[:, 2, t, 0:NEXP], rt[:, 4, t, :], xtr[:, t, 2:3], None, ALU.mult))
            def dispatch(at_, key):
                for m, a in ((Pm, 1), (PG, 2)):
                    for t in range(NT):
                        do(v.tensor_scalar(m[:, t, :], C("iota"), pos[:, 0, t, at_], pos[:, a, t, at_], ALU.is_equal, ALU.mult),
                           c.sig("dispatch_ready", key) if a == 2 and t else None)

            gs, rs = vat["sw_ffn_norm_g_3"]

            def split(hi, lo, x, s):
                do(v.tensor_copy(hi, x))
                do(v.tensor_tensor(lo, x, hi.bitcast(F32), ALU.subtract), s)

            def gathered(key):
                for q in range(2):
                    b, x = bank("hg" + key, q), eact[:, 1, :]
                    do(v.tensor_tensor(x.rearrange("p (a b) -> p a b", a=4), b[:, :].rearrange("p (a b) -> p a b", a=4),
                                       spread(vcol[:, gs, rs + 4 * q:rs + 4 * q + 4], P), ALU.mult), J.free("hg" + key, q))
                    split(flat(hg_hi[:, 4 * q:4 * q + 4, :]), flat(hg_lo[:, 4 * q:4 * q + 4, :]), x,
                          c.sig("gathered", key, 1) if q else None)

            dispatch(slice(0, 1), "first")
            big, rank = xtr[:, 4, :], xtr[:, 5, :]
            before_ = cmp[:, 0, 0:64].rearrange("p (e j) -> p e j", e=8)
            do(v.tensor_scalar(big, xtr[:, 3, :], float(P), None, ALU.is_gt))
            do(v.tensor_tensor(before_, rep(big, 8), C("lower").rearrange("p (e j) -> p e j", e=8), ALU.mult))
            do(v.tensor_reduce(rank, before_, AX, ALU.add))
            do(v.memset(rid[:, :], 0.0))
            do(v.tensor_copy(rid[:, 0:8], C("eid")))
            do(v.tensor_reduce(rid[:, 15:16], big, AX, ALU.add))
            do(v.tensor_scalar(rid[:, 15:16], rid[:, 15:16], float(NEXP), None, ALU.add))
            one = xtr[:, 6, :]
            six = cmp[:, 1, 0:48].rearrange("p (a e) -> p a e", e=8)
            for x in range(EXTRA):
                do(v.tensor_scalar(one, rank, float(x), None, ALU.is_equal))
                do(v.tensor_tensor(one, one, big, ALU.mult))
                do(v.tensor_tensor_reduce(cmp[:, 0, 0:8], one, C("eid"), 1.0, 0.0, ALU.mult, ALU.add, rid[:, 8 + x:9 + x]))
                for a in range(3):
                    do(v.tensor_tensor(six[:, 2 * a:2 * a + 2, :], pos[:, a, :, 0:NEXP], rep(one, 2), ALU.mult))
                    do(v.tensor_reduce(pos[:, a, :, NEXP + x], six[:, 2 * a:2 * a + 2, :], AX, ALU.add))
                do(v.tensor_scalar(pos[:, 0, :, NEXP + x], pos[:, 0, :, NEXP + x], float(-P), None, ALU.add))
            do(v.tensor_copy(ridi[:, :], rid[:, :]), c.sig("rounds_ready"))
            gathered("first")
            s = c.sig("lo_ready", "credit", by=HALVES - 2 * len(POOL_PIECES))
            v.tensor_copy(xtr[:, 7, 1:2], ones[:, 0:1]).then_inc(s.sem, HALVES - 2 * len(POOL_PIECES))
            n_rounds = dve.value_load(ridi[0:1, 15:16], min_val=NEXP, max_val=NROUND)
            with dve.Fori(0, n_rounds) as r:
                c.enter(r)
                n, at_ = FFE // 512, [0]

                def low(upto):
                    for hp in (x for x in range(at_[0], upto) if x // 2 not in POOL_PIECES):
                        dve.wait_ge(*c.at("hi_ready", hp))
                        s, lo = W.place(ROUND_PIECES[hp // 2]), (hp % 2) * (PIECE // 2)
                        v.tensor_tensor(w_lo[:, hp % SPLITS, :], ring[:, s, lo:lo + PIECE // 2],
                                        w_hi[:, hp % SPLITS, :].bitcast(F32), ALU.subtract).then_inc(c.sig("lo_ready", hp).sem, 1)
                    at_[0] = upto

                low(SPLITS)
                for g in range(n + 1):
                    if g < n:
                        low(8 * g + 13)
                        b = bank("xu", g)
                        dve.wait_ge(*J.emptied("xg", g))
                        if g >= 2:
                            dve.wait_ge(*J.full("xt", g - 2))
                        do(v.tensor_tensor(eact[:, g % 2, :], esg[:, g % 2, :], b[:, :], ALU.mult), J.free("xu", g))
                    if g >= 1:
                        dve.wait_ge(*c.at("act_high", g - 1))
                        do(v.tensor_tensor(flat(act_lo[:, 4 * (g - 1):4 * g, :]), ps[J.bank("xt", g - 1)][:, :],
                                           flat(act_hi[:, 4 * (g - 1):4 * g, :]).bitcast(F32), ALU.subtract), J.free("xt", g - 1))
                    if g == 3:
                        dispatch(bass.ds(r + 1, 1), "next")
                    if g == n - 1:
                        gathered("next")
                low(HALVES)
                dve.wait_ge(*c.at("piece_used", "xdown", FFE // P - 1))
                do(v.tensor_copy(ey[:, 512:1024], acc[1][:, :]), c.sig("expert_out1", 0))
                for t in range(NT):
                    for h in range(2):
                        x = xres[:, t, h * 512:(h + 1) * 512]
                        do(v.tensor_tensor(x, x, bank("xs", t, h)[:, :], ALU.add), J.free("xs", t, h))
                c.leave()
            do(v.tensor_copy(mcol[:, 0, 0:1], ones[:, 0:1]), c.sig("x_ready", 5))

        @block.gpsimd
        def _(pool):
            g = nc.gpsimd

            def do(ins, s=None):
                s = s or c.sig("pool_step")
                ins.then_inc(s.sem, 1)
                pool.wait_ge(s.sem, s.val)

            def rstd(stage, src, dst, n, width, eps=RMS_EPS):
                do(g.tensor_scalar(dst, src, 1.0 / width, eps, ALU.mult, ALU.add))
                do(g.tensor_tensor(dst, dst, half_c[:, 0:n], ALU.pow), c.sig("rstd", stage))

            def norm(stage):
                s0 = 4 * NORMS.index(stage)
                pool.wait_ge(*c.at("squares_v", stage))
                rstd(stage, st[:, s0:s0 + 2], st[:, s0 + 2:s0 + 4], NT, D)

            pool.wait_ge(*c.at("exponent"))
            norm("pre")
            pool.wait_ge(*J.full("vm", 1, 1))
            for dst, col in ((gm, 2 * D), (gf, 5 * D)):
                pool.dma_start(dst, everywhere(A["ada_b_2"][:, col:col + D], D)).then_inc(c.sem("gates_bias_in"), 16)
            pool.wait_ge(*c.at("moments"))
            var = cmp[:, 1, 1:1 + 4 * MH:2]
            do(g.tensor_scalar(var, var, LN_EPS, None, ALU.add))
            do(g.tensor_tensor(var, var, half_c[:, 0:2 * MH], ALU.pow), c.sig("rstd", "mlstm"))
            pool.wait_ge(*c.at("squares", "post1"))
            for t in range(NT):
                do(g.tensor_tensor(st[:, 4 + 2 * t:5 + 2 * t], st[:, 4 + 2 * t:5 + 2 * t], st[:, 5 + 2 * t:6 + 2 * t], ALU.add))
            rstd("post1", st[:, 4:8:2], st[:, 40:42], NT, D)
            if upto < 2:
                return
            norm("mix2")
            pool.wait_ge(*c.at("x_ready", 1))
            pool.dma_start(wide[:, :], everywhere(A["final_norm_g_2"], D)).then_inc(c.sem("final_gain_in"), 16)
            pool.wait_ge(*c.at("squares_v", "subln"))
            rstd("subln", st[:, 44:52], st[:, 52:60], 8, P)
            norm("ffn2")
            if upto >= 3:
                pool.dma_start(memx, A["mem_3"].rearrange("a (t p) d -> p (a t) d", p=P)).then_inc(c.sem("mem_in"), 16)
                norm("mem")
            norm("final2")
            if upto < 3:
                return
            norm("cv")
            for k in range(1):
                pool.wait_ge(*J.emptied("cvp", 0))
                y, x = cT[:, k, :], uT[:, k, :]
                do(g.tensor_scalar(y, x, vec("cv_dw_w_3", CC * (CONVW - 1) + k), vec("cv_dw_b_3", k), ALU.mult, ALU.add))
                for d in range(1, CONVW):
                    do(g.tensor_scalar(tap[:, d:S], x[:, 0:S - d], vec("cv_dw_w_3", CC * (CONVW - 1 - d) + k), None, ALU.mult))
                    do(g.tensor_tensor(y[:, d:S], y[:, d:S], tap[:, d:S], ALU.add), c.sig("conv_pool", k) if d == CONVW - 1 else None)
            norm("cvf")
            if upto < 4:
                return
            norm("sw")
            if upto < 5:
                return
            norm("moe")
            pool.wait_ge(*c.at("rounds_ready"))
            n_rounds = pool.value_load(ridi[0:1, 15:16], min_val=NEXP, max_val=NROUND)
            with pool.Fori(0, n_rounds) as r:
                c.enter(r)
                for i in POOL_PIECES:
                    for hp in (2 * i, 2 * i + 1):
                        pool.wait_ge(*c.at("hi_ready", hp))
                        lo = (hp % 2) * (PIECE // 2)
                        g.tensor_tensor(w_lo[:, hp % SPLITS, :], ring[:, W.place(ROUND_PIECES[i]), lo:lo + PIECE // 2],
                                        w_hi[:, hp % SPLITS, :].bitcast(F32), ALU.subtract).then_inc(c.sig("lo_ready_pool", hp).sem, 1)
                c.leave()

        del block
    return c, J, W


NORMS = ["pre", "post1", "mix2", "ffn2", "mem", "final2", "cv", "cvf", "sw", "moe"]
_INS = ["x", "rel_bias", "g_pre", "g_post", "w_in", "conv_w", "conv_b", "wq_m", "wk_m", "wv_m", "w_if", "b_if", "mh_norm",
        "skip", "w_out", "c_2", "ada_w_2", "ada_b_2", "mix_norm_g_2", "w_in_2", "lambda_q1_2", "lambda_k1_2",
        "lambda_q2_2", "lambda_k2_2", "diff_subln_g_2", "w_out_2", "ffn_norm_g_2", "w_ff1_2", "w_ff2_2",
        "final_norm_g_2", "mem_3", "mem_norm_g_3", "w_mem_kv_3", "mem_k_norm_g_3", "cv_attn_norm_g_3", "cv_w_in_3",
        "cv_b_glu_3", "cv_dw_w_3", "cv_dw_b_3", "cv_ln_g_3", "cv_ln_b_3", "cv_memq_norm_g_3", "cv_w_out_3",
        "cv_ffn_norm_g_3", "cv_w_gate_3", "cv_w_up_3", "cv_w_down_3", "sw_attn_norm_g_3", "sw_w_in_3", "sw_q_norm_g_3",
        "sw_k_norm_g_3", "sw_sinks_3", "sw_memq_norm_g_3", "sw_w_out_3", "sw_ffn_norm_g_3", "sw_router_3",
        "sw_we_gate_3", "sw_we_up_3", "sw_we_down_3"]


def build(core, inputs, upto=9):
    table, const_at = constants()
    known = None
    for _ in range(2):
        nc = core()
        arrays, A = {"consts": table}, {}
        for name in _INS:
            arrays[name] = np.ascontiguousarray(inputs[name])
        for name, a in arrays.items():
            A[name] = nc.dram_tensor(f"in_{name}", a.shape, F32, kind="ExternalInput").ap()
        out = nc.dram_tensor("out_dram", (1, S, D), F32, kind="ExternalOutput").ap()
        known = program(nc, A, out, const_at, known, upto)
    return nc, {f"in_{name}": a for name, a in arrays.items()}


def kernel(**inputs):
    import concourse.bacc as bacc
    from concourse.bass_utils import run_bass_kernel_spmd
    nc, arrays = build(lambda: bacc.Bacc("TRN2", target_bir_lowering=False, num_devices=1), inputs)
    r = run_bass_kernel_spmd(nc, [arrays], core_ids=[0])
    return r.results[0]["out_dram"]
```

```python
from contextlib import ExitStack

import numpy as np

import concourse.bass as bass
from concourse import mybir

F32 = mybir.dt.float32
F32R = mybir.dt.float32r
I32 = mybir.dt.int32
ALU = mybir.AluOpType
ACT = mybir.ActivationFunctionType
AX = mybir.AxisListType.X

P = 128
S = 256
NT = S // P
D = 1024
KC = D // P
HEADS1, DH1 = 8, 128
MH, MD = 4, 256
H64 = 64
NDIFF, NSB = 4, 8
FF2 = 4096
CONV, CONVW = 768, 31
CC = CONV // P
CONV_PE = (4, 5)
DIAGS = 16
MEMH = 4
SWAH, SWAKV = 12, 4
FFD = 2816
NEXP, FFE = 8, 3584
EXTRA = (2 * S) // (P + 1)
NROUND = NEXP + EXTRA
RING = 7
PIECE = 2048
NEG = -1e30
RMS_EPS, LN_EPS = 1e-6, 1e-5
LAMBDA_INIT = 0.2

ROUND_JOBS = 28
ROUND_PIECES = [(w, g, h) for g in range(FFE // 512) for w in ("xgate", "xup") for h in range(2)] \
    + [("xdown", k) for k in range(FFE // 256)]
HALVES = 2 * len(ROUND_PIECES)


def ffn_order(ups, down, n):
    return [p for g in range(n + 1) for p in [(w, g) for w in ups if g < n] + [(down, g - 1)] * (g > 0)]


FFN = {"ff": ffn_order(("ff1",), "ff2", FF2 // 256), "dn": ffn_order(("gate", "up"), "down", FFD // 256)}
POOL_PIECES = (0,)
SPLITS = 6
SPLIT_KEYS = [("w_in2", 512 * g, h) for g in range(6) for h in range(2)]
SPLIT_SLOTS = 3
B1_BETWEEN = {0: 3072, 1: 3584, 3: 4096, 5: 4608, 7: 5120, 9: 5632}
SW_BETWEEN = {8: 0, 12: 1}
ADA = [0, 1, 2, 3, 6, 7, 8, 9, 4, 5, 10, 11]
T384 = [(0, 0, 1), (1, 128, 2)]
T512 = [(0, 0, 2), (1, 256, 2)]


def constants():
    p = np.arange(P)[:, None]
    t = np.arange(S)[None, :]
    f = np.float32
    causal = np.concatenate([np.where(t[:, :P] <= p, 0, NEG), np.where(t <= p + P, 0, NEG)], 1)
    chunk = np.concatenate([np.where(t[:, :P] // 64 <= p // 64, 0, NEG), np.where(t // 64 <= (p + P) // 64, 0, NEG)], 1)
    d0, d1 = p - t[:, :P], p + P - t
    dist = np.concatenate([d0, d1], 1)
    window = np.where((dist >= 0) & (dist < 128), 0, NEG)
    inv = (1.0 / (f(10000.0) ** (np.arange(0, 64, 2, dtype=f) / f(64)))).astype(f)
    ang = (np.arange(S, dtype=f)[:, None] * inv[None, :]).astype(f)
    ang = np.concatenate([ang, ang], 1)
    cos, sin = np.cos(ang).T, np.sin(ang).T
    rot = np.zeros((P, P))
    for h in (0, 64):
        for i in range(32):
            rot[h + 32 + i, h + i] = -1.0
            rot[h + i, h + 32 + i] = 1.0
    n = np.arange(511) - 255
    d = np.maximum(-n, 0)
    nf = np.maximum(d, 1).astype(f)
    large = 16 + (np.log(nf / f(16)) / f(np.log(2048 / 16)) * f(16)).astype(np.int32)
    bucket = np.where(d < 16, d, np.minimum(large, 31))
    rel = np.zeros((P, 511))
    rel[bucket, np.arange(511)] = 1.0
    rel[:, n > 0] = 0.0
    rel[32, n > 0] = NEG
    e, j = np.arange(8)[:, None], np.arange(8)[None, :]
    hsel = np.zeros((P, MH, P))
    for h in range(MH):
        hsel[h, h] = 1.0
    parts = {
        "ident": np.eye(P), "ones": np.ones((P, P)),
        "upto": np.concatenate([p <= t, p + P <= t], 1), "before": np.concatenate([p < t, p + P < t], 1),
        "after": p > t[:, :P], "causal": causal, "chunk": chunk,
        "earlier": np.concatenate([p < t, p + P < t[:, P:]], 1), "dist": np.maximum(dist, 0), "window": window,
        "block4": np.repeat(p // 4 == np.arange(32)[None, :], 4, 1), "half": (p // 64) == (np.arange(P)[None, :] // 64),
        "rot": rot, "cos": np.tile(cos, (2, 1)), "sin": np.tile(sin, (2, 1)), "rel": rel, "hsel": hsel.reshape(P, -1),
        "iota": np.broadcast_to(np.arange(P)[None, :], (P, P)), "lower": np.broadcast_to((j < e).reshape(1, 64), (P, 64)),
        "eid": np.broadcast_to(np.arange(8)[None, :], (P, 8)), "slots": np.broadcast_to(np.arange(4)[None, :], (P, 4)),
        "eps": np.broadcast_to(np.array([[RMS_EPS, LN_EPS]]), (P, 2)),
    }
    at, out, n = {}, [], 0
    for k, a in parts.items():
        at[k] = (n, n + a.shape[1])
        n += a.shape[1]
        out.append(np.asarray(a, f))
    return np.ascontiguousarray(np.concatenate(out, 1)), at


class Signal:
    def __init__(self, name, sem, val, base):
        self.name, self.sem, self.val, self.base = name, sem, val, base


class Count:

    def __init__(self, known=None):
        self.known, self.seen, self.n, self.sems = known, {}, {}, {}
        self.loop, self.start, self.per = None, {}, {}

    def sem(self, name):
        if name not in self.sems:
            self.sems[name] = self.make(name)
        return self.sems[name]

    def enter(self, r):
        self.loop, self.start = r, dict(self.n)

    def leave(self):
        for b in range(4):
            self.per[f"filled{b}"] = self.per[f"drained{b}"] = ROUND_JOBS // 4
        for k, v in self.n.items():
            if v != self.start.get(k, 0) and k not in self.per:
                self.per[k] = v - self.start.get(k, 0)
        self.loop = None

    def value(self, name, v):
        per = self.known.per.get(name, 0) if self.known else 0
        return v if self.loop is None or per == 0 else self.loop * per + v

    def sig(self, name, *key, by=1):
        self.n[name] = self.n.get(name, 0) + by
        self.seen[(name,) + key] = self.n[name]
        return Signal(name, self.sem(name), self.value(name, self.n[name]), self.n[name])

    def at(self, name, *key):
        v = self.known.seen[(name,) + key] if self.known else 1
        return self.sem(name), self.value(name, v)

    def before(self, name, *key):
        v = self.known.seen[(name,) + key] - self.known.per[name] if self.known else 1
        return self.sem(name), self.value(name, v)


class Jobs:

    def __init__(self, count, known=None):
        self.c, self.known, self.n, self.seen = count, known, 0, {}

    def number(self, *key):
        return self.known.seen[key] if self.known else self.seen.get(key, 0)

    def bank(self, *key):
        return self.number(*key) % 4

    def fill(self, pe, *key):
        n = self.n
        self.seen[key] = n
        self.n += 1
        if n >= 4:
            name = f"drained{n % 4}"
            pe.wait_ge(self.c.sem(name), self.c.value(name, n // 4))
        return n % 4

    def filled(self, *key):
        n = self.number(*key)
        name = f"filled{n % 4}"
        self.c.n[name] = max(self.c.n.get(name, 0), n // 4 + 1)
        return Signal(name, self.c.sem(name), self.c.value(name, n // 4 + 1), n // 4 + 1)

    def full(self, *key):
        n = self.number(*key)
        name = f"filled{n % 4}"
        return self.c.sem(name), self.c.value(name, n // 4 + 1)

    def free(self, *key):
        n = self.number(*key)
        name = f"drained{n % 4}"
        self.c.n[name] = max(self.c.n.get(name, 0), n // 4 + 1)
        return Signal(name, self.c.sem(name), self.c.value(name, n // 4 + 1), n // 4 + 1)

    def emptied(self, *key):
        n = self.number(*key)
        name = f"drained{n % 4}"
        return self.c.sem(name), self.c.value(name, n // 4 + 1)


class Stream:

    def __init__(self, count, known=None):
        self.c, self.known, self.n, self.number, self.freed = count, known, 0, {}, {}
        self.slot, self.landing, self.halves = [0] * RING, {}, {}

    def free(self, key, signal):
        n = self.number[key]
        self.freed[n] = (signal.name, signal.base)

    def half_free(self, hp, signal):
        self.halves[hp] = (signal.name, signal.base)

    def half_wait(self, hp):
        name, v = self.known.halves[(hp - SPLITS) % HALVES] if self.known else ("piece_used", 1)
        if hp < SPLITS and self.known:
            v -= self.c.known.per[name]
        return self.c.sem(name), self.c.value(name, v)

    def ffn_key(self, stage, p):
        name, g = FFN[stage][p]
        return (name, g) if name in ("ff2", "down") else (name, 256 * g, 0)

    def split_used(self, hp):
        name, v = self.known.halves["d", hp] if self.known else ("d_used", 1)
        return self.c.sem(name), v

    def ffn_used(self, stage, hp):
        name, v = self.known.halves[stage, hp] if self.known else ("ff_used", 1)
        return self.c.sem(name), v

    def place(self, key):
        return self.known.landing[key][0] if self.known else 0

    def landed(self, key):
        s, v = self.known.landing[key] if self.known else (0, 16)
        return self.c.sem(f"landed{s}"), self.c.loop * (16 * len(ROUND_PIECES) // RING) + v

    def low_name(self, hp):
        return "lo_ready_pool" if hp // 2 in POOL_PIECES else "lo_ready"

    def ready(self, key):
        s, v = self.known.landing[key] if self.known else (0, 16)
        return self.c.sem(f"landed{s}"), v


def program(nc, A, out, const_at, known=None, upto=9):
    c = Count(known[0] if known else None)
    J = Jobs(c, known[1] if known else None)
    W = Stream(c, known[2] if known else None)
    ctx = ExitStack()
    with ctx:
        c.make = lambda name: ctx.enter_context(nc.semaphore(name))
        if known:
            for name in known[0].sems:
                c.sem(name)

        def sb(name, *shape, dt=F32):
            return ctx.enter_context(nc.sbuf_tensor(name, [P, *shape], dt))

        consts = sb("consts", max(b for _, b in const_at.values()))

        def C(name, n=0):
            a, b = const_at[name]
            v = consts[:, a:b]
            return v.rearrange("p (a b) -> p a b", a=n) if n else v

        ident, ones = C("ident"), C("ones")
        ring = sb("ring", RING, PIECE)
        xres = sb("xres", NT, D)
        nrm = sb("nrm", NT, D)
        wide = sb("wide", D)
        vcol = sb("vcol", 4, P)
        st = sb("st", 64)
        smx = sb("smx", 6, 8)
        gl = sb("gl", 2, 8)
        lg = sb("lg", 2, 24)
        aT = sb("aT", 512)
        fcol = sb("fcol", 2, 4)
        mcol = sb("mcol", 4, 16)
        half_c = sb("half_c", 16)
        relb = sb("relb", HEADS1)
        brow = sb("brow", 8)
        sinkb = sb("sinkb", SWAH)
        fsink = sb("fsink", SWAH)
        lamv = sb("lamv", 4, H64)
        lam = sb("lam", 4)
        wif = sb("wif", 24, 8)
        wraw = sb("wraw", 24, 4)
        rw = sb("rw", KC, NEXP)
        ccol = sb("ccol", KC)
        modc = sb("modc", 32)
        rt = sb("rt", 6, NT, NEXP)
        cmp = sb("cmp", 2, NT * 64)
        pos = sb("pos", 3, NT, NROUND + 1)
        xtr = sb("xtr", 8, 8)
        rid = sb("rid", 16)
        ridi = sb("ridi", 16, dt=I32)
        with ExitStack() as phase:
            def sa(name, *shape):
                return phase.enter_context(nc.sbuf_tensor(name, [P, *shape], F32))

            arena = sa("arena", 16 * 1024)
            bd = sa("bd", 24, P)
            logit = sa("logit", 4, 512)
            probT = sa("probT", 2, 512)
            hT = sa("hT", KC, S)
            junk = sa("junk", D)
        with ExitStack() as phase:
            def sp_(name, *shape, dt=F32R):
                return phase.enter_context(nc.sbuf_tensor(name, [P, *shape], dt))

            sp_("units_0_to_5", 6 * 1024, dt=F32)
            d_lo = sp_("d_lo", SPLIT_SLOTS, PIECE // 2)
            sp_("units_9_to_15", 7 * 1024, dt=F32)
            d_hi = sp_("d_hi", SPLIT_SLOTS, PIECE // 2)
            dT_lo = sp_("dT_lo", KC, S)
            sp_("over_probT", 2, 512, dt=F32)
            dT_hi = sp_("dT_hi", KC, S)
        with ExitStack() as phase:
            def se(name, *shape, dt=F32):
                return phase.enter_context(nc.sbuf_tensor(name, [P, *shape], dt))

            w_hi, w_lo = se("w_hi", SPLITS, PIECE // 2, dt=F32R), se("w_lo", SPLITS, PIECE // 2, dt=F32R)
            with ExitStack() as inner:
                def sf(name, *shape, dt=F32R):
                    return inner.enter_context(nc.sbuf_tensor(name, [P, *shape], dt))

                sf("units_12_to_15", 4 * 1024, dt=F32)
                hT_hi, hT_lo = sf("hT_hi", KC, S), sf("hT_lo", KC, S)
                f_hi, f_lo = sf("f_hi", 4, 512), sf("f_lo", 4, 512)
            act_hi, act_lo = se("act_hi", 28, P, dt=F32R), se("act_lo", 28, P, dt=F32R)
            esg, ey = se("esg", 2, 512), se("ey", D)
            Pm, PG, pgT = se("Pm", NT, P), se("PG", NT, P), se("pgT", S)
            eact = se("eact", 2, 512)
            hg_hi, hg_lo = se("hg_hi", KC, P, dt=F32R), se("hg_lo", KC, P, dt=F32R)
        ps = [ctx.enter_context(nc.psum_tensor(f"bank{i}", [P, 512], F32)) for i in range(4)]
        acc = [ctx.enter_context(nc.psum_tensor(f"sum{i}", [P, 512], F32)) for i in range(4)]
        relrow = nc.dram_tensor("relrow", (P, HEADS1, 511), F32, kind="Internal").ap()

        def U(unit, *dims, off=0):
            n = int(np.prod(dims))
            v = arena[:, unit * 1024 + off:unit * 1024 + off + n]
            return v.rearrange("p (a b) -> p a b", a=dims[0]) if len(dims) == 2 else v

        relrep = U(0, HEADS1, 512)
        relw = logit[:, 0:2, :].rearrange("p a (b n) -> p (a b) n", n=P)
        mix1 = U(0, 16, S)
        relbias = U(4, HEADS1, 384)
        qT, kT, vt = U(8, 8, S), U(10, 8, S), U(12, NT, D)
        xmT, xcT, vm = U(14, 8, S), U(4, 8, S), U(6, NT, D)
        qmT, kmT, vmT = U(8, 8, S), U(10, 8, S), U(12, 8, S)
        vrows = [U(15, P, off=P * g) for g in range(4)]
        qraw = U(12, 4, 512)
        qdT, kdT, vd = U(0, 4, S), U(1, 4, S), U(2, NT, 512)
        sqT, skT, sv = U(3, 4, S), U(4, 4, S), U(5, NT, 512)
        mix2 = U(12, 8, S)
        dlogit = U(9, 6, 512)
        gm, gf = U(15, D), U(14, D)
        sbw = [U(6, 2, 1152), U(8, 2, 1152, off=256), U(0, 2, 1152)]
        adasum = [probT[:, 0, :], probT[:, 1, :], junk[:, 0:512], junk[:, 512:1024]]
        cact = hT[:, 0:4, :].rearrange("p a (b n) -> p (a b) n", n=P)

        def tile(stage):
            return dlogit if stage in ("d", "dd") else logit

        memkT, memv = U(15, 2, S), U(15, NT, 256, off=512)
        memx, memT = U(12, NT, D), U(12, KC, S)
        uT, cT = U(0, CC, S), U(2, CC, S)
        mqT, mq2 = U(4, 2, S), U(4, 512, off=512)
        sg3 = U(8, 4, 512)
        lnw, tap = U(10, 2, S), U(10, S, off=512)
        sq3 = U(5, CC, S)
        mix3 = U(13, 8, S)
        diag = U(12, DIAGS, P)
        ffa = {"ff": U(15, 2, 512), "dn": U(12, 2, 512)}
        hsq = U(7, 2, 512)
        rsw = U(11, 2, 512)
        swq, swk = U(0, 6, S), U(2, 2, S)
        swv = U(3, NT, 256)
        vgroups = [
            [("g_pre", 8), ("conv_w", 32), ("conv_b", 8), ("mh_norm", 8), ("skip", 8), ("mix_norm_g_2", 8),
             ("c_2", 8), ("ada_b_2", 48)],
            [("ffn_norm_g_2", 8), ("mem_norm_g_3", 8), ("cv_attn_norm_g_3", 8), ("cv_b_glu_3", 12), ("cv_dw_b_3", 6),
             ("cv_ln_g_3", 6), ("cv_ln_b_3", 6), ("cv_ffn_norm_g_3", 8), ("sw_attn_norm_g_3", 8),
             ("sw_ffn_norm_g_3", 8), ("diff_subln_g_2", 1), ("cv_memq_norm_g_3", 0), ("sw_q_norm_g_3", 0),
             ("sw_memq_norm_g_3", 0), ("mem_k_norm_g_3", 0), ("sw_k_norm_g_3", 0)],
            [("cv_dw_w_3", 96)], [("cv_dw_w_3", 90)],
        ]
        vat, vload = {}, []
        for g, group in enumerate(vgroups):
            r, loads = 0, []
            for name, n in group:
                src = A[name]
                src = src.rearrange({1: "a -> a", 2: "a b -> (a b)", 3: "a b c -> (a b c)"}[len(src.shape)])
                if n == 0:
                    for h in range(2):
                        loads.append((vrows[g][r:r + 1, h * H64:(h + 1) * H64], src.rearrange("(a b) -> a b", a=1)))
                else:
                    first = 96 if g == 3 else 0
                    loads.append((vrows[g][r:r + n, :], src.rearrange("(a b) -> a b", b=P)[first:first + n, :]))
                vat.setdefault(name, (g, r))
                r += n or 1
            vload.append((r, loads))

        def vec(name, i=0):
            g, r = vat[name]
            if name == "cv_dw_w_3" and i >= 96:
                g, r, i = 3, 0, i - 96
            return vcol[:, g, r + i:r + i + 1]

        def everywhere(src, n):
            return bass.AP(tensor=src.tensor, offset=src.offset, ap=[[0, P], [1, n]])

        block = ctx.enter_context(nc.Block())

        @block.sync
        def _(sp):
            for dst, src in vload[0][1]:
                sp.dma_start(dst, src).then_inc(c.sem("vrows_in0"), 16)
            sp.dma_start(xres[:, :, :], A["x"].rearrange("a (t p) d -> p (a t) d", p=P)).then_inc(c.sem("x_in"), 16)
            sp.dma_start(consts[:, 0:2 * P], A["consts"][:, 0:2 * P]).then_inc(c.sem("ident_in"), 16)
            base = [None]

            def piece(key, *loads):
                n = W.n
                W.n += 1
                W.number[key] = n
                s = n % RING
                if base[0] is not None:
                    i = n - base[0] - RING
                    hp = (2 * i + 1) % HALVES
                    sp.wait_ge(*(c.at if i >= 0 else c.before)(W.low_name(hp), hp))
                    if i < 0:
                        name, v = W.known.freed[n - RING] if W.known else ("piece_used", 1)
                        sp.wait_ge(c.sem(name), v)
                elif n >= RING:
                    name, v = W.known.freed[n - RING] if W.known else ("piece_used", 1)
                    sp.wait_ge(c.sem(name), c.value(name, v))
                for dst, src in loads:
                    sp.dma_start(dst(ring[:, s, :]), src).then_inc(c.sem(f"landed{s}"), 16)
                    W.slot[s] += 16
                W.landing[key] = (s, W.slot[s])

            def shaped(a, b, lo=0, hi=None):
                return lambda slot: slot[:, 0:a * b].rearrange("p (a b) -> p a b", a=a)[:, :, lo:b if hi is None else hi]

            def columns(name, w, col, cols=512):
                v = w.rearrange("(k p) n -> p k n", p=P)
                if cols == 256:
                    piece((name, col, 0), (shaped(KC, 256), v[:, :, col:col + 256]))
                    return
                for h in range(2):
                    piece((name, col, h), (shaped(4, 512), v[:, 4 * h:4 * h + 4, col:col + 512]))

            def chunk_rows(name, w, k):
                piece((name, k), (shaped(2, D), w.rearrange("(k p) n -> p k n", p=P)[:, 2 * k:2 * k + 2, :]))

            def ffn(stage, **weights):
                for p, (name, g) in enumerate(FFN[stage]):
                    if len(W.ffn_key(stage, p)) == 2:
                        chunk_rows(name, weights[name], g)
                    else:
                        columns(name, weights[name], 256 * g, 256)

            for i, beside in enumerate(((0,), (1,), (2,), (3, 4), (5, 6), (7,))):
                for x in beside:
                    columns("ada", A["ada_w_2"][0], 512 * ADA[x])
                columns("w_in", A["w_in"][0], 512 * i)
            for g in range(3072, 6144, 512):
                columns("w_in", A["w_in"][0], g)
            for name, i in (("w_out", 0), ("ada", 8), ("w_out", 1), ("w_out", 2), ("w_out", 3), ("ada", 9), ("ada", 10), ("ada", 11)):
                if name == "ada":
                    columns("ada", A["ada_w_2"][0], 512 * ADA[i])
                else:
                    chunk_rows("w_out", A["w_out"][0], i)
            for k in range(4, 8):
                chunk_rows("w_out", A["w_out"][0], k)
            if upto >= 2:
                for g in range(0, 3072, 512):
                    columns("w_in2", A["w_in_2"][0], g)
                for k in range(4):
                    chunk_rows("w_out2", A["w_out_2"][0], k)
                ffn("ff", ff1=A["w_ff1_2"][0], ff2=A["w_ff2_2"][0])
            if upto >= 3:
                columns("mem", A["w_mem_kv_3"], 0)
                for g in (0, 256, 512):
                    columns("cv_in", A["cv_w_in_3"][0], g, 256)
                    columns("cv_in", A["cv_w_in_3"][0], CONV + g, 256)
                columns("cv_in", A["cv_w_in_3"][0], 2 * CONV, 256)
                for k in (3, 0, 1, 2):
                    chunk_rows("cv_out", A["cv_w_out_3"][0], k)
                ffn("dn", gate=A["cv_w_gate_3"][0], up=A["cv_w_up_3"][0], down=A["cv_w_down_3"][0])
            if upto >= 4:
                v = A["sw_w_in_3"][0].rearrange("(k p) n -> p k n", p=P)

                for g in range(2):
                    for h in range(2):
                        piece(("sw_in", g, h),
                              *((shaped(4, 512, P * x + H64 * y, P * x + H64 * (y + 1)),
                                 v[:, 4 * h:4 * h + 4, 384 * g + 192 * y + H64 * x:384 * g + 192 * y + H64 * (x + 1)])
                                for x in range(3) for y in range(2)),
                              (shaped(4, 512, 384), v[:, 4 * h:4 * h + 4, 768 + P * g:768 + P * (g + 1)]))
                columns("sw_in", A["sw_w_in_3"][0], 1024)
                for k in range(4):
                    chunk_rows("sw_out", A["sw_w_out_3"][0], k)
            if upto >= 5:
                base[0], slot0 = W.n, list(W.slot)
                gate, up, down = (A[f"sw_we_{x}_3"].rearrange("a e (k p) n -> (a e) p k n", p=P) for x in ("gate", "up", "down"))

                def expert(e):
                    W.n, W.slot = base[0], list(slot0)
                    for key in ROUND_PIECES:
                        if key[0] == "xdown":
                            piece(key, (shaped(2, D), down[e, :, 2 * key[1]:2 * key[1] + 2, :]))
                        else:
                            w, (_, g, h) = gate if key[0] == "xgate" else up, key
                            piece(key, (shaped(4, 512), w[e, :, 4 * h:4 * h + 4, g * 512:(g + 1) * 512]))
                    assert W.n - base[0] == 6 * RING and HALVES % SPLITS == 0

                with sp.Fori(0, NEXP) as r:
                    c.loop = r
                    expert(r)
                    c.loop = None
                sp.wait_ge(*c.at("rounds_ready"))
                n_rounds = sp.value_load(ridi[0:1, 15:16], min_val=NEXP, max_val=NROUND)
                with sp.If(n_rounds > NEXP):
                    with sp.Fori(NEXP, n_rounds) as r:
                        e = sp.value_load(ridi[0:1, bass.ds(r, 1)], min_val=0, max_val=NEXP - 1)
                        c.loop = r
                        expert(e)
                        c.loop = None
            sp.wait_ge(*c.at("x_ready", min(upto, 5)))
            sp.dma_start(out.rearrange("a (t p) d -> p (a t) d", p=P), xres[:, :, :]).then_inc(c.sem("out_stored"), 16)
            sp.wait_ge(c.sem("out_stored"), 16)

        @block.tensor
        def _(pe):
            mm = nc.tensor.matmul

            def landed(key):
                s, v = W.known.landing[key] if W.known else (0, 16)
                pe.wait_ge(c.sem(f"landed{s}"), v if c.loop is None else c.loop * 96 + v)
                return ring[:, s, :]

            def chunks(name, col, cols=512):
                if cols == 256:
                    v = landed((name, col, 0)).rearrange("p (k n) -> p k n", k=KC)
                    return [v[:, k, :] for k in range(KC)], [(name, col, 0)]
                w = []
                for h in range(2):
                    v = landed((name, col, h)).rearrange("p (k n) -> p k n", k=4)
                    w += [v[:, k, :] for k in range(4)]
                return w, [(name, col, 0), (name, col, 1)]

            def done(last, *key):
                s = J.filled(*key)
                last.then_inc(s.sem, 1)
                return s

            def free(keys, signal):
                for k in keys:
                    W.free(k, signal)

            def turn(stage, src, n=KC):
                for q in range(n // 2):
                    b = J.fill(pe, stage, q)
                    for j in range(2):
                        for t in range(NT):
                            last = nc.tensor.transpose(ps[b][:, j * S + t * P:j * S + (t + 1) * P],
                                                       src[:, t, (2 * q + j) * P:(2 * q + j + 1) * P], ident)
                    done(last, stage, q)

            def turned(stage, n=4):
                for q in range(n):
                    pe.wait_ge(*J.emptied(stage, q))

            def proj_T(stage, w, c0, q, hT=hT):
                b = J.fill(pe, stage, q)
                for j in range(2):
                    for k in range(KC):
                        last = mm(ps[b][:, j * S:(j + 1) * S], w[k][:, c0 + j * P:c0 + (j + 1) * P], hT[:, k, :],
                                  start=(k == 0), stop=(k == KC - 1))
                return done(last, stage, q)

            def cols_T(stage, name, col, cols=512):
                w, keys = chunks(name, col, cols)
                for q in range(cols // 256):
                    s = proj_T(stage, w, q * 256, col // 256 + q)
                free(keys, s)

            def cols_tok(stage, name, col):
                w, keys = chunks(name, col)
                for t in range(NT):
                    b = J.fill(pe, stage, col, t)
                    for k in range(KC):
                        last = mm(ps[b][:, :], hT[:, k, t * P:(t + 1) * P], w[k], start=(k == 0), stop=(k == KC - 1))
                    s = done(last, stage, col, t)
                free(keys, s)

            def split_cols(stage, name, col, jobs, tok):
                banks = [J.fill(pe, stage, *job) for job in jobs]
                for half in range(4):
                    hp = 2 * SPLIT_KEYS.index((name, col, 0)) + half
                    pe.wait_ge(*c.at("d_lo", hp))
                    hi, lo = (w[:, hp % SPLIT_SLOTS, :].rearrange("p (k n) -> p k n", k=2) for w in (d_hi, d_lo))
                    for q in range(2):
                        for k in range(2):
                            kk = 2 * half + k
                            if hp < 4 and q + k == 0:
                                pe.wait_ge(*c.at("h_split", "mix2", half))
                            o = ps[banks[q]]
                            if tok:
                                t = slice(q * P, (q + 1) * P)
                                mm(o[:, :], dT_hi[:, kk, t], hi[:, k, :], start=(kk == 0), stop=False)
                                mm(o[:, :], dT_hi[:, kk, t], lo[:, k, :], start=False, stop=False)
                                last = mm(o[:, :], dT_lo[:, kk, t], hi[:, k, :], start=False, stop=(kk == KC - 1))
                            else:
                                for j in range(2):
                                    x, cols = o[:, j * S:(j + 1) * S], slice(q * S + j * P, q * S + (j + 1) * P)
                                    mm(x, hi[:, k, cols], dT_hi[:, kk, :], start=(kk + j == 0), stop=False)
                                    mm(x, hi[:, k, cols], dT_lo[:, kk, :], start=False, stop=False)
                                    last = mm(x, lo[:, k, cols], dT_hi[:, kk, :], start=False, stop=(kk == KC - 1 and j == 1))
                        if half == 3:
                            s = done(last, stage, *jobs[q])
                    if half < 3:
                        s = c.sig("d_used", hp)
                        last.then_inc(s.sem, 1)
                    W.halves["d", hp] = (s.name, s.base)

            def sum_rows(stage, name, n, mixT, ready=lambda k: None, ks=None, first=0, last_=None):
                last_ = n - 1 if last_ is None else last_
                for k in ks or range(n):
                    w = landed((name, k)).rearrange("p (k n) -> p k n", k=2)
                    ready(k)
                    for t in range(NT):
                        for j in range(2):
                            for h in range(2):
                                last = mm(acc[2 * t + h][:, :], mixT[:, 2 * k + j, t * P:(t + 1) * P],
                                          w[:, j, h * 512:(h + 1) * 512], start=(k == first and j == 0), stop=(k == last_ and j == 1))
                        if k == last_ and t == 0:
                            last.then_inc(c.sig("sums0", stage).sem, 1)
                    s = c.sig("piece_used", stage, k)
                    last.then_inc(s.sem, 1)
                    free([(name, k)], s)

            def scores(stage, i, segs, score):
                b = J.fill(pe, stage + "S", i)
                for t, col, nk in segs:
                    last = score(i, t, ps[b][:, col:col + nk * P], nk)
                done(last, stage + "S", i)

            def turn_probs(stage, h, segs, buf):
                pe.wait_ge(*c.at("probs_ready", stage, h))
                b = J.fill(pe, stage + "T", h)
                for x in range(sum(nk for _, _, nk in segs)):
                    last = nc.tensor.transpose(ps[b][:, x * P:(x + 1) * P], tile(stage)[:, buf, x * P:(x + 1) * P], ident)
                done(last, stage + "T", h)

            def out_T(stage, h, segs, v, base, width):
                pe.wait_ge(*J.emptied(stage + "T", h))
                b = J.fill(pe, stage + "O", h)
                x = 0
                for t, col, nk in segs:
                    for k in range(nk):
                        last = mm(ps[b][base:base + width, t * P:(t + 1) * P], v(k), probT[:, h % 2, x * P:(x + 1) * P],
                                  start=(k == 0), stop=(k == nk - 1))
                        x += 1
                done(last, stage + "O", h)

            def attend(stage, H, segs, score, v, place, between=lambda i: None):
                for i in range(H + 3):
                    if i < H:
                        scores(stage, i, segs, score)
                    between(i)
                    if 2 <= i < H + 2:
                        turn_probs(stage, i - 2, segs, (i - 2) % 4)
                    if i >= 3:
                        out_T(stage, i - 3, segs, v(i - 3), *place(i - 3))

            def head_rms(stage, *qs):
                for q in qs:
                    pe.wait_ge(*c.at("squares", stage, q))
                    b = J.fill(pe, stage, q)
                    done(mm(ps[b][:, :], C("half"), hsq[:, q % 2, :], start=True, stop=True), stage, q)

            def columns_of(g):
                pe.wait_ge(c.sem(f"vrows_in{g}"), 16 * len(vload[g][1]))
                b, r = J.fill(pe, "vec", g), vload[g][0]
                done(nc.tensor.transpose(ps[b][:, 0:r], vrows[g][0:r, :], ident[0:r, 0:r]), "vec", g)

            pe.wait_ge(c.sem("ident_in"), 16)
            columns_of(0)

            pe.wait_ge(*c.at("normed", "pre"))
            turn("pre", nrm)
            turned("pre")

            def ada_columns(*places):
                for x in places:
                    pe.wait_ge(*c.at("ada_sum", x, 1))
                    b = J.fill(pe, "ada", ADA[x])
                    for j in range(4):
                        last = mm(ps[b][:, j:j + 1], adasum[x % 4][:, j * P:(j + 1) * P], ones[:, 0:1], start=True, stop=True)
                    done(last, "ada", ADA[x])

            def ada_gates(*places):
                for g in (ADA[x] for x in places):
                    w, keys = chunks("ada", g * 512)
                    b = J.fill(pe, "ada", g)
                    for k in range(KC):
                        last = mm(ps[b][:, :], cact[:, k, :], w[k], start=(k == 0), stop=(k == KC - 1))
                    free(keys, done(last, "ada", g))

            cols_T("b1p", "w_in", 0)
            cols_T("b1p", "w_in", 512)
            ada_columns(0, 1)
            pe.wait_ge(*c.at("rel_wide"))
            pe.wait_ge(c.sem("consts_in"), 16)
            for h in range(HEADS1):
                b = J.fill(pe, "rel", h)
                done(mm(ps[b][:, 0:511], relw[0:33, h, :], C("rel")[0:33, :], start=True, stop=True), "rel", h)
            for g in range(1, 4):
                columns_of(g)
            cols_T("b1p", "w_in", 1024)
            ada_columns(2)
            cols_T("b1p", "w_in", 1536)
            ada_columns(3, 4)
            cols_tok("b1v", "w_in", 2048)
            ada_columns(5, 6)
            cols_tok("b1v", "w_in", 2560)
            ada_columns(7)
            for q in range(8):
                pe.wait_ge(*J.emptied("b1p", q))
            for col in (2048, 2560):
                for t in range(NT):
                    pe.wait_ge(*J.emptied("b1v", col, t))

            def b1_between(i):
                if i in B1_BETWEEN:
                    cols_T("b1p", "w_in", B1_BETWEEN[i])

            attend("b1", HEADS1, T384,
                   lambda h, t, dst, nk: mm(dst, qT[:, h, t * P:(t + 1) * P], kT[:, h, 0:nk * P], start=True, stop=True),
                   lambda h: lambda k: vt[:, k, h * P:(h + 1) * P], lambda h: (0, P), b1_between)

            pe.wait_ge(*c.at("bd_ready"))
            for q in range(16, 20):
                pe.wait_ge(*J.emptied("b1p", q))
            for m, key, src in ((2, "vmT", xmT), (0, "qm", xcT), (1, "km", xcT)):
                for q in range(4):
                    if m == 0:
                        pe.wait_ge(*c.at("conv_ready", 2 * q + 1))
                    b = J.fill(pe, key, q)
                    for j in range(2):
                        last = mm(ps[b][:, j * S:(j + 1) * S], bd[:, 8 * m + 2 * q + j, :], src[:, 2 * q + j, :],
                                  start=True, stop=True)
                    done(last, key, q)
            for t in range(NT):
                for q in range(2):
                    b = J.fill(pe, "vm", t, q)
                    for j in range(4):
                        last = mm(ps[b][:, j * P:(j + 1) * P], xmT[:, 4 * q + j, t * P:(t + 1) * P], bd[:, 16 + 4 * q + j, :],
                                  start=True, stop=True)
                    done(last, "vm", t, q)
            def b1_out(*ks):
                sum_rows("b1", "w_out", 8, mix1, lambda k: pe.wait_ge(*J.emptied("mlstm", k - 4)) if k >= 4 else None, ks)

            for h in range(HEADS1):
                pe.wait_ge(*J.emptied("b1O", h))
            b1_out(0)
            pe.wait_ge(*c.at("c_ready"))
            ada_gates(8)
            pe.wait_ge(c.sem("wif_in"), 32)
            for key in ("qm", "km", "vmT"):
                for q in range(4):
                    pe.wait_ge(*J.emptied(key, q))
            b = J.fill(pe, "gates")
            for t in range(NT):
                o = ps[b][:, t * 8:t * 8 + 8]
                for m, src in enumerate((qmT, kmT, vmT)):
                    for k in range(KC):
                        mm(o, src[:, k, t * P:(t + 1) * P], wif[:, 8 * m + k, :], start=(m + k == 0), stop=False)
                last = mm(o, ones[0:1, :], brow[0:1, 0:8], start=False, stop=True)
            done(last, "gates")
            b1_out(1)
            pe.wait_ge(*c.at("loggates"))
            b = J.fill(pe, "Frow")
            for k in range(NT):
                mm(ps[b][0:MH, 0:S], gl[:, k, 4:8], C("upto", 2)[:, k, :], start=(k == 0), stop=(k == 1))
            for k in range(NT):
                last = mm(ps[b][0:MH, S + k * P:S + (k + 1) * P], gl[:, k, 0:4], ident, start=True, stop=True)
            done(last, "Frow")
            b = J.fill(pe, "Fcol")
            for t in range(NT):
                for k in range(t + 1):
                    last = mm(ps[b][:, t * 4:t * 4 + 4], C("upto", 2)[:, k, t * P:(t + 1) * P], gl[:, k, 4:8],
                              start=(k == 0), stop=(k == t))
            done(last, "Fcol")
            pe.wait_ge(*c.at("a_rows"))
            for t in range(NT):
                for q in range(2):
                    pe.wait_ge(*J.emptied("vm", t, q))
            for i in range(MH + 2):
                if i < MH:
                    b = J.fill(pe, "mA", i)
                    for t, col, nk in T384:
                        last = mm(ps[b][:, col:col + nk * P], C("hsel", MH)[0:MH, i, :], aT[0:MH, 0:nk * P], start=True, stop=True)
                    done(last, "mA", i)
                    b = J.fill(pe, "mS", i)
                    for t, col, nk in T384:
                        for k in range(2):
                            last = mm(ps[b][:, col:col + nk * P], qmT[:, 2 * i + k, t * P:(t + 1) * P], kmT[:, 2 * i + k, 0:nk * P],
                                      start=(k == 0), stop=(k == 1))
                    done(last, "mS", i)
                if i in (1, 3):
                    b1_out(2 + i // 2)
                if 1 <= i <= MH:
                    turn_probs("m", i - 1, T384, (i - 1) % 4)
                if i >= 2:
                    h = i - 2
                    pe.wait_ge(*J.emptied("mT", h))
                    b = J.fill(pe, "mO", h)
                    for t, x, k, stop in ((0, 0, 0, True), (1, 1, 0, False), (1, 2, 1, True)):
                        last = mm(ps[b][:, t * S:(t + 1) * S], probT[:, h % 2, x * P:(x + 1) * P], vm[:, k, h * MD:(h + 1) * MD],
                                  start=(k == 0), stop=stop)
                    done(last, "mO", h)
            ada_gates(9, 10, 11)
            pe.wait_ge(*c.at("normed", "mlstm"))
            turn("mlstm", nrm)
            b1_out(4, 5, 6, 7)

            if upto < 2:
                return
            pe.wait_ge(*c.at("normed", "mix2"))
            turn("mix2", nrm)
            for x, col in enumerate((0, 512)):
                split_cols("dqk", "w_in2", col, ((2 * x,), (2 * x + 1,)), False)
            for q in range(4):
                pe.wait_ge(*J.emptied("dqk", q))
                b = J.fill(pe, "rot", q)
                done(mm(ps[b][:, :], C("rot"), qraw[:, q, :], start=True, stop=True), "rot", q)
            split_cols("b2v", "w_in2", 1024, ((1024, 0), (1024, 1)), True)
            for q in range(4):
                pe.wait_ge(*c.at("roped", q))
            for t in range(NT):
                pe.wait_ge(*J.emptied("b2v", 1024, t))

            def diff_score(i, t, dst, nk):
                h, m = i // 2, 64 * (i % 2)
                return mm(dst, qdT[m:m + 64, h, t * P:(t + 1) * P], kdT[m:m + 64, h, 0:nk * P], start=True, stop=True)

            def stick_logits(i):
                for h in (2 * i, 2 * i + 1):
                    m, ch = 64 * (h % 2), h // 2
                    b = J.fill(pe, "sbz", h)
                    mm(ps[b][:, 0:S], skT[m:m + 64, ch, 0:P], sqT[m:m + 64, ch, :], start=True, stop=True)
                    done(mm(ps[b][:, S:S + P], skT[m:m + 64, ch, P:S], sqT[m:m + 64, ch, P:S], start=True, stop=True), "sbz", h)

            for i in range(NDIFF + 3):
                if i < NDIFF:
                    scores("d", 2 * i, T384, diff_score)
                    scores("d", 2 * i + 1, T384, diff_score)
                if i < 2:
                    split_cols("sqk", "w_in2", 1536 + 512 * i, ((6 + 2 * i,), (7 + 2 * i,)), False)
                if i == 2:
                    split_cols("b2v", "w_in2", 2560, ((2560, 0), (2560, 1)), True)
                if i == NDIFF:
                    for q in range(6, 10):
                        pe.wait_ge(*J.emptied("sqk", q))
                    stick_logits(0)
                if 2 <= i < NDIFF + 2:
                    turn_probs("dd", i - 2, T384, 2 * ((i - 2) % 3))
                if i >= 3:
                    h = i - 3
                    pe.wait_ge(*J.emptied("ddT", h))
                    b = J.fill(pe, "ddO", h)
                    for t, x, k, stop in ((0, 0, 0, True), (1, 1, 0, False), (1, 2, 1, True)):
                        last = mm(ps[b][:, t * P:(t + 1) * P], probT[:, h % 2, x * P:(x + 1) * P], vd[:, k, h * P:(h + 1) * P],
                                  start=(k == 0), stop=stop)
                    done(last, "ddO", h)
            for t in range(NT):
                pe.wait_ge(*J.emptied("b2v", 2560, t))
            for i in range(1, NSB // 2 + 2):
                if i < NSB // 2:
                    stick_logits(i)
                if 1 <= i <= NSB // 2:
                    pe.wait_ge(*c.at("log1m_ready", i - 1))
                    for h in (2 * i - 2, 2 * i - 1):
                        l1 = sbw[h // 2 % 3][:, h % 2, 0:384]
                        b = J.fill(pe, "sbs", h)
                        mm(ps[b][:, 0:S], C("after"), l1[:, 0:S], start=True, stop=False)
                        mm(ps[b][:, P:S], ones, l1[:, S:S + P], start=False, stop=True)
                        done(mm(ps[b][:, S:S + P], C("after"), l1[:, S:S + P], start=True, stop=True), "sbs", h)
                if i == 1:
                    pe.wait_ge(*c.at("normed", "subln"))
                    turn("subln", nrm, 4)
                if i in (2, 3):
                    pe.wait_ge(*J.emptied("subln", i - 2))
                    sum_rows("b2", "w_out2", 4, mix2, ks=(i - 2,))
                if i >= 2:
                    pe.wait_ge(*c.at("sticks_ready", i - 2))
                    for h in (2 * i - 4, 2 * i - 3):
                        m, a = 64 * (h % 2), sbw[h // 2 % 3][:, h % 2, 384:768]
                        b = J.fill(pe, "sbo", h)
                        mm(ps[b][m:m + 64, 0:S], sv[:, 0, h * 64:(h + 1) * 64], a[:, 0:S], start=True, stop=False)
                        done(mm(ps[b][m:m + 64, P:S], sv[:, 1, h * 64:(h + 1) * 64], a[:, S:S + P], start=False, stop=True), "sbo", h)
            for h in range(NSB):
                pe.wait_ge(*J.emptied("sbo", h))
            sum_rows("b2", "w_out2", 4, mix2, ks=(2, 3))
            def ffn(stage):
                def split(hp):
                    pe.wait_ge(*c.at("ff_lo", stage, hp))
                    return w_hi[:, hp % SPLITS, :], w_lo[:, hp % SPLITS, :]

                def used(hp, last, job=None):
                    s = done(last, *job) if job else c.sig("ff_used", stage, hp)
                    if not job:
                        last.then_inc(s.sem, 1)
                    W.halves[stage, hp] = (s.name, s.base)

                n = FFN[stage][-1][1] + 1
                for p, (name, g) in enumerate(FFN[stage]):
                    rows = len(W.ffn_key(stage, p)) == 2
                    if rows:
                        pe.wait_ge(*c.at("f_ready", stage, g))
                    else:
                        b = J.fill(pe, name, g)
                    if rows:
                        for y in range(2 * NT):
                            half, t = (y % 2, y // 2) if g == n - 1 else (y // 2, y % 2)
                            hp = 2 * p + half
                            hi, lo = split(hp)
                            tok = slice(half * S + t * P, half * S + (t + 1) * P)
                            for x, (a, w) in enumerate(((f_hi, hi), (f_hi, lo), (f_lo, hi))):
                                for h in range(2):
                                    last = mm(acc[2 * t + h][:, :], a[:, g % 4, tok], w[:, h * 512:(h + 1) * 512],
                                              start=(g + half + x == 0), stop=(g == n - 1 and half == 1 and x == 2))
                            if t == 1:
                                used(hp, last)
                            elif half == 1 and g == n - 1:
                                last.then_inc(c.sig("sums0", stage).sem, 1)
                    else:
                        for half in range(2):
                            hp = 2 * p + half
                            hi, lo = split(hp)
                            hi, lo = (w.rearrange("p (k n) -> p k n", k=4) for w in (hi, lo))
                            for k in range(4):
                                kk = 4 * half + k
                                if p == 0 and kk % 2 == 0:
                                    pe.wait_ge(*c.at("h_split", {"ff": "ffn2", "dn": "cvf"}[stage], kk // 2))
                                for j in range(2):
                                    o, cols = ps[b][:, j * S:(j + 1) * S], slice(j * P, (j + 1) * P)
                                    mm(o, hi[:, k, cols], hT_hi[:, kk, :], start=(kk + j == 0), stop=False)
                                    mm(o, hi[:, k, cols], hT_lo[:, kk, :], start=False, stop=False)
                                    last = mm(o, lo[:, k, cols], hT_hi[:, kk, :], start=False, stop=(kk == KC - 1 and j == 1))
                            used(hp, last, (name, g) if half else None)
                    if (stage, name, g) == ("ff", "ff1", 12) and upto >= 3:
                        turn_memory()

            def turn_memory():
                pe.wait_ge(*c.at("normed", "mem"))
                turn("mem", nrm)

            pe.wait_ge(*c.at("normed", "ffn2"))
            turn("ffn2", nrm)
            ffn("ff")
            if upto < 3:
                return

            turned("mem")
            w, keys = chunks("mem", 0)
            proj_T("memk", w, 0, 0, memT)
            b = J.fill(pe, "memv")
            for t in range(NT):
                for k in range(KC):
                    last = mm(ps[b][:, t * 256:(t + 1) * 256], memT[:, k, t * P:(t + 1) * P], w[k][:, 256:512],
                              start=(k == 0), stop=(k == KC - 1))
            free(keys, done(last, "memv"))
            head_rms("memk2", 0)

            def mem_attend(stage, qsrc):
                attend(stage, MEMH, T512,
                       lambda h, t, dst, nk: mm(dst, qsrc[64 * (h % 2):64 * (h % 2) + 64, h // 2, t * P:(t + 1) * P],
                                                memkT[64 * (h % 2):64 * (h % 2) + 64, h // 2, :], start=True, stop=True),
                       lambda h: lambda k: memv[:, k, h * 64:(h + 1) * 64], lambda h: (64 * (h % 2), 64))

            pe.wait_ge(*c.at("normed", "cv"))
            turn("cv", nrm)
            turned("cv")
            for g in range(3):
                cols_T("cvp", "cv_in", CONV + 256 * g, 256)
                cols_T("cvp", "cv_in", 256 * g, 256)
            cols_T("cvp", "cv_in", 2 * CONV, 256)
            head_rms("cvq2", 0)
            pe.wait_ge(*J.emptied("cvp", 2))
            for x, k in enumerate(CONV_PE):
                for d in range(CONVW):
                    n = x * CONVW + d
                    pe.wait_ge(*c.at("tap_ready", n))
                    mm(acc[x][:, d:S], diag[:, n % DIAGS, :], uT[:, k, 0:S - d], start=(d == 0), stop=(d == CONVW - 1))\
                        .then_inc(c.sig("tap_used", n).sem, 1)
            pe.wait_ge(*c.at("head_normed", "memk2", 0))
            pe.wait_ge(*J.emptied("memv"))
            pe.wait_ge(*c.at("head_normed", "cvq2", 0))
            mem_attend("cm", mqT)
            for key, src in (("cmean", cT), ("cvar", sq3)):
                for k in range(CC):
                    if k == 0 or key == "cmean":
                        pe.wait_ge(*(c.at("conv_pool" if k < 1 else "cmean_in", k) if key == "cmean" else c.at("cvar_in")))
                    if k == 0:
                        b = J.fill(pe, key)
                    last = mm(ps[b][:, 0:S], ones, src[:, k, :], start=(k == 0), stop=(k == CC - 1))
                done(last, key)
                if key == "cmean":
                    for h in range(MEMH):
                        pe.wait_ge(*J.emptied("cmO", h))
                    sum_rows("cv", "cv_out", 4, mix3, ks=(3,), first=3, last_=2)
            sum_rows("cv", "cv_out", 4, mix3, lambda k: pe.wait_ge(*c.at("conv_act", 2 * k + 1)), (0, 1, 2), 3, 2)
            pe.wait_ge(*c.at("normed", "cvf"))
            turn("cvf", nrm)
            ffn("dn")
            if upto < 4:
                return

            pe.wait_ge(*c.at("normed", "sw"))
            turn("sw", nrm)
            turned("sw")
            for g in range(2):
                w, keys = [], []
                for h in range(2):
                    v = landed(("sw_in", g, h)).rearrange("p (k n) -> p k n", k=4)
                    w += [v[:, k, :] for k in range(4)]
                    keys.append(("sw_in", g, h))
                for q in range(2):
                    b = J.fill(pe, "swp", 2 * g + q)
                    for j in range(2):
                        x = 2 * q + j
                        for k in range(KC):
                            last = mm(ps[b][:, j * S:(j + 1) * S], w[k][:, x * P:(x + 1) * P], hT[:, k, :],
                                      start=(k == 0), stop=(k == KC - 1))
                    s = done(last, "swp", 2 * g + q)
                free(keys, s)
                head_rms("swn", g)
            w, keys = chunks("sw_in", 1024)
            b = J.fill(pe, "swv")
            for t in range(NT):
                for k in range(KC):
                    last = mm(ps[b][:, t * 256:(t + 1) * 256], hT[:, k, t * P:(t + 1) * P], w[k][:, 0:256],
                              start=(k == 0), stop=(k == KC - 1))
            done(last, "swv")
            head_rms("swn", 2)
            free(keys, proj_T("swm", w, 256, 0))
            head_rms("swn", 3)
            pe.wait_ge(*J.emptied("swv"))
            pe.wait_ge(*c.at("head_normed", "swn", 3))

            def swa_score(h, t, dst, nk):
                g, y, x = h // 6, 64 * (h % 6 // 3), h % 3
                return mm(dst, swq[y:y + 64, 3 * g + x, t * P:(t + 1) * P], swk[y:y + 64, g, 0:nk * P], start=True, stop=True)

            def sw_between(i):
                if i == 0:
                    head_rms("swn", 4)
                if i in SW_BETWEEN:
                    for h in range(4 * SW_BETWEEN[i], 4 * SW_BETWEEN[i] + 4):
                        pe.wait_ge(*J.emptied("swO", h))
                    sum_rows("so", "sw_out", 4, mix3, ks=(SW_BETWEEN[i],))

            attend("sw", SWAH, T384, swa_score, lambda h: lambda k: swv[:, k, (h // 3) * 64:(h // 3 + 1) * 64],
                   lambda h: (64 * (h % 2), 64), sw_between)
            pe.wait_ge(*c.at("head_normed", "swn", 4))
            mem_attend("sm", mqT)
            for st_, hs in (("sw", range(8, SWAH)), ("sm", range(MEMH))):
                for h in hs:
                    pe.wait_ge(*J.emptied(st_ + "O", h))
            sum_rows("so", "sw_out", 4, mix3, ks=(2, 3))
            if upto < 5:
                return

            pe.wait_ge(*c.at("normed", "moe"))
            turn("moe", nrm)
            turned("moe")
            pe.wait_ge(c.sem("rw_in"), 16)
            b = J.fill(pe, "router")
            for t in range(NT):
                for k in range(KC):
                    last = mm(ps[b][:, t * 8:t * 8 + 8], hT[:, k, t * P:(t + 1) * P], rw[:, k, :], start=(k == 0), stop=(k == KC - 1))
            done(last, "router")
            pe.wait_ge(*c.at("selected"))
            b = J.fill(pe, "slots")
            for t in range(NT):
                for k in range(t + 1):
                    mm(ps[b][:, t * 8:t * 8 + 8], C("before", 2)[:, k, t * P:(t + 1) * P], rt[:, 1, k, :], start=(k == 0), stop=(k == t))
            for k in range(NT):
                last = mm(ps[b][:, 16:24], ones, rt[:, 1, k, :], start=(k == 0), stop=(k == NT - 1))
            done(last, "slots")

            def gather(turn_):
                pe.wait_ge(*c.at("dispatch_ready", turn_))
                for q in range(2):
                    b = J.fill(pe, "hg" + turn_, q)
                    for j in range(4):
                        for t in range(NT):
                            last = mm(ps[b][:, j * P:(j + 1) * P], nrm[:, t, (4 * q + j) * P:(4 * q + j + 1) * P], Pm[:, t, :],
                                      start=(t == 0), stop=(t == NT - 1))
                    done(last, "hg" + turn_, q)

            def turn_gates():
                b = J.fill(pe, "pgT")
                for t in range(NT):
                    last = nc.tensor.transpose(ps[b][:, t * P:(t + 1) * P], PG[:, t, :], ident)
                done(last, "pgT")

            gather("first")
            pe.wait_ge(*c.at("rounds_ready"))
            n_rounds = pe.value_load(ridi[0:1, 15:16], min_val=NEXP, max_val=NROUND)
            with pe.Fori(0, n_rounds) as r:
                c.enter(r)

                def split(hp):
                    pe.wait_ge(*c.at(W.low_name(hp), hp))
                    return w_hi[:, hp % SPLITS, :], w_lo[:, hp % SPLITS, :]

                def turn_act(g):
                    pe.wait_ge(*J.emptied("xu", g))
                    b = J.fill(pe, "xt", g)
                    for j in range(4):
                        last = nc.tensor.transpose(ps[b][:, j * P:(j + 1) * P], eact[:, g % 2, j * P:(j + 1) * P], ident)
                    done(last, "xt", g)

                pe.wait_ge(*c.before("gathered", "next", 1))
                for g in range(FFE // 512):
                    for x, key in enumerate(("xg", "xu")):
                        b = J.fill(pe, key, g)
                        for q in range(4):
                            hp = 8 * g + 4 * x + q
                            hi, lo = split(hp)
                            for j in range(2):
                                k = 2 * q + j
                                cols = slice(j * 512, (j + 1) * 512)
                                mm(ps[b][:, :], hg_hi[:, k, :], hi[:, cols], start=(k == 0), stop=False)
                                mm(ps[b][:, :], hg_hi[:, k, :], lo[:, cols], start=False, stop=False)
                                last = mm(ps[b][:, :], hg_lo[:, k, :], hi[:, cols], start=False, stop=(k == KC - 1))
                            if q < 3:
                                s = c.sig("half_used", hp)
                                last.then_inc(s.sem, 1)
                            else:
                                s = done(last, key, g)
                            W.half_free(hp, s)
                    if g == 0:
                        turn_gates()
                    if g >= 1:
                        turn_act(g - 1)
                gather("next")
                turn_act(FFE // 512 - 1)
                for k in range(FFE // P):
                    hp = 8 * (FFE // 512) + k
                    if k % 4 == 0:
                        pe.wait_ge(*J.emptied("xt", k // 4))
                    hi, lo = split(hp)
                    for a, w in ((act_hi, hi), (act_hi, lo), (act_lo, hi)):
                        for h in range(2):
                            last = mm(acc[h][:, :], a[:, k, :], w[:, h * 512:(h + 1) * 512],
                                      start=(k == 0 and a is act_hi and w is hi), stop=(k == FFE // P - 1 and a is act_lo))
                    s = c.sig("piece_used", "xdown", k)
                    last.then_inc(s.sem, 1)
                    W.half_free(hp, s)
                pe.wait_ge(*J.emptied("pgT"))
                pe.wait_ge(*c.at("expert_out", 0))
                pe.wait_ge(*c.at("expert_out1", 0))
                for t in range(NT):
                    for h in range(2):
                        b = J.fill(pe, "xs", t, h)
                        done(mm(ps[b][:, :], pgT[:, t * P:(t + 1) * P], ey[:, h * 512:(h + 1) * 512], start=True, stop=True), "xs", t, h)
                c.leave()
        @block.scalar
        def _(act):
            def do(ins, s=None):
                s = s or c.sig("act_step")
                ins.then_inc(s.sem, 1)
                act.wait_ge(s.sem, s.val)

            def go(ins, s):
                ins.then_inc(s.sem, 1)

            f = nc.scalar.activation

            for g, (r, loads) in enumerate(vload):
                for dst, src in loads if g else ():
                    act.dma_start(dst, src).then_inc(c.sem(f"vrows_in{g}"), 16)
                if g == 0:
                    act.dma_start(relb[0:32, :], A["rel_bias"]).then_inc(c.sem("rel_in"), 16)
                    act.dma_start(consts[:, 2 * P:], A["consts"][:, 2 * P:]).then_inc(c.sem("consts_in"), 16)
            act.dma_start(wif[:, :, :], A["w_if"][0].rearrange("(k p) n -> p k n", p=P)).then_inc(c.sem("wif_in"), 16)
            act.dma_start(brow[0:1, :], A["b_if"]).then_inc(c.sem("wif_in"), 16)
            for m, name in enumerate(("wq_m", "wk_m", "wv_m")):
                act.dma_start(wraw[:, 8 * m:8 * m + 8, :], A[name][0].rearrange("(k n) i o -> (n i) k o", k=8))\
                    .then_inc(c.sem("wraw_in"), 16)
            act.dma_start(wide[:, :], everywhere(A["g_post"], D)).then_inc(c.sem("wide_in"), 16)
            act.dma_start(sinkb[:, :], everywhere(A["sw_sinks_3"], SWAH)).then_inc(c.sem("small_in"), 16)
            for i, name in enumerate(("lambda_q1_2", "lambda_k1_2", "lambda_q2_2", "lambda_k2_2")):
                act.dma_start(lamv[:, i, :], everywhere(A[name], H64)).then_inc(c.sem("small_in"), 16)
            act.dma_start(rw[:, :, :], A["sw_router_3"][0].rearrange("(k p) n -> p k n", p=P)).then_inc(c.sem("rw_in"), 16)

            def copy(dst, key, cols=512, lo=0, rows=slice(0, P), func=ACT.Copy):
                act.wait_ge(*J.full(*key))
                do(f(dst, ps[J.bank(*key)][rows, lo:lo + cols], func), J.free(*key))

            def pair(buf, q):
                return buf[:, 2 * q:2 * q + 2, :].rearrange("p a b -> p (a b)")

            def exps(stage, i, segs, buf, sink=None):
                act.wait_ge(*c.at("max_ready", stage, i))
                for t, col, nk in segs:
                    x = tile(stage)[:, buf, col:col + nk * P]
                    do(f(x, x, ACT.Exp, bias=smx[:, buf, t:t + 1], accum_out=smx[:, buf, 2 + t:3 + t]),
                       c.sig("exp_done", stage, i) if t == 1 and sink is None else None)
                if sink is not None:
                    for t in range(NT):
                        do(f(smx[:, buf, 6 + t:7 + t], sink, ACT.Exp, bias=smx[:, buf, t:t + 1]),
                           c.sig("exp_done", stage, i) if t == 1 else None)

            def probs_T(stage, h, segs, prev):
                if h >= 2:
                    act.wait_ge(*J.full(prev, h - 2))
                copy(probT[:, h % 2, 0:P * sum(nk for _, _, nk in segs)], (stage + "T", h), P * sum(nk for _, _, nk in segs))

            def head_rms(stage, raws, q0=0):
                for q, raw in enumerate(raws, q0):
                    if q >= 2:
                        act.wait_ge(*J.full(stage, q - 2))
                    do(f(hsq[:, q % 2, :], raw, ACT.Square), c.sig("squares", stage, q))
                    act.wait_ge(*J.full(stage, q))
                    if q >= 2:
                        act.wait_ge(*c.at("head_normed", stage, q - 2))
                    do(f(rsw[:, q % 2, :], ps[J.bank(stage, q)][:, :], ACT.Sqrt, scale=1.0 / H64, bias=C("eps")[:, 0:1]),
                       J.free(stage, q))

            def columns_of(g):
                copy(vcol[:, g, 0:vload[g][0]], ("vec", g), vload[g][0])

            act.wait_ge(*J.emptied("vec", 0))
            do(f(ccol[:, :], vcol[:, vat["c_2"][0], vat["c_2"][1]:vat["c_2"][1] + KC], ACT.Silu), c.sig("c_act"))
            for q in range(4):
                copy(pair(qT, q), ("b1p", q))
            for h in range(HEADS1):
                copy(relrep[:, h, 0:511], ("rel", h), 511)
            act.dma_start(relrow, relrep[:, :, 0:511]).then_inc(c.sem("relrow_out"), 16)
            act.wait_ge(c.sem("relrow_out"), 16)
            for first, lo, n in ((255, 0, P), (127, P, S)):
                act.dma_start(relbias[:, :, lo:lo + n],
                              bass.AP(tensor=relrow.tensor, offset=first, ap=[[HEADS1 * 511 - 1, P], [511, HEADS1], [1, n]]))\
                    .then_inc(c.sem("relbias_in"), 16)
            for g in range(1, 4):
                columns_of(g)
            for q in range(4):
                copy(pair(kT, q), ("b1p", 4 + q))
            for i in range(HEADS1 + 3):
                if i < HEADS1:
                    exps("b1", i, T384, i % 4)
                if i in B1_BETWEEN:
                    for q in (B1_BETWEEN[i] // 256, B1_BETWEEN[i] // 256 + 1):
                        if q < 16:
                            copy(pair(mix1, q - 12), ("b1p", q), func=ACT.Silu)
                        elif q < 20:
                            copy(pair(xmT, q - 16), ("b1p", q))
                        else:
                            copy(pair(mix1, q - 20 + 4), ("b1p", q), func=ACT.Silu)
                if 2 <= i < HEADS1 + 2:
                    probs_T("b1", i - 2, T384, "b1O")
            for q in range(4):
                copy(pair(vmT, q), ("vmT", q))
            for k in range(KC):
                act.wait_ge(*c.at("conv", k))
                do(f(xcT[:, k, :], xcT[:, k, :], ACT.Silu), c.sig("conv_ready", k))
            for key, dst in (("qm", qmT), ("km", kmT)):
                for q in range(4):
                    copy(pair(dst, q), (key, q))
            act.wait_ge(*c.at("gates_in"))
            do(f(lg[:, :, 0:4], gl[:, :, 4:8], ACT.Abs))
            do(f(lg[:, :, 4:8], lg[:, :, 0:4], ACT.Exp, scale=-1.0))
            do(f(lg[:, :, 8:12], lg[:, :, 4:8], ACT.Ln, bias=ones[:, 0:1]), c.sig("softplus", "gates"))
            for i in range(MH + 2):
                if i < MH:
                    act.wait_ge(*c.at("max_ready", "m", i))
                    for t, col, nk in T384:
                        x = logit[:, i % 4, col:col + nk * P]
                        do(f(x, x, ACT.Exp, bias=mcol[:, i, 2 + t:3 + t]))
                    do(f(mcol[:, i, 6:8], mcol[:, i, 4:6], ACT.Exp, scale=-1.0), c.sig("exp_done", "m", i))
                if 1 <= i <= MH:
                    probs_T("m", i - 1, T384, "mO")
            for t in range(NT):
                act.wait_ge(*(c.at("piece_used", "b1", 7) if t else c.at("sums0", "b1")))
                for h in range(2):
                    do(f(logit[:, 2 * t + h, :], acc[2 * t + h][:, :], ACT.Square, accum_out=st[:, 4 + 2 * t + h:5 + 2 * t + h]),
                       c.sig("squares", "post1", t) if h else None)
            if upto < 2:
                return
            split_at = [0]

            def split_high(upto):
                for hp in range(split_at[0], upto):
                    key = SPLIT_KEYS[hp // 2]
                    if hp % 2 == 0:
                        act.wait_ge(*W.ready(key))
                    if hp >= SPLIT_SLOTS:
                        act.wait_ge(*W.split_used(hp - SPLIT_SLOTS))
                    lo = (hp % 2) * (PIECE // 2)
                    go(f(d_hi[:, hp % SPLIT_SLOTS, :], ring[:, W.place(key), lo:lo + PIECE // 2], ACT.Copy), c.sig("d_hi", hp))
                split_at[0] = upto

            split_high(7)
            for q in range(4):
                copy(qraw[:, q, :], ("dqk", q))
                if q == 1:
                    split_high(11)
                if q == 3:
                    split_high(15)
                    for t in range(NT):
                        copy(vd[:, t, :], ("b2v", 1024, t))
            for i in range(2):
                act.wait_ge(*c.at("lambda_dots"))
                do(f(lam[:, i:i + 1], lam[:, i:i + 1], ACT.Exp), c.sig("lambda_exp") if i else None)
            def softplus(i):
                for h in (2 * i, 2 * i + 1):
                    act.wait_ge(*J.emptied("sbz", h))
                z, x = sbw[i % 3][:, :, 0:384], sbw[i % 3][:, :, 384:768]
                do(f(x, z, ACT.Abs))
                do(f(x, x, ACT.Exp, scale=-1.0))
                do(f(x, x, ACT.Ln, bias=ones[:, 0:1]), c.sig("softplus", i))

            for i in range(NDIFF + 2):
                if i < NDIFF:
                    exps("d", 2 * i, T384, 2 * i % 6)
                    exps("d", 2 * i + 1, T384, (2 * i + 1) % 6)
                split_high(min(19 + 4 * i, 2 * len(SPLIT_KEYS)) if i < 3 else split_at[0])
                if i < 2:
                    for q in (6 + 2 * i, 7 + 2 * i):
                        copy(pair(sqT if q < 8 else skT, q % 2), ("sqk", q))
                if i == 2:
                    for t in range(NT):
                        copy(sv[:, t, :], ("b2v", 2560, t))
                if i == NDIFF:
                    softplus(0)
                if i >= 2:
                    probs_T("dd", i - 2, T384, "ddO")
            for i in range(1, NSB // 2 + 2):
                if i >= 2:
                    for h in (2 * i - 4, 2 * i - 3):
                        act.wait_ge(*J.emptied("sbs", h))
                    x = sbw[(i - 2) % 3][:, :, 384:768]
                    do(f(x, x, ACT.Exp), c.sig("exp_done", "sb", i - 2))
                if i < NSB // 2:
                    softplus(i)
                if i >= 2:
                    for h in (2 * i - 4, 2 * i - 3):
                        m = 64 * (h % 2)
                        copy(mix2[m:m + 64, 4 + h // 2, :], ("sbo", h), S, rows=slice(m, m + 64))
            def high_parts(stage):
                at_ = [0]

                def high(upto):
                    for hp in range(at_[0], min(upto, 2 * len(FFN[stage]))):
                        key = W.ffn_key(stage, hp // 2)
                        if hp % 2 == 0:
                            act.wait_ge(*W.ready(key))
                        if hp >= SPLITS:
                            act.wait_ge(*W.ffn_used(stage, hp - SPLITS))
                        lo = (hp % 2) * (PIECE // 2)
                        go(f(w_hi[:, hp % SPLITS, :], ring[:, W.place(key), lo:lo + PIECE // 2], ACT.Copy), c.sig("ff_hi", stage, hp))
                        at_[0] = hp + 1

                return high

            def ffn(stage, high, name_in, func):
                for p, (name, g) in enumerate(FFN[stage]):
                    high(2 * p + SPLITS + 1)
                    if name == name_in:
                        if g >= 2:
                            act.wait_ge(*c.at("f_ready", stage, g - 2))
                        copy(ffa[stage][:, g % 2, :], (name, g), func=func)

            high = high_parts("ff")
            high(SPLITS)
            ffn("ff", high, "ff1", ACT.Relu)
            if upto < 3:
                return

            copy(pair(memkT, 0), ("memk", 0))
            copy(memv[:, :, :].rearrange("p a b -> p (a b)"), ("memv",))
            head_rms("memk2", [pair(memkT, 0)])

            def memory(stage):
                for i in range(MEMH + 3):
                    if i < MEMH:
                        exps(stage, i, T512, i % 4)
                    if 2 <= i < MEMH + 2:
                        probs_T(stage, i - 2, T512, stage + "O")
                    if i >= 3:
                        m, h = 64 * ((i - 3) % 2), i - 3
                        copy(mix3[m:m + 64, 6 + h // 2, :], (stage + "O", h), S, rows=slice(m, m + 64))

            def taps(first, end):
                for n in range(first, end):
                    if n >= DIAGS:
                        act.wait_ge(*c.at("tap_used", n - DIAGS))
                    col = vec("cv_dw_w_3", CC * (CONVW - 1 - n % CONVW) + CONV_PE[n // CONVW])
                    go(f(diag[:, n % DIAGS, :], ident, ACT.Copy, scale=col), c.sig("tap_ready", n))

            act.wait_ge(*c.at("normed", "cv"))
            taps(0, DIAGS)
            for g in range(3):
                key = ("cvp", 3 + g)
                act.wait_ge(*J.full(*key))
                for j in range(2):
                    do(f(sg3[:, g, j * S:(j + 1) * S], ps[J.bank(*key)][:, j * S:(j + 1) * S], ACT.Sigmoid,
                         bias=vec("cv_b_glu_3", CC + 2 * g + j)), J.free(*key) if j else None)
            copy(pair(mqT, 0), ("cvp", 6))
            head_rms("cvq2", [pair(mqT, 0)])
            taps(DIAGS, CONVW * len(CONV_PE))
            memory("cm")
            act.wait_ge(*c.at("centred"))
            flat = lambda v: v.rearrange("p a b -> p (a b)")
            do(f(flat(sq3), flat(cT), ACT.Square), c.sig("cvar_in"))
            act.wait_ge(*J.full("cvar"))
            do(f(lnw[:, 1, :], ps[J.bank("cvar")][:, 0:S], ACT.Sqrt, scale=1.0 / CONV, bias=C("eps")[:, 1:2]), J.free("cvar"))
            act.wait_ge(*c.at("conv_normed"))
            for k in range(CC):
                do(f(mix3[:, k, :], cT[:, k, :], ACT.Silu, scale=vec("cv_ln_g_3", k), bias=vec("cv_ln_b_3", k)),
                   c.sig("conv_act", k))
            high = high_parts("dn")
            high(SPLITS)
            ffn("dn", high, "gate", ACT.Silu)
            if upto < 4:
                return
            for g in range(2):
                copy(flat(swq[:, 3 * g:3 * g + 2, :]), ("swp", 2 * g))
                key = ("swp", 2 * g + 1)
                act.wait_ge(*J.full(*key))
                do(f(swq[:, 3 * g + 2, :], ps[J.bank(*key)][:, 0:S], ACT.Copy))
                do(f(swk[:, g, :], ps[J.bank(*key)][:, S:2 * S], ACT.Copy), J.free(*key))
                head_rms("swn", [pair(swq, 1), pair(swq, 2), pair(swk, 0)] if g else [pair(swq, 0)], g)
            copy(flat(swv), ("swv",))
            copy(pair(mqT, 0), ("swm", 0))
            head_rms("swn", [pair(mqT, 0)], 4)
            for i in range(SWAH + 3):
                if i < SWAH:
                    exps("sw", i, T384, i % 4, sinkb[:, i:i + 1])
                if 2 <= i < SWAH + 2:
                    probs_T("sw", i - 2, T384, "swO")
                if i >= 3:
                    m, h = 64 * ((i - 3) % 2), i - 3
                    copy(mix3[m:m + 64, h // 2, :], ("swO", h), S, rows=slice(m, m + 64))
            memory("sm")
            if upto < 5:
                return

            act.wait_ge(*c.at("router_max"))
            for t in range(NT):
                do(f(rt[:, 2, t, :], rt[:, 0, t, :], ACT.Exp, bias=xtr[:, t, 0:1]), c.sig("exp_done", "router") if t else None)

            act.wait_ge(*c.at("rounds_ready"))
            n_rounds = act.value_load(ridi[0:1, 15:16], min_val=NEXP, max_val=NROUND)
            with act.Fori(0, n_rounds) as r:
                c.enter(r)
                n, at_ = FFE // 512, [0]

                def high(upto):
                    for hp in range(at_[0], upto):
                        if hp % 2 == 0:
                            act.wait_ge(*W.landed(ROUND_PIECES[hp // 2]))
                        act.wait_ge(*W.half_wait(hp))
                        s, lo = W.place(ROUND_PIECES[hp // 2]), (hp % 2) * (PIECE // 2)
                        go(f(w_hi[:, hp % SPLITS, :], ring[:, s, lo:lo + PIECE // 2], ACT.Copy), c.sig("hi_ready", hp))
                    at_[0] = upto

                high(SPLITS)
                for g in range(n + 1):
                    if g < n:
                        high(8 * g + 9)
                        if g >= 2:
                            act.wait_ge(*J.emptied("xu", g - 2))
                        copy(esg[:, g % 2, :], ("xg", g), func=ACT.Silu)
                        high(8 * g + 13)
                    if g == 0:
                        copy(pgT[:, :], ("pgT",), S)
                    if g >= 1:
                        act.wait_ge(*J.full("xt", g - 1))
                        do(f(flat(act_hi[:, 4 * (g - 1):4 * g, :]), ps[J.bank("xt", g - 1)][:, :], ACT.Copy), c.sig("act_high", g - 1))
                high(HALVES)
                act.wait_ge(*c.at("piece_used", "xdown", FFE // P - 1))
                do(f(ey[:, 0:512], acc[0][:, :], ACT.Copy), c.sig("expert_out", 0))
                c.leave()
        @block.vector
        def _(dve):
            v = nc.vector

            def do(ins, s=None):
                s = s or c.sig("vec_step")
                ins.then_inc(s.sem, 1)
                dve.wait_ge(s.sem, s.val)

            def rep(ap, n):
                return bass.AP(tensor=ap.tensor, offset=ap.offset, ap=[ap.ap[0], [0, n], ap.ap[1]])

            def spread(ap, n):
                return bass.AP(tensor=ap.tensor, offset=ap.offset, ap=[ap.ap[0], ap.ap[1], [0, n]])

            def bank(*key):
                dve.wait_ge(*J.full(*key))
                return ps[J.bank(*key)]

            def pair(buf, q):
                return buf[:, 2 * q:2 * q + 2, :].rearrange("p a b -> p (a b)")

            def flat(x):
                return x.rearrange("p a b -> p (a b)")

            def norm(stage, src, dst=nrm, before=lambda t: None):
                s0 = 4 * NORMS.index(stage)
                for t in range(NT):
                    before(t)
                    do(v.tensor_tensor_reduce(junk[:, :], src[:, t, :], src[:, t, :], 1.0, 0.0, ALU.mult, ALU.add,
                                              st[:, s0 + t:s0 + t + 1]), c.sig("squares_v", stage, t))
                for t in range(NT):
                    dve.wait_ge(*c.at("rstd", stage, t))
                    do(v.tensor_scalar(dst[:, t, :], src[:, t, :], st[:, s0 + 2 + t:s0 + 3 + t], None, ALU.mult),
                       c.sig("normed", stage) if t else None)

            def gains(stage, gain, shift=None, n=KC, dst=hT, k0=0):
                for q in range(n // 2):
                    b = bank(stage, q)
                    for j in range(2):
                        k = 2 * q + j
                        do(v.tensor_scalar(dst[:, k0 + k, :], b[:, j * S:(j + 1) * S], gain(k), shift(k) if shift else None,
                                           ALU.mult, ALU.add if shift else ALU.bypass), J.free(stage, q) if j else None)

            def logits(stage, i, segs, buf, scale, bias, slope=None, sink=None):
                b = bank(stage + "S", i)
                n = P * sum(nk for _, _, nk in segs)
                x = tile(stage)[:, buf, 0:n]
                if bias is None:
                    do(v.tensor_scalar(x, b[:, 0:n], scale, None, ALU.mult), J.free(stage + "S", i))
                else:
                    do(v.scalar_tensor_tensor(x, b[:, 0:n], scale, bias, ALU.mult, ALU.add), J.free(stage + "S", i))
                if slope is not None:
                    do(v.scalar_tensor_tensor(x, C("dist"), slope, x, ALU.mult, ALU.add))
                for t, col, nk in segs:
                    do(v.tensor_reduce(smx[:, buf, t:t + 1], tile(stage)[:, buf, col:col + nk * P], AX, ALU.max, negate=True),
                       c.sig("max_ready", stage, i) if t and sink is None else None)
                if sink is not None:
                    do(v.tensor_scalar(smx[:, buf, 0:2], smx[:, buf, 0:2], sink, None, ALU.min), c.sig("max_ready", stage, i))

            def probs(stage, i, segs, buf, sink=False):
                dve.wait_ge(*c.at("exp_done", stage, i))
                if sink:
                    do(v.tensor_tensor(smx[:, buf, 2:4], smx[:, buf, 2:4], smx[:, buf, 6:8], ALU.add))
                do(v.reciprocal(smx[:, buf, 4:6], smx[:, buf, 2:4]))
                for t, col, nk in segs:
                    x = logit[:, buf, col:col + nk * P]
                    do(v.tensor_scalar(x, x, smx[:, buf, 4 + t:5 + t], None, ALU.mult), c.sig("probs_ready", stage, i) if t else None)

            def head_normed(stage, raws, gain, q0=0):
                for q, raw in enumerate(raws, q0):
                    dve.wait_ge(*J.emptied(stage, q))
                    do(v.reciprocal(rsw[:, q % 2, :], rsw[:, q % 2, :]))
                    do(v.scalar_tensor_tensor(raw, raw, gain[q - q0], rsw[:, q % 2, :], ALU.mult, ALU.mult),
                       c.sig("head_normed", stage, q))

            def add_sums(stage, last, gate=None):
                def add(t):
                    dve.wait_ge(*(c.at(*last) if t else c.at("sums0", stage)))
                    for h in range(2):
                        x, a = xres[:, t, h * 512:(h + 1) * 512], acc[2 * t + h][:, :]
                        if gate is not None:
                            do(v.tensor_tensor(junk[:, 0:512], a, gate[:, h * 512:(h + 1) * 512], ALU.mult))
                            a = junk[:, 0:512]
                        do(v.tensor_tensor(x, x, a, ALU.add), c.sig("x_ready", X_READY[stage]) if stage in X_READY and t + h == 2 else None)

                return add

            def split(hi, lo, x, s):
                do(v.tensor_copy(hi, x))
                do(v.tensor_tensor(lo, x, hi.bitcast(F32), ALU.subtract), s)

            def split_gains(stage, gain, shift=None, hi=hT_hi, lo=hT_lo):
                for q in range(KC // 2):
                    b, x = bank(stage, q), junk[:, (q % 2) * 512:(q % 2) * 512 + 512]
                    for j in range(2):
                        k = 2 * q + j
                        do(v.tensor_scalar(x[:, j * S:(j + 1) * S], b[:, j * S:(j + 1) * S], gain(k), shift(k) if shift else None,
                                           ALU.mult, ALU.add if shift else ALU.bypass), J.free(stage, q) if j else None)
                    split(pair(hi, q), pair(lo, q), x, c.sig("h_split", stage, q))

            def low_parts(stage):
                at_ = [0]

                def low(upto):
                    for hp in range(at_[0], min(upto, 2 * len(FFN[stage]))):
                        key = W.ffn_key(stage, hp // 2)
                        dve.wait_ge(*c.at("ff_hi", stage, hp))
                        lo, s = (hp % 2) * (PIECE // 2), c.sig("ff_lo", stage, hp)
                        v.tensor_tensor(w_lo[:, hp % SPLITS, :], ring[:, W.place(key), lo:lo + PIECE // 2],
                                        w_hi[:, hp % SPLITS, :].bitcast(F32), ALU.subtract).then_inc(s.sem, 1)
                        if hp % 2:
                            W.free(key, s)
                        at_[0] = hp + 1

                return low

            def f_split(stage, g):
                if g >= 4:
                    dve.wait_ge(*W.ffn_used(stage, 2 * FFN[stage].index((FFN[stage][-1][0], g - 4)) + 1))
                split(f_hi[:, g % 4, :], f_lo[:, g % 4, :], ffa[stage][:, g % 2, :], c.sig("f_ready", stage, g))

            do(v.memset(half_c[:, :], -0.5), c.sig("exponent"))
            s = c.sig("lo_ready", "credit", by=HALVES - 2 * len(POOL_PIECES))
            v.memset(xtr[:, 7, :], 0.0).then_inc(s.sem, HALVES - 2 * len(POOL_PIECES))
            dve.wait_ge(c.sem("x_in"), 16)
            norm("pre", xres)
            def ada_sum(*places):
                for x in places:
                    if x >= 4:
                        dve.wait_ge(*J.full("ada", ADA[x - 4]))
                    for h in range(2):
                        key, y = ("ada", 512 * ADA[x], h), adasum[x % 4]
                        dve.wait_ge(*W.ready(key))
                        w = ring[:, W.place(key), :].rearrange("p (k n) -> p k n", k=4)
                        for k in range(4):
                            cond, s = ccol[:, 4 * h + k:4 * h + k + 1], c.sig("ada_sum", x, h) if k == 3 else None
                            if h + k == 0:
                                do(v.tensor_scalar(y, w[:, k, :], cond, None, ALU.mult))
                            else:
                                do(v.scalar_tensor_tensor(y, w[:, k, :], cond, y, ALU.mult, ALU.add), s)
                        W.free(key, s)

            def ada(*places):
                ga, ra = vat["ada_b_2"]
                for g in (ADA[x] for x in places):
                    b, part, half = bank("ada", g), g // 2, g % 2
                    if part in (2, 5):
                        if half == 0:
                            dve.wait_ge(c.sem("gates_bias_in"), 32)
                        x = (gm if part == 2 else gf)[:, half * 512:(half + 1) * 512]
                        do(v.tensor_tensor(x, x, b[:, :], ALU.add), J.free("ada", g))
                    else:
                        o = 8 * {0: 0, 1: 1, 3: 2, 4: 3}[part] + 4 * half
                        do(v.tensor_tensor(modc[:, o:o + 4], b[:, 0:4], vcol[:, ga, ra + 4 * g:ra + 4 * g + 4], ALU.add), J.free("ada", g))

            def values(col):
                for t in range(NT):
                    do(v.tensor_copy(vt[:, t, col - 2048:col - 2048 + 512], bank("b1v", col, t)[:, :]), J.free("b1v", col, t))

            do(v.tensor_copy(vcol[:, 0, 0:vload[0][0]], bank("vec", 0)[:, 0:vload[0][0]]), J.free("vec", 0))
            gains("pre", lambda k: vec("g_pre", k))
            dve.wait_ge(*c.at("c_act"))
            ada_sum(0)
            do(v.memset(relb[32:33, :], 1.0))
            dve.wait_ge(c.sem("rel_in"), 16)
            do(v.tensor_copy(relw[0:33, :, :], spread(relb[0:33, :], P)), c.sig("rel_wide"))
            ada_sum(1)
            ada(0, 1)
            ada_sum(2)
            ada(2)
            ada_sum(3, 4)
            ada(3, 4)
            ada_sum(5, 6)
            values(2048)
            ada(5, 6)
            ada_sum(7)
            values(2560)
            ada(7)
            dve.wait_ge(c.sem("wraw_in"), 48)
            dve.wait_ge(c.sem("consts_in"), 16)
            for m in range(24):
                w = wraw[:, m, :]
                do(v.tensor_tensor(bd[:, m, :].rearrange("p (n o) -> p n o", o=4), rep(w, 32),
                                   C("block4").rearrange("p (n o) -> p n o", o=4), ALU.mult), c.sig("bd_ready") if m == 23 else None)
            dve.wait_ge(c.sem("relbias_in"), 32)
            for i in range(HEADS1 + 3):
                if i < HEADS1:
                    logits("b1", i, T384, i % 4, DH1 ** -0.5, relbias[:, i, :])
                if 1 <= i <= HEADS1:
                    probs("b1", i - 1, T384, (i - 1) % 4)
                if i >= 3:
                    h = i - 3
                    dve.wait_ge(*J.emptied("b1p", 12 + h // 2))
                    do(v.tensor_tensor(mix1[:, h, :], mix1[:, h, :], bank("b1O", h)[:, 0:S], ALU.mult), J.free("b1O", h))
            for k in range(KC):
                dve.wait_ge(*J.emptied("b1p", 16 + k // 2))
                y, x = xcT[:, k, :], xmT[:, k, :]
                do(v.tensor_scalar(y, x, vec("conv_w", 24 + k), vec("conv_b", k), ALU.mult, ALU.add))
                for d in (1, 2, 3):
                    do(v.scalar_tensor_tensor(y[:, d:S], x[:, 0:S - d], vec("conv_w", 8 * (3 - d) + k), y[:, d:S], ALU.mult, ALU.add),
                       c.sig("conv", k) if d == 3 else None)
            dve.wait_ge(*J.full("b1p", 23))
            for k in range(KC):
                do(v.tensor_scalar(cact[:, k, :], ones, ccol[:, k:k + 1], None, ALU.mult), c.sig("c_ready") if k == KC - 1 else None)
            for t in range(NT):
                for q in range(2):
                    do(v.tensor_copy(vm[:, t, q * 512:(q + 1) * 512], bank("vm", t, q)[:, :]), J.free("vm", t, q))
            ada(8)
            do(v.tensor_copy(flat(gl[:, :, :]), bank("gates")[:, 0:16]), J.free("gates"))
            go = c.sig("gates_in")
            do(v.tensor_scalar(lg[:, :, 12:16], gl[:, :, 4:8], 0.0, None, ALU.min), go)
            dve.wait_ge(*c.at("softplus", "gates"))
            do(v.tensor_tensor(gl[:, :, 4:8], lg[:, :, 12:16], lg[:, :, 8:12], ALU.subtract), c.sig("loggates"))
            b = bank("Frow")
            do(v.tensor_copy(aT[0:MH, S:2 * S], b[0:MH, 0:S]))
            do(v.tensor_tensor(aT[0:MH, 0:S], b[0:MH, S:2 * S], aT[0:MH, S:2 * S], ALU.subtract), J.free("Frow"))
            do(v.tensor_copy(flat(fcol[:, :, :]), bank("Fcol")[:, 0:8]), J.free("Fcol"))
            do(v.tensor_copy(mcol[:, 0, 0:1], ones[:, 0:1]), c.sig("a_rows"))
            stats = cmp[:, 0, :]
            moments = cmp[:, 1, :]
            for i in range(MH + 2):
                if i < MH:
                    x = logit[:, i % 4, 0:384]
                    do(v.tensor_tensor(x, bank("mA", i)[:, 0:384], C("causal"), ALU.add), J.free("mA", i))
                    for t, col, nk in T384:
                        do(v.tensor_reduce(mcol[:, i, t:t + 1], logit[:, i % 4, col:col + nk * P], AX, ALU.max))
                    do(v.tensor_scalar(mcol[:, i, 2:4], mcol[:, i, 0:2], 0.0, -1.0, ALU.max, ALU.mult))
                    do(v.tensor_tensor(mcol[:, i, 4:6], fcol[:, :, i], mcol[:, i, 2:4], ALU.subtract), c.sig("max_ready", "m", i))
                if 1 <= i <= MH:
                    h = i - 1
                    dve.wait_ge(*c.at("exp_done", "m", h))
                    b = bank("mS", h)
                    for t, col, nk in T384:
                        x = logit[:, h % 4, col:col + nk * P]
                        do(v.scalar_tensor_tensor(x, b[:, col:col + nk * P], MD ** -0.5, x, ALU.mult, ALU.mult,
                                                  accum_out=mcol[:, h, 8 + t:9 + t]), J.free("mS", h) if t else None)
                    m = mcol[:, h, :]
                    do(v.tensor_scalar(m[:, 10:12], m[:, 8:10], -1.0, None, ALU.mult), c.sig("probs_ready", "m", h))
                    do(v.tensor_tensor(m[:, 10:12], m[:, 8:10], m[:, 10:12], ALU.max))
                    do(v.tensor_tensor(m[:, 10:12], m[:, 10:12], m[:, 6:8], ALU.max))
                    do(v.reciprocal(m[:, 12:14], m[:, 10:12]))
                if i >= 2:
                    h = i - 2
                    b = bank("mO", h)
                    for t in range(NT):
                        x = nrm[:, t, h * MD:(h + 1) * MD]
                        do(v.tensor_scalar(x, b[:, t * S:(t + 1) * S], mcol[:, h, 12 + t:13 + t], None, ALU.mult),
                           J.free("mO", h) if t else None)
                        do(v.bn_stats(stats[:, 0:6], x))
                        do(v.bn_aggr(moments[:, 2 * (NT * h + t):2 * (NT * h + t) + 2], stats[:, 0:6]),
                           c.sig("moments") if h == MH - 1 and t else None)
            ada(9, 10, 11)
            for o, name in ((8, "mix_norm_g_2"), (24, "ffn_norm_g_2")):
                gg, rr = vat[name]
                do(v.scalar_tensor_tensor(modc[:, o:o + 8], modc[:, o:o + 8], 1.0, vcol[:, gg, rr:rr + 8], ALU.add, ALU.mult))
            dve.wait_ge(*c.at("rstd", "mlstm"))
            for h in range(MH):
                for t in range(NT):
                    x, j = nrm[:, t, h * MD:(h + 1) * MD], 2 * (NT * h + t)
                    do(v.tensor_scalar(x, x, moments[:, j:j + 1], moments[:, j + 1:j + 2], ALU.subtract, ALU.mult),
                       c.sig("normed", "mlstm") if h == MH - 1 and t else None)
            for q in range(4):
                b = bank("mlstm", q)
                for j in range(2):
                    k = 2 * q + j
                    x = junk[:, j * S:(j + 1) * S]
                    do(v.tensor_scalar(x, xcT[:, k, :], vec("skip", k), None, ALU.mult))
                    do(v.scalar_tensor_tensor(x, b[:, j * S:(j + 1) * S], vec("mh_norm", k), x, ALU.mult, ALU.add))
                    do(v.tensor_tensor(mix1[:, 8 + k, :], mix1[:, 8 + k, :], x, ALU.mult), J.free("mlstm", q) if j else None)
            dve.wait_ge(c.sem("wide_in"), 16)

            def post1(t):
                dve.wait_ge(*c.at("rstd", "post1", t))
                for h in range(2):
                    cs = slice(h * 512, (h + 1) * 512)
                    do(v.scalar_tensor_tensor(nrm[:, t, cs], acc[2 * t + h][:, :], st[:, 40 + t:41 + t], wide[:, cs], ALU.mult, ALU.mult))
                    do(v.tensor_tensor(xres[:, t, cs], xres[:, t, cs], nrm[:, t, cs], ALU.add), c.sig("x_ready", 1) if t + h == 2 else None)

            norm("mix2", xres, before=post1)
            if upto < 2:
                return
            dve.wait_ge(c.sem("small_in"), 80)
            for i in range(2):
                do(v.tensor_tensor_reduce(junk[:, 0:H64], lamv[:, 2 * i, :], lamv[:, 2 * i + 1, :], 1.0, 0.0, ALU.mult, ALU.add,
                                          lam[:, i:i + 1]), c.sig("lambda_dots") if i else None)
            split_at = [0]

            def split_low(upto):
                for hp in range(split_at[0], upto):
                    key = SPLIT_KEYS[hp // 2]
                    dve.wait_ge(*c.at("d_hi", hp))
                    lo, s = (hp % 2) * (PIECE // 2), c.sig("d_lo", hp)
                    v.tensor_tensor(d_lo[:, hp % SPLIT_SLOTS, :], ring[:, W.place(key), lo:lo + PIECE // 2],
                                    d_hi[:, hp % SPLIT_SLOTS, :].bitcast(F32), ALU.subtract).then_inc(s.sem, 1)
                    if hp % 2:
                        W.free(key, s)
                split_at[0] = upto

            split_low(SPLIT_SLOTS)
            split_gains("mix2", lambda k: modc[:, 8 + k:9 + k], lambda k: modc[:, k:k + 1], dT_hi, dT_lo)
            split_low(11)
            for q in range(4):
                split_low(11 + q // 2 * (q - 1))
                dve.wait_ge(*J.emptied("dqk", q))
                x = qraw[:, q, :].rearrange("p (a b) -> p a b", a=2)
                a, d = (junk[:, o:o + 512].rearrange("p (a b) -> p a b", a=2) for o in (0, 512))
                do(v.tensor_tensor(a, x, rep(C("cos"), 2), ALU.mult))
                do(v.tensor_tensor(d, bank("rot", q)[:, :].rearrange("p (a b) -> p a b", a=2), rep(C("sin"), 2), ALU.mult), J.free("rot", q))
                do(v.tensor_tensor(pair(qdT if q < 2 else kdT, q % 2), junk[:, 0:512], junk[:, 512:1024], ALU.add), c.sig("roped", q))
            dve.wait_ge(*c.at("lambda_exp"))
            do(v.tensor_scalar(lam[:, 2:3], lam[:, 0:1], lam[:, 1:2], LAMBDA_INIT, ALU.subtract, ALU.add))
            do(v.tensor_scalar(lam[:, 2:3], lam[:, 2:3], -1.0, None, ALU.mult))
            split_low(15)
            earlier = rep(C("earlier"), 2)

            def stick_logits(i):
                for h in (2 * i, 2 * i + 1):
                    do(v.tensor_scalar(sbw[i % 3][:, h % 2, 0:384], bank("sbz", h)[:, 0:384], H64 ** -0.5, None, ALU.mult), J.free("sbz", h))

            def stick_logs(i):
                z, sp_, lb = (sbw[i % 3][:, :, o:o + 384] for o in (0, 384, 768))
                dve.wait_ge(*c.at("softplus", i))
                do(v.scalar_tensor_tensor(lb, z, 0.0, sp_, ALU.min, ALU.subtract))
                do(v.tensor_tensor(z, lb, z, ALU.subtract))
                do(v.tensor_tensor(z, z, earlier, ALU.mult), c.sig("log1m_ready", i))

            for i in range(NDIFF + 3):
                if i < NDIFF:
                    for j in (2 * i, 2 * i + 1):
                        logits("d", j, T384, j % 6, H64 ** -0.5, C("chunk"))
                if i < 3:
                    split_low(min(19 + 4 * i, 2 * len(SPLIT_KEYS)))
                if i == NDIFF:
                    stick_logits(0)
                if 1 <= i <= NDIFF:
                    h = i - 1
                    p0, p1 = 2 * h % 6, (2 * h + 1) % 6
                    dve.wait_ge(*c.at("exp_done", "d", 2 * h + 1))
                    for p in (p0, p1):
                        do(v.reciprocal(smx[:, p, 4:6], smx[:, p, 2:4]))
                    do(v.tensor_scalar(smx[:, p1, 4:6], smx[:, p1, 4:6], lam[:, 2:3], None, ALU.mult))
                    for t, col, nk in T384:
                        x, y = dlogit[:, p0, col:col + nk * P], dlogit[:, p1, col:col + nk * P]
                        do(v.tensor_scalar(x, x, smx[:, p0, 4 + t:5 + t], None, ALU.mult))
                        do(v.scalar_tensor_tensor(x, y, smx[:, p1, 4 + t:5 + t], x, ALU.mult, ALU.add),
                           c.sig("probs_ready", "dd", h) if t else None)
                if i >= 3:
                    h = i - 3
                    do(v.tensor_copy(nrm[:, :, h * P:(h + 1) * P], bank("ddO", h)[:, 0:S].rearrange("p (t d) -> p t d", t=NT)),
                       J.free("ddO", h))
            stick_logs(0)
            for t in range(NT):
                do(v.tensor_tensor(junk[:, t * 512:(t + 1) * 512], nrm[:, t, 0:512], nrm[:, t, 0:512], ALU.mult))
            do(v.tensor_reduce(st[:, 44:52], junk[:, :].rearrange("p (a b) -> p a b", b=P), AX, ALU.add), c.sig("squares_v", "subln"))
            dve.wait_ge(*c.at("rstd", "subln"))
            for t in range(NT):
                x = nrm[:, t, 0:512].rearrange("p (a b) -> p a b", b=P)
                do(v.tensor_tensor(x, x, spread(st[:, 52 + 4 * t:56 + 4 * t], P), ALU.mult), c.sig("normed", "subln") if t else None)
            for i in range(1, NSB // 2 + 2):
                if i >= 2:
                    for h in (2 * i - 4, 2 * i - 3):
                        w = sbw[(i - 2) % 3][:, h % 2, :]
                        do(v.tensor_tensor(w[:, 384:768], bank("sbs", h)[:, 0:384], w[:, 768:1152], ALU.add), J.free("sbs", h))
                if i == 2:
                    for q in range(2):
                        b = bank("subln", q)
                        for j in range(2):
                            do(v.tensor_scalar(mix2[:, 2 * q + j, :], b[:, j * S:(j + 1) * S], vec("diff_subln_g_2"), 1.0 - LAMBDA_INIT,
                                               ALU.mult, ALU.mult), J.free("subln", q) if j else None)
                if i < NSB // 2:
                    stick_logits(i)
                if 2 <= i <= NSB // 2:
                    stick_logs(i - 1)
                if i >= 2:
                    a = sbw[(i - 2) % 3][:, :, 384:768]
                    dve.wait_ge(*c.at("exp_done", "sb", i - 2))
                    do(v.tensor_tensor(a, a, earlier, ALU.mult), c.sig("sticks_ready", i - 2))
            low = low_parts("ff")
            low(SPLITS)
            norm("ffn2", xres, before=add_sums("b2", ("piece_used", "b2", 3), gm))
            split_gains("ffn2", lambda k: modc[:, 24 + k:25 + k], lambda k: modc[:, 16 + k:17 + k])
            for p, (name, g) in enumerate(FFN["ff"]):
                low(2 * p + SPLITS + 1)
                if name == "ff1":
                    x = ffa["ff"][:, g % 2, :]
                    dve.wait_ge(*J.emptied("ff1", g))
                    do(v.tensor_tensor(x, x, x, ALU.mult))
                    f_split("ff", g)
                    if g == 8 and upto >= 3:
                        dve.wait_ge(c.sem("mem_in"), 16)
                        norm("mem", memx)
                    if g == 12 and upto >= 3:
                        gains("mem", lambda k: vec("mem_norm_g_3", k), dst=memT)
            norm("final2", xres, before=add_sums("ff", ("ff_used", "ff", 2 * len(FFN["ff"]) - 1), gf))
            dve.wait_ge(c.sem("final_gain_in"), 16)

            def final2(t):
                do(v.tensor_tensor(xres[:, t, :], nrm[:, t, :], wide[:, :], ALU.mult), c.sig("x_ready", 2) if t else None)

            norm("cv", xres, before=final2)
            if upto < 3:
                return
            gains("cv", lambda k: vec("cv_attn_norm_g_3", k))
            head_normed("memk2", [pair(memkT, 0)], [vec("mem_k_norm_g_3")])
            def glu(g):
                b = bank("cvp", g)
                dve.wait_ge(*J.emptied("cvp", 3 + g))
                for j in range(2):
                    do(v.scalar_tensor_tensor(uT[:, 2 * g + j, :], b[:, j * S:(j + 1) * S], vec("cv_b_glu_3", 2 * g + j),
                                              sg3[:, g, j * S:(j + 1) * S], ALU.add, ALU.mult), J.free("cvp", g) if j else None)

            def conv(k):
                y, x = cT[:, k, :], uT[:, k, :]
                do(v.tensor_scalar(y, x, vec("cv_dw_w_3", CC * (CONVW - 1) + k), vec("cv_dw_b_3", k), ALU.mult, ALU.add))
                for d in range(1, CONVW):
                    do(v.scalar_tensor_tensor(y[:, d:S], x[:, 0:S - d], vec("cv_dw_w_3", CC * (CONVW - 1 - d) + k), y[:, d:S],
                                              ALU.mult, ALU.add), c.sig("cmean_in", k) if d == CONVW - 1 else None)

            glu(0)
            conv(1)
            glu(1)
            glu(2)
            conv(2)
            conv(3)
            head_normed("cvq2", [pair(mqT, 0)], [vec("cv_memq_norm_g_3")])

            def memory(stage, between=lambda i: None):
                for i in range(MEMH + 1):
                    if i < MEMH:
                        logits(stage, i, T512, i % 4, H64 ** -0.5, None)
                    between(i)
                    if i >= 1:
                        probs(stage, i - 1, T512, (i - 1) % 4)

            memory("cm")
            for x, k in enumerate(CONV_PE):
                dve.wait_ge(*c.at("tap_used", (x + 1) * CONVW - 1))
                do(v.tensor_scalar(cT[:, k, :], acc[x][:, 0:S], vec("cv_dw_b_3", k), None, ALU.add), c.sig("cmean_in", k))
            do(v.tensor_scalar(lnw[:, 0, :], bank("cmean")[:, 0:S], 1.0 / CONV, None, ALU.mult), J.free("cmean"))
            do(v.tensor_tensor(cT[:, :, :], cT[:, :, :], rep(lnw[:, 0, :], CC), ALU.subtract), c.sig("centred"))
            dve.wait_ge(*J.emptied("cvar"))
            do(v.reciprocal(lnw[:, 1, :], lnw[:, 1, :]))
            do(v.tensor_tensor(cT[:, :, :], cT[:, :, :], rep(lnw[:, 1, :], CC), ALU.mult), c.sig("conv_normed"))
            low = low_parts("dn")
            low(SPLITS)
            norm("cvf", xres, before=add_sums("cv", ("piece_used", "cv", 2)))
            split_gains("cvf", lambda k: vec("cv_ffn_norm_g_3", k))
            for p, (name, g) in enumerate(FFN["dn"]):
                low(2 * p + SPLITS + 1)
                if name == "up":
                    x, b = ffa["dn"][:, g % 2, :], bank("up", g)
                    dve.wait_ge(*J.emptied("gate", g))
                    do(v.tensor_tensor(x, x, b[:, :], ALU.mult), J.free("up", g))
                    f_split("dn", g)
            norm("sw", xres, before=add_sums("dn", ("ff_used", "dn", 2 * len(FFN["dn"]) - 1)))
            if upto < 4:
                return
            gains("sw", lambda k: vec("sw_attn_norm_g_3", k))
            head_normed("swn", [pair(swq, 0), pair(swq, 1), pair(swq, 2), pair(swk, 0)],
                        [vec("sw_q_norm_g_3")] * 3 + [vec("sw_k_norm_g_3")])
            do(v.tensor_scalar(fsink[:, :], sinkb[:, :], -1.0, None, ALU.mult))
            for i in range(SWAH + 1):
                if i < SWAH:
                    logits("sw", i, T384, i % 4, H64 ** -0.5, C("window"), -(2.0 ** (-8.0 * (i + 1) / SWAH)), fsink[:, i:i + 1])
                if i == 1:
                    head_normed("swn", [pair(mqT, 0)], [vec("sw_memq_norm_g_3")], 4)
                if i >= 1:
                    probs("sw", i - 1, T384, (i - 1) % 4, sink=True)
            memory("sm")
            norm("moe", xres, before=add_sums("so", ("piece_used", "so", 3)))
            if upto < 5:
                return
            gains("moe", lambda k: vec("sw_ffn_norm_g_3", k))
            do(v.tensor_copy(flat(rt[:, 0, :, :]), bank("router")[:, 0:16]), J.free("router"))
            for t in range(NT):
                l = rt[:, 0, t, :]
                above, below = (cmp[:, x, 0:64].rearrange("p (e j) -> p e j", e=8) for x in range(2))
                lower = C("lower").rearrange("p (e j) -> p e j", e=8)
                do(v.tensor_tensor(above, rep(l, 8), spread(l, 8), ALU.is_gt))
                do(v.tensor_tensor(below, rep(l, 8), spread(l, 8), ALU.is_equal))
                do(v.tensor_tensor(below, below, lower, ALU.mult))
                do(v.tensor_tensor(above, above, below, ALU.add))
                do(v.tensor_reduce(rt[:, 3, t, :], above, AX, ALU.add))
                do(v.tensor_scalar(rt[:, 1, t, :], rt[:, 3, t, :], 2.0, None, ALU.is_lt), c.sig("selected") if t else None)
            for t in range(NT):
                do(v.tensor_reduce(xtr[:, t, 0:1], rt[:, 0, t, :], AX, ALU.max, negate=True), c.sig("router_max") if t else None)
            dve.wait_ge(*c.at("exp_done", "router"))
            for t in range(NT):
                do(v.tensor_tensor_reduce(rt[:, 4, t, :], rt[:, 2, t, :], rt[:, 1, t, :], 1.0, 0.0, ALU.mult, ALU.add, xtr[:, t, 1:2]))
                do(v.reciprocal(xtr[:, t, 2:3], xtr[:, t, 1:2]))
            b = bank("slots")
            do(v.memset(pos[:, :, :, :].rearrange("p a t r -> p (a t r)"), 0.0))
            do(v.tensor_copy(pos[:, 0, :, 0:NEXP], b[:, 0:16].rearrange("p (t e) -> p t e", t=NT)))
            do(v.tensor_copy(xtr[:, 3, :], b[:, 16:24]), J.free("slots"))
            do(v.tensor_copy(pos[:, 1, :, 0:NEXP], rt[:, 1, :, :]))
            for t in range(NT):
                do(v.tensor_scalar(pos[:, 2, t, 0:NEXP], rt[:, 4, t, :], xtr[:, t, 2:3], None, ALU.mult))
            def dispatch(at_, key):
                for m, a in ((Pm, 1), (PG, 2)):
                    for t in range(NT):
                        do(v.tensor_scalar(m[:, t, :], C("iota"), pos[:, 0, t, at_], pos[:, a, t, at_], ALU.is_equal, ALU.mult),
                           c.sig("dispatch_ready", key) if a == 2 and t else None)

            gs, rs = vat["sw_ffn_norm_g_3"]

            def gathered(key):
                for q in range(2):
                    b, x = bank("hg" + key, q), eact[:, 1, :]
                    do(v.tensor_tensor(x.rearrange("p (a b) -> p a b", a=4), b[:, :].rearrange("p (a b) -> p a b", a=4),
                                       spread(vcol[:, gs, rs + 4 * q:rs + 4 * q + 4], P), ALU.mult), J.free("hg" + key, q))
                    split(flat(hg_hi[:, 4 * q:4 * q + 4, :]), flat(hg_lo[:, 4 * q:4 * q + 4, :]), x,
                          c.sig("gathered", key, 1) if q else None)

            dispatch(slice(0, 1), "first")
            big, rank = xtr[:, 4, :], xtr[:, 5, :]
            before_ = cmp[:, 0, 0:64].rearrange("p (e j) -> p e j", e=8)
            do(v.tensor_scalar(big, xtr[:, 3, :], float(P), None, ALU.is_gt))
            do(v.tensor_tensor(before_, rep(big, 8), C("lower").rearrange("p (e j) -> p e j", e=8), ALU.mult))
            do(v.tensor_reduce(rank, before_, AX, ALU.add))
            do(v.memset(rid[:, :], 0.0))
            do(v.tensor_copy(rid[:, 0:8], C("eid")))
            do(v.tensor_reduce(rid[:, 15:16], big, AX, ALU.add))
            do(v.tensor_scalar(rid[:, 15:16], rid[:, 15:16], float(NEXP), None, ALU.add))
            one = cmp[:, 1, 0:8 * EXTRA].rearrange("p (x e) -> p x e", e=8)
            hit = cmp[:, 1, 32:32 + 16 * EXTRA].rearrange("p (t x e) -> p t x e", t=NT, e=8)
            do(v.tensor_tensor(one, rep(rank, EXTRA), spread(C("slots")[:, 0:EXTRA], 8), ALU.is_equal))
            do(v.tensor_tensor(one, one, rep(big, EXTRA), ALU.mult))
            do(v.tensor_tensor(hit[:, 0, :, :], one, rep(C("eid"), EXTRA), ALU.mult))
            do(v.tensor_reduce(rid[:, 8:8 + EXTRA], hit[:, 0, :, :], AX, ALU.add))
            for a in range(3):
                for t in range(NT):
                    do(v.tensor_tensor(hit[:, t, :, :], one, rep(pos[:, a, t, 0:NEXP], EXTRA), ALU.mult))
                do(v.tensor_reduce(pos[:, a, :, NEXP:NEXP + EXTRA], hit, AX, ALU.add))
            do(v.tensor_scalar(pos[:, 0, :, NEXP:NEXP + EXTRA], pos[:, 0, :, NEXP:NEXP + EXTRA], float(-P), None, ALU.add))
            do(v.tensor_copy(ridi[:, :], rid[:, :]), c.sig("rounds_ready"))
            gathered("first")
            n_rounds = dve.value_load(ridi[0:1, 15:16], min_val=NEXP, max_val=NROUND)
            with dve.Fori(0, n_rounds) as r:
                c.enter(r)
                n, at_ = FFE // 512, [0]

                def low(upto):
                    for hp in (x for x in range(at_[0], upto) if x // 2 not in POOL_PIECES):
                        dve.wait_ge(*c.at("hi_ready", hp))
                        s, lo = W.place(ROUND_PIECES[hp // 2]), (hp % 2) * (PIECE // 2)
                        v.tensor_tensor(w_lo[:, hp % SPLITS, :], ring[:, s, lo:lo + PIECE // 2],
                                        w_hi[:, hp % SPLITS, :].bitcast(F32), ALU.subtract).then_inc(c.sig("lo_ready", hp).sem, 1)
                    at_[0] = upto

                low(SPLITS)
                for g in range(n + 1):
                    if g < n:
                        low(8 * g + 13)
                        b = bank("xu", g)
                        dve.wait_ge(*J.emptied("xg", g))
                        if g >= 2:
                            dve.wait_ge(*J.full("xt", g - 2))
                        do(v.tensor_tensor(eact[:, g % 2, :], esg[:, g % 2, :], b[:, :], ALU.mult), J.free("xu", g))
                    if g >= 1:
                        dve.wait_ge(*c.at("act_high", g - 1))
                        do(v.tensor_tensor(flat(act_lo[:, 4 * (g - 1):4 * g, :]), ps[J.bank("xt", g - 1)][:, :],
                                           flat(act_hi[:, 4 * (g - 1):4 * g, :]).bitcast(F32), ALU.subtract), J.free("xt", g - 1))
                    if g == 3:
                        dispatch(bass.ds(r + 1, 1), "next")
                    if g == n - 1:
                        gathered("next")
                low(HALVES)
                dve.wait_ge(*c.at("piece_used", "xdown", FFE // P - 1))
                do(v.tensor_copy(ey[:, 512:1024], acc[1][:, :]), c.sig("expert_out1", 0))
                for t in range(NT):
                    for h in range(2):
                        x = xres[:, t, h * 512:(h + 1) * 512]
                        do(v.tensor_tensor(x, x, bank("xs", t, h)[:, :], ALU.add), J.free("xs", t, h))
                c.leave()
            do(v.tensor_copy(mcol[:, 0, 0:1], ones[:, 0:1]), c.sig("x_ready", 5))

        @block.gpsimd
        def _(pool):
            g = nc.gpsimd

            def do(ins, s=None):
                s = s or c.sig("pool_step")
                ins.then_inc(s.sem, 1)
                pool.wait_ge(s.sem, s.val)

            def rstd(stage, src, dst, n, width, eps=RMS_EPS):
                do(g.tensor_scalar(dst, src, 1.0 / width, eps, ALU.mult, ALU.add))
                do(g.tensor_tensor(dst, dst, half_c[:, 0:n], ALU.pow), c.sig("rstd", *stage))

            def norm(stage):
                s0 = 4 * NORMS.index(stage)
                for t in range(NT):
                    pool.wait_ge(*c.at("squares_v", stage, t))
                    rstd((stage, t), st[:, s0 + t:s0 + t + 1], st[:, s0 + 2 + t:s0 + 3 + t], 1, D)

            pool.wait_ge(*c.at("exponent"))
            norm("pre")
            pool.wait_ge(*J.full("vm", 1, 1))
            for dst, col in ((gm, 2 * D), (gf, 5 * D)):
                pool.dma_start(dst, everywhere(A["ada_b_2"][:, col:col + D], D)).then_inc(c.sem("gates_bias_in"), 16)
            pool.wait_ge(*c.at("moments"))
            var = cmp[:, 1, 1:1 + 4 * MH:2]
            do(g.tensor_scalar(var, var, LN_EPS, None, ALU.add))
            do(g.tensor_tensor(var, var, half_c[:, 0:2 * MH], ALU.pow), c.sig("rstd", "mlstm"))
            for t in range(NT):
                pool.wait_ge(*c.at("squares", "post1", t))
                do(g.tensor_tensor(st[:, 4 + 2 * t:5 + 2 * t], st[:, 4 + 2 * t:5 + 2 * t], st[:, 5 + 2 * t:6 + 2 * t], ALU.add))
                rstd(("post1", t), st[:, 4 + 2 * t:5 + 2 * t], st[:, 40 + t:41 + t], 1, D)
            norm("mix2")
            if upto < 2:
                return
            pool.wait_ge(*c.at("x_ready", 1))
            pool.dma_start(wide[:, :], everywhere(A["final_norm_g_2"], D)).then_inc(c.sem("final_gain_in"), 16)
            pool.wait_ge(*c.at("squares_v", "subln"))
            rstd(("subln",), st[:, 44:52], st[:, 52:60], 8, P)
            norm("ffn2")
            if upto >= 3:
                pool.dma_start(memx, A["mem_3"].rearrange("a (t p) d -> p (a t) d", p=P)).then_inc(c.sem("mem_in"), 16)
                norm("mem")
            norm("final2")
            norm("cv")
            if upto < 3:
                return
            for k in range(1):
                pool.wait_ge(*J.emptied("cvp", 0))
                y, x = cT[:, k, :], uT[:, k, :]
                do(g.tensor_scalar(y, x, vec("cv_dw_w_3", CC * (CONVW - 1) + k), vec("cv_dw_b_3", k), ALU.mult, ALU.add))
                for d in range(1, CONVW):
                    do(g.tensor_scalar(tap[:, d:S], x[:, 0:S - d], vec("cv_dw_w_3", CC * (CONVW - 1 - d) + k), None, ALU.mult))
                    do(g.tensor_tensor(y[:, d:S], y[:, d:S], tap[:, d:S], ALU.add), c.sig("conv_pool", k) if d == CONVW - 1 else None)
            norm("cvf")
            norm("sw")
            if upto < 4:
                return
            norm("moe")
            if upto < 5:
                return
            pool.wait_ge(*c.at("rounds_ready"))
            n_rounds = pool.value_load(ridi[0:1, 15:16], min_val=NEXP, max_val=NROUND)
            with pool.Fori(0, n_rounds) as r:
                c.enter(r)
                for i in POOL_PIECES:
                    for hp in (2 * i, 2 * i + 1):
                        pool.wait_ge(*c.at("hi_ready", hp))
                        lo = (hp % 2) * (PIECE // 2)
                        g.tensor_tensor(w_lo[:, hp % SPLITS, :], ring[:, W.place(ROUND_PIECES[i]), lo:lo + PIECE // 2],
                                        w_hi[:, hp % SPLITS, :].bitcast(F32), ALU.subtract).then_inc(c.sig("lo_ready_pool", hp).sem, 1)
                c.leave()

        del block
    return c, J, W


X_READY = {"dn": 3, "so": 4}
NORMS = ["pre", "post1", "mix2", "ffn2", "mem", "final2", "cv", "cvf", "sw", "moe"]
_INS = ["x", "rel_bias", "g_pre", "g_post", "w_in", "conv_w", "conv_b", "wq_m", "wk_m", "wv_m", "w_if", "b_if", "mh_norm",
        "skip", "w_out", "c_2", "ada_w_2", "ada_b_2", "mix_norm_g_2", "w_in_2", "lambda_q1_2", "lambda_k1_2",
        "lambda_q2_2", "lambda_k2_2", "diff_subln_g_2", "w_out_2", "ffn_norm_g_2", "w_ff1_2", "w_ff2_2",
        "final_norm_g_2", "mem_3", "mem_norm_g_3", "w_mem_kv_3", "mem_k_norm_g_3", "cv_attn_norm_g_3", "cv_w_in_3",
        "cv_b_glu_3", "cv_dw_w_3", "cv_dw_b_3", "cv_ln_g_3", "cv_ln_b_3", "cv_memq_norm_g_3", "cv_w_out_3",
        "cv_ffn_norm_g_3", "cv_w_gate_3", "cv_w_up_3", "cv_w_down_3", "sw_attn_norm_g_3", "sw_w_in_3", "sw_q_norm_g_3",
        "sw_k_norm_g_3", "sw_sinks_3", "sw_memq_norm_g_3", "sw_w_out_3", "sw_ffn_norm_g_3", "sw_router_3",
        "sw_we_gate_3", "sw_we_up_3", "sw_we_down_3"]


def build(core, inputs, upto=9):
    table, const_at = constants()
    known = None
    for _ in range(2):
        nc = core()
        arrays, A = {"consts": table}, {}
        for name in _INS:
            arrays[name] = np.ascontiguousarray(inputs[name])
        for name, a in arrays.items():
            A[name] = nc.dram_tensor(f"in_{name}", a.shape, F32, kind="ExternalInput").ap()
        out = nc.dram_tensor("out_dram", (1, S, D), F32, kind="ExternalOutput").ap()
        known = program(nc, A, out, const_at, known, upto)
    return nc, {f"in_{name}": a for name, a in arrays.items()}


def kernel(**inputs):
    import concourse.bacc as bacc
    from concourse.bass_utils import run_bass_kernel_spmd
    nc, arrays = build(lambda: bacc.Bacc("TRN2", target_bir_lowering=False, num_devices=1), inputs)
    r = run_bass_kernel_spmd(nc, [arrays], core_ids=[0])
    return r.results[0]["out_dram"]
```
